# Optimizing a Trainium2 kernel written in Bass

```python
import jax
import jax.numpy as jnp
from jax import lax
import numpy as np
import math
import jax, jax.numpy as jnp

D_MODEL = 1024
BATCH = 1
SEQ = 256
DEPTH = 1

N_BRANCH = 4
BRANCH_WIDTH = 512
RWKV_HEADS = 8
RWKV_HEAD_DIM = BRANCH_WIDTH // RWKV_HEADS
RWKV_DECAY_RANK = 64
RWKV_ICL_RANK = 64
RWKV_VALUE_RANK = 32
RWKV_GATE_RANK = 128
RWKV_LNX_EPS = 64e-5
HGRN_HEADS = 4
HGRN_HEAD_DIM = BRANCH_WIDTH // HGRN_HEADS
MLSTM_HEADS = 4
MLSTM_HEAD_DIM = BRANCH_WIDTH // MLSTM_HEADS
CHUNK = 64
LRU_BLOCKS = 8
LRU_BLOCK_DIM = BRANCH_WIDTH // LRU_BLOCKS
LRU_C = 8.0
CONV_WIDTH = 4
N_EXPERTS = 32
TOP_K = 4
D_EXPERT = 1024
SWIGLU_LIMIT = 7.0
SWIGLU_ALPHA = 1.702
EXPERT_BLOCK = 128
D_PLE = 256
LN_EPS = 1e-5
NORM_EPS = 1e-6
DEEPNORM_ALPHA = (2 * DEPTH) ** 0.25
DEEPNORM_BETA = (8 * DEPTH) ** -0.25

RWKV_SPLITS = (BRANCH_WIDTH, BRANCH_WIDTH, BRANCH_WIDTH, RWKV_DECAY_RANK, RWKV_ICL_RANK, RWKV_GATE_RANK)
RWKV_COLS = 3 * BRANCH_WIDTH + RWKV_DECAY_RANK + RWKV_ICL_RANK + RWKV_GATE_RANK
HGRN_COLS = 4 * BRANCH_WIDTH
MLSTM_SPLITS = (BRANCH_WIDTH, BRANCH_WIDTH, BRANCH_WIDTH, BRANCH_WIDTH, MLSTM_HEADS, MLSTM_HEADS)
MLSTM_COLS = 4 * BRANCH_WIDTH + 2 * MLSTM_HEADS
LRU_COLS = 2 * BRANCH_WIDTH
GATE_COLS = N_BRANCH * D_MODEL
N_COLS_BASE = RWKV_COLS + HGRN_COLS + MLSTM_COLS + LRU_COLS + GATE_COLS
N_COLS_REST = N_COLS_BASE + RWKV_VALUE_RANK

F32 = jnp.float32


def _split(z, sizes):
    return jnp.split(z, np.cumsum(sizes)[:-1].tolist(), axis=-1)

def _layernorm(x, g, b, dtype):
    xf = x.astype(F32)
    xc = xf - jnp.mean(xf, -1, keepdims=True)
    var = jnp.mean(xc * xc, -1, keepdims=True)
    return (xc * lax.rsqrt(var + LN_EPS) * g + b).astype(dtype)

def _head_layernorm(y, eps):
    yc = y - jnp.mean(y, -1, keepdims=True)
    out = yc * lax.rsqrt(jnp.mean(yc * yc, -1, keepdims=True) + eps)
    return out.reshape(out.shape[:-2] + (-1,))

def _head_rmsnorm(y, eps):
    out = y * lax.rsqrt(jnp.mean(y * y, -1, keepdims=True) + eps)
    return out.reshape(out.shape[:-2] + (-1,))

def _token_shift(z):
    return jnp.pad(z, ((0, 0), (1, 0), (0, 0)))[:, :-1]

def _causal_conv(z, w, b):
    seq = z.shape[1]
    zp = jnp.pad(z, ((0, 0), (CONV_WIDTH - 1, 0), (0, 0)))
    out = b
    for j in range(CONV_WIDTH):
        out = out + zp[:, j:j + seq] * w[j]
    return out

def _to_heads(t, n_heads):
    bsz, seq, width = t.shape
    return t.reshape(bsz, seq, n_heads, width // n_heads).transpose(0, 2, 1, 3)

def _from_heads(t):
    return t.transpose(0, 2, 1, 3)

def _to_chunks(t):
    bsz, nh, seq = t.shape[:3]
    t = t.reshape((bsz, nh, seq // CHUNK, CHUNK) + t.shape[3:])
    return jnp.moveaxis(t, 2, 0)

def _from_chunks(t):
    nc, bsz, nh, c, dv = t.shape
    return jnp.moveaxis(t, 0, 2).reshape(bsz, nh, nc * c, dv)

def rwkv7_mix(zA, v_first, v_mix, mu, w0, w2, a0, a2, g2, k_k, k_a, r_k, lnx_g, lnx_b):
    bsz, seq = zA.shape[:2]
    zA = zA + (_token_shift(zA) - zA) * mu
    r, k, v, xw, xa, xg = _split(zA, RWKV_SPLITS)
    w_log = -jax.nn.softplus(-(w0 + jnp.tanh(xw) @ w2)) - 0.5
    decay = jnp.exp(-jnp.exp(w_log))
    a = jax.nn.sigmoid(a0 + xa @ a2)
    g = jax.nn.sigmoid(xg) @ g2
    if v_mix is not None:
        v = v + (v_first - v) * jax.nn.sigmoid(v_mix)

    def hs(t):
        return t.reshape(bsz, seq, RWKV_HEADS, RWKV_HEAD_DIM)

    kk = hs(k * k_k)
    kk = kk / jnp.maximum(jnp.sqrt(jnp.sum(kk * kk, -1, keepdims=True)), 1e-12)
    k = k * (1.0 + (a - 1.0) * k_a)
    rh, kh, vh, dh, ah = hs(r), hs(k), hs(v), hs(decay), hs(a)
    neg_kk = -kk
    kk_a = kk * ah

    def step(state, inp):
        r_t, w_t, k_t, v_t, a_t, b_t = inp
        sa = jnp.einsum('bhvk,bhk->bhv', state, a_t)
        state = state * w_t[:, :, None, :] + sa[..., None] * b_t[:, :, None, :] + v_t[..., None] * k_t[:, :, None, :]
        return state, jnp.einsum('bhvk,bhk->bhv', state, r_t)

    xs = tuple(jnp.moveaxis(t, 1, 0) for t in (rh, dh, kh, vh, neg_kk, kk_a))
    state0 = jnp.zeros((bsz, RWKV_HEADS, RWKV_HEAD_DIM, RWKV_HEAD_DIM), F32)
    _, y = lax.scan(step, state0, xs)
    y = jnp.moveaxis(y, 0, 1)
    y = _head_layernorm(y, RWKV_LNX_EPS) * lnx_g + lnx_b
    bonus = (jnp.sum(rh * kh * r_k, -1, keepdims=True) * vh).reshape(bsz, seq, BRANCH_WIDTH)
    return (y + bonus) * g, v

def _gla_chunked(q, k, v, log_f):
    bsz, nh, _, dk = q.shape
    dv = v.shape[-1]
    causal = jnp.tril(jnp.ones((CHUNK, CHUNK), bool))

    def chunk(state, inp):
        qc, kc, vc, lf = inp
        bcum = jnp.cumsum(lf, axis=-2)
        o_inter = jnp.einsum('bhtd,bhde->bhte', qc * jnp.exp(bcum), state)
        diff = bcum[:, :, :, None, :] - bcum[:, :, None, :, :]
        pair_decay = jnp.exp(jnp.where(causal[:, :, None], diff, -jnp.inf))
        attn = jnp.einsum('bhtd,bhsd,bhtsd->bhts', qc, kc, pair_decay)
        o = o_inter + jnp.einsum('bhts,bhse->bhte', attn, vc)
        b_last = bcum[:, :, -1]
        state = jnp.exp(b_last)[..., None] * state + jnp.einsum('bhsd,bhse->bhde', kc * jnp.exp(b_last[:, :, None] - bcum), vc)
        return state, o

    state0 = jnp.zeros((bsz, nh, dk, dv), F32)
    _, o = lax.scan(chunk, state0, tuple(_to_chunks(t) for t in (q, k, v, log_f)))
    return _from_chunks(o)

def hgrn2_mix(zB, lb, norm_w):
    q, f, i, g = _split(zB, (BRANCH_WIDTH,) * 4)
    q = jax.nn.silu(q)
    log_f = jnp.logaddexp(jnp.log(lb), jnp.log1p(-lb) + jax.nn.log_sigmoid(f))
    k = (1.0 - lb) * jax.nn.sigmoid(-f)
    o = _gla_chunked(*(_to_heads(t, HGRN_HEADS) for t in (q, k, i, log_f)))
    o = _head_rmsnorm(_from_heads(o), NORM_EPS) * norm_w
    return o * jax.nn.silu(g)

def _mlstm_chunked(q, k, v, i_pre, log_f):
    bsz, nh, _, dk = q.shape
    dv = v.shape[-1]
    causal = jnp.tril(jnp.ones((CHUNK, CHUNK), bool))

    def chunk(carry, inp):
        c_mat, n_vec, m_prev = carry
        qc, kc, vc, ic, lf = inp
        fcum = jnp.cumsum(lf, axis=-1)
        log_w = jnp.where(causal, fcum[..., :, None] - fcum[..., None, :] + ic[..., None, :], -jnp.inf)
        log_inter = fcum + m_prev[..., None]
        m_t = jnp.maximum(log_inter, jnp.max(log_w, -1))
        w_intra = jnp.exp(log_w - m_t[..., None])
        w_inter = jnp.exp(log_inter - m_t)
        s_qk = jnp.einsum('bhtd,bhsd->bhts', qc, kc) * w_intra
        num = w_inter[..., None] * jnp.einsum('bhtd,bhde->bhte', qc, c_mat) + jnp.einsum('bhts,bhse->bhte', s_qk, vc)
        den = w_inter * jnp.einsum('bhtd,bhd->bht', qc, n_vec) + jnp.sum(s_qk, -1)
        h = num / jnp.maximum(jnp.abs(den), jnp.exp(-m_t))[..., None]
        f_last = fcum[..., -1]
        log_s = f_last[..., None] - fcum + ic
        m_new = jnp.maximum(f_last + m_prev, jnp.max(log_s, -1))
        ws = jnp.exp(log_s - m_new[..., None])
        carry_decay = jnp.exp(f_last + m_prev - m_new)
        c_mat = carry_decay[..., None, None] * c_mat + jnp.einsum('bhs,bhsd,bhse->bhde', ws, kc, vc)
        n_vec = carry_decay[..., None] * n_vec + jnp.einsum('bhs,bhsd->bhd', ws, kc)
        return (c_mat, n_vec, m_new), h

    carry0 = (jnp.zeros((bsz, nh, dk, dv), F32), jnp.zeros((bsz, nh, dk), F32), jnp.full((bsz, nh), -1e30, F32))
    _, h = lax.scan(chunk, carry0, tuple(_to_chunks(t) for t in (q, k, v, i_pre, log_f)))
    return _from_chunks(h)

def mlstm_mix(zC, conv_w, conv_b, i_bias, f_bias, norm_w):
    q, k, v, o, ig, fg = _split(zC, MLSTM_SPLITS)
    qk = jax.nn.silu(_causal_conv(jnp.concatenate([q, k], -1), conv_w, conv_b))
    q, k = _split(qk, (BRANCH_WIDTH, BRANCH_WIDTH))
    qh = _to_heads(q, MLSTM_HEADS)
    kh = _to_heads(k, MLSTM_HEADS) * MLSTM_HEAD_DIM ** -0.5
    vh = _to_heads(v, MLSTM_HEADS)
    i_pre = (ig + i_bias).transpose(0, 2, 1)
    log_f = jax.nn.log_sigmoid(fg + f_bias).transpose(0, 2, 1)
    h = _mlstm_chunked(qh, kh, vh, i_pre, log_f)
    h = _head_layernorm(_from_heads(h), NORM_EPS) * norm_w
    return jax.nn.sigmoid(o) * h

def _linear_combine(left, right):
    a_l, b_l = left
    a_r, b_r = right
    return a_l * a_r, a_r * b_l + b_r

def rglru_mix(zD, conv_w, conv_b, wx, bx, wa, ba, lam):
    xr, gate = _split(zD, (BRANCH_WIDTH, BRANCH_WIDTH))
    xc = _causal_conv(xr, conv_w, conv_b)
    bsz, seq = xc.shape[:2]
    xb = xc.reshape(bsz, seq, LRU_BLOCKS, LRU_BLOCK_DIM)
    gate_x = jax.nn.sigmoid(jnp.einsum('bsgi,gij->bsgj', xb, wx) + bx).reshape(bsz, seq, BRANCH_WIDTH)
    gate_a = jax.nn.sigmoid(jnp.einsum('bsgi,gij->bsgj', xb, wa) + ba).reshape(bsz, seq, BRANCH_WIDTH)
    log_a = LRU_C * gate_a * jax.nn.log_sigmoid(lam)
    mult = jnp.sqrt(-jnp.expm1(2.0 * log_a)).at[:, 0].set(1.0)
    _, h = lax.associative_scan(_linear_combine, (jnp.exp(log_a), mult * gate_x * xc), axis=1)
    return h * jax.nn.gelu(gate)

def _expert_ffn(xb, w_gu, b_gu, w_down, b_down):
    gu = xb @ w_gu + b_gu
    gate, up = gu[:, :D_EXPERT], gu[:, D_EXPERT:]
    gate = jnp.minimum(gate, SWIGLU_LIMIT)
    up = jnp.clip(up, -SWIGLU_LIMIT, SWIGLU_LIMIT)
    glu = gate * jax.nn.sigmoid(SWIGLU_ALPHA * gate)
    return ((up + 1.0) * glu) @ w_down + b_down

def moe(xf, router_w, router_b, w_gu, b_gu, w_down, b_down):
    n_tok = xf.shape[0]
    logits = (xf @ router_w + router_b).astype(F32)
    top_val, top_idx = lax.top_k(logits, TOP_K)
    gate = jax.nn.softmax(top_val, axis=-1)
    n_assign = n_tok * TOP_K
    n_blocks = -(-n_assign // EXPERT_BLOCK) + N_EXPERTS
    n_slots = n_blocks * EXPERT_BLOCK
    e_flat = top_idx.reshape(-1)
    order = jnp.argsort(e_flat)
    e_sorted = e_flat[order]
    counts = jnp.bincount(e_flat, length=N_EXPERTS)
    padded = (counts + EXPERT_BLOCK - 1) // EXPERT_BLOCK * EXPERT_BLOCK
    start = jnp.cumsum(counts) - counts
    pad_end = jnp.cumsum(padded)
    pad_start = pad_end - padded
    dest = pad_start[e_sorted] + jnp.arange(n_assign) - start[e_sorted]
    slot_tok = jnp.zeros((n_slots,), jnp.int32).at[dest].set((order // TOP_K).astype(jnp.int32))
    slot_w = jnp.zeros((n_slots,), F32).at[dest].set(gate.reshape(-1)[order])
    block_e = jnp.minimum(jnp.searchsorted(pad_end, jnp.arange(n_blocks) * EXPERT_BLOCK, side='right'), N_EXPERTS - 1)
    xs = xf[slot_tok].reshape(n_blocks, EXPERT_BLOCK, -1)

    def run_block(args):
        xb, e = args
        return _expert_ffn(xb, w_gu[e], b_gu[e], w_down[e], b_down[e])

    ys = lax.map(run_block, (xs, block_e)).reshape(n_slots, -1)
    return jnp.zeros(xf.shape, F32).at[slot_tok].add(ys.astype(F32) * slot_w[:, None])

def first_inputs(seed: int = 0) -> dict:
    key = jax.random.key(seed)
    ks = iter(jax.random.split(key, 64))
    L, W, D = DEPTH, BRANCH_WIDTH, D_MODEL

    def nrm(shape, scale):
        return scale * jax.random.normal(next(ks), shape, F32)

    def uni(shape, lo, hi):
        return jax.random.uniform(next(ks), shape, F32, lo, hi)

    return {
        'x': nrm((BATCH, SEQ, D), 1.0),
        'p': nrm((L, BATCH, SEQ, D_PLE), 1.0),
        'w_in_first': nrm((D, N_COLS_BASE), D ** -0.5),
        'w_in_rest': nrm((L - 1, D, N_COLS_REST), D ** -0.5),
        'rwkv_mu': uni((L, RWKV_COLS), 0.0, 1.0),
        'rwkv_w0': uni((L, W), -6.0, 0.0),
        'rwkv_w2': nrm((L, RWKV_DECAY_RANK, W), 0.5 * RWKV_DECAY_RANK ** -0.5),
        'rwkv_a0': nrm((L, W), 0.1),
        'rwkv_a2': nrm((L, RWKV_ICL_RANK, W), 0.5 * RWKV_ICL_RANK ** -0.5),
        'rwkv_v0': nrm((L - 1, W), 0.1),
        'rwkv_v2': nrm((L - 1, RWKV_VALUE_RANK, W), 0.5 * RWKV_VALUE_RANK ** -0.5),
        'rwkv_g2': nrm((L, RWKV_GATE_RANK, W), RWKV_GATE_RANK ** -0.5),
        'rwkv_k_k': 0.85 + nrm((L, W), 0.05),
        'rwkv_k_a': 1.0 + nrm((L, W), 0.05),
        'rwkv_r_k': nrm((L, RWKV_HEADS, RWKV_HEAD_DIM), 0.1),
        'rwkv_lnx_g': 1.0 + nrm((L, W), 0.05),
        'rwkv_lnx_b': nrm((L, W), 0.02),
        'hgrn_lower_bounds': nrm((L, W), 1.0),
        'hgrn_norm_w': 1.0 + nrm((L, W), 0.05),
        'mlstm_conv_w': nrm((L, CONV_WIDTH, 2 * W), CONV_WIDTH ** -0.5),
        'mlstm_conv_b': nrm((L, 2 * W), 0.02),
        'mlstm_i_bias': nrm((L, MLSTM_HEADS), 0.1),
        'mlstm_f_bias': jnp.linspace(3.0, 6.0, MLSTM_HEADS, dtype=F32) + nrm((L, MLSTM_HEADS), 0.1),
        'mlstm_norm_w': 1.0 + nrm((L, W), 0.05),
        'lru_conv_w': nrm((L, CONV_WIDTH, W), CONV_WIDTH ** -0.5),
        'lru_conv_b': nrm((L, W), 0.02),
        'lru_wx': nrm((L, LRU_BLOCKS, LRU_BLOCK_DIM, LRU_BLOCK_DIM), LRU_BLOCK_DIM ** -0.5),
        'lru_bx': nrm((L, LRU_BLOCKS, LRU_BLOCK_DIM), 0.02),
        'lru_wa': nrm((L, LRU_BLOCKS, LRU_BLOCK_DIM, LRU_BLOCK_DIM), LRU_BLOCK_DIM ** -0.5),
        'lru_ba': nrm((L, LRU_BLOCKS, LRU_BLOCK_DIM), 0.02),
        'lru_lambda': uni((L, W), 3.5, 9.0),
        'w_branch': nrm((L, N_BRANCH, W, D), W ** -0.5),
        'w_out': nrm((L, D, D), DEEPNORM_BETA * D ** -0.5),
        'ln1_g': 1.0 + nrm((L, D), 0.05),
        'ln1_b': nrm((L, D), 0.02),
        'router_w': nrm((L, D, N_EXPERTS), D ** -0.5),
        'router_b': nrm((L, N_EXPERTS), 0.01),
        'expert_w_gu': nrm((L, N_EXPERTS, D, 2 * D_EXPERT), D ** -0.5),
        'expert_b_gu': nrm((L, N_EXPERTS, 2 * D_EXPERT), 0.02),
        'expert_w_down': nrm((L, N_EXPERTS, D_EXPERT, D), DEEPNORM_BETA * D_EXPERT ** -0.5),
        'expert_b_down': nrm((L, N_EXPERTS, D), 0.02),
        'ple_gate_w': nrm((L, D, D), D ** -0.5),
        'ple_proj_w': nrm((L, D_PLE, D), DEEPNORM_BETA * D_PLE ** -0.5),
        'ln2_g': 1.0 + nrm((L, D), 0.05),
        'ln2_b': nrm((L, D), 0.02),
    }

def first_block(x, p, w_in_first, w_in_rest, rwkv_mu, rwkv_w0, rwkv_w2, rwkv_a0, rwkv_a2, rwkv_v0, rwkv_v2,
              rwkv_g2, rwkv_k_k, rwkv_k_a, rwkv_r_k, rwkv_lnx_g, rwkv_lnx_b, hgrn_lower_bounds, hgrn_norm_w,
              mlstm_conv_w, mlstm_conv_b, mlstm_i_bias, mlstm_f_bias, mlstm_norm_w, lru_conv_w, lru_conv_b,
              lru_wx, lru_bx, lru_wa, lru_ba, lru_lambda, w_branch, w_out, ln1_g, ln1_b, router_w, router_b,
              expert_w_gu, expert_b_gu, expert_w_down, expert_b_down, ple_gate_w, ple_proj_w, ln2_g, ln2_b):
    dt = x.dtype
    bsz, seq, _ = x.shape
    lb_all = jnp.cumsum(jax.nn.softmax(hgrn_lower_bounds.astype(F32), axis=0), axis=0)
    lb_all = lb_all - lb_all[0]
    v_first = None
    for layer in range(DEPTH):
        w_in = w_in_first if layer == 0 else w_in_rest[layer - 1]
        z = (x @ w_in).astype(F32)
        zA, zB, zC, zD, zG = _split(z[..., :N_COLS_BASE], (RWKV_COLS, HGRN_COLS, MLSTM_COLS, LRU_COLS, GATE_COLS))
        v_mix = None if layer == 0 else rwkv_v0[layer - 1] + z[..., N_COLS_BASE:] @ rwkv_v2[layer - 1]
        yA, v_cur = rwkv7_mix(zA, v_first, v_mix, rwkv_mu[layer], rwkv_w0[layer], rwkv_w2[layer], rwkv_a0[layer],
                              rwkv_a2[layer], rwkv_g2[layer], rwkv_k_k[layer], rwkv_k_a[layer], rwkv_r_k[layer],
                              rwkv_lnx_g[layer], rwkv_lnx_b[layer])
        if layer == 0:
            v_first = v_cur
        yB = hgrn2_mix(zB, lb_all[layer], hgrn_norm_w[layer])
        yC = mlstm_mix(zC, mlstm_conv_w[layer], mlstm_conv_b[layer], mlstm_i_bias[layer], mlstm_f_bias[layer],
                       mlstm_norm_w[layer])
        yD = rglru_mix(zD, lru_conv_w[layer], lru_conv_b[layer], lru_wx[layer], lru_bx[layer], lru_wa[layer],
                       lru_ba[layer], lru_lambda[layer])
        gates = jax.nn.sigmoid(zG).reshape(bsz, seq, N_BRANCH, D_MODEL)
        merged = jnp.zeros((bsz, seq, D_MODEL), F32)
        for n, yb in enumerate((yA, yB, yC, yD)):
            merged = merged + gates[:, :, n] * (yb @ w_branch[layer, n])
        mix = merged @ w_out[layer]
        x = _layernorm(DEEPNORM_ALPHA * x + mix, ln1_g[layer], ln1_b[layer], dt)
        moe_out = moe(x.reshape(bsz * seq, D_MODEL), router_w[layer], router_b[layer], expert_w_gu[layer],
                      expert_b_gu[layer], expert_w_down[layer], expert_b_down[layer]).reshape(bsz, seq, D_MODEL)
        ple = jax.nn.sigmoid(x @ ple_gate_w[layer]) * (p[layer] @ ple_proj_w[layer])
        x = _layernorm(DEEPNORM_ALPHA * x + moe_out + ple, ln2_g[layer], ln2_b[layer], dt)
    return x


HEAD_DIM = 64
HEADS_PER_GROUP = 8
ATTN_GROUPS = ((128, 1), (512, 4), (2048, 16))
N_GROUPS = len(ATTN_GROUPS)
N_ATTN_HEADS = N_GROUPS * HEADS_PER_GROUP
ATTN_WIDTH = HEADS_PER_GROUP * HEAD_DIM
QKV_WIDTH = N_GROUPS * 3 * ATTN_WIDTH
BLOCK = 128
POOL_WINDOWS = (2, 4, 8, 16)
POOL_GROUPS = len(POOL_WINDOWS)
POOL_WIDTH = D_MODEL // 2
PGW = POOL_WIDTH // POOL_GROUPS
NUM_BUCKETS = 32
MAX_DISTANCE = 2048
EPS = 1e-6
SPLIT_SIZES = (QKV_WIDTH, ATTN_WIDTH, POOL_WIDTH, POOL_WIDTH, D_MODEL, D_MODEL)
SPLIT_POINTS = (QKV_WIDTH,
                QKV_WIDTH + ATTN_WIDTH,
                QKV_WIDTH + ATTN_WIDTH + POOL_WIDTH,
                QKV_WIDTH + ATTN_WIDTH + 2 * POOL_WIDTH,
                QKV_WIDTH + ATTN_WIDTH + 2 * POOL_WIDTH + D_MODEL)
IN_WIDTH = QKV_WIDTH + ATTN_WIDTH + 2 * POOL_WIDTH + 2 * D_MODEL


def rmsnorm(x, g):
    xf = x.astype(jnp.float32)
    y = xf * lax.rsqrt(jnp.mean(xf * xf, axis=-1, keepdims=True) + EPS)
    return (y * g.astype(jnp.float32)).astype(x.dtype)

def t5_bucket(n):
    max_exact = NUM_BUCKETS // 2
    nf = jnp.maximum(n, 1).astype(jnp.float32)
    large = max_exact + (jnp.log(nf / max_exact) / math.log(MAX_DISTANCE / max_exact)
                         * (NUM_BUCKETS - max_exact)).astype(jnp.int32)
    large = jnp.minimum(large, NUM_BUCKETS - 1)
    return jnp.where(n < max_exact, n, large)

def to_sub(t, dil):
    B, S = t.shape[:2]
    L = S // dil
    t = t.reshape((B, L, dil) + t.shape[2:])
    t = jnp.moveaxis(t, 2, 1)
    return t.reshape((B * dil, L) + t.shape[3:])

def from_sub(t, B, dil):
    L = t.shape[1]
    t = t.reshape((B, dil, L) + t.shape[2:])
    t = jnp.moveaxis(t, 1, 2)
    return t.reshape((B, L * dil) + t.shape[3:])

def dilated_window_attention(q, k, v, dil, n_back, bias_g):
    B, S, H, Dh = q.shape
    L = S // dil
    nb = -(-L // BLOCK)
    pad = nb * BLOCK - L
    Bd = B * dil

    def sub(t):
        return jnp.pad(to_sub(t, dil), ((0, 0), (0, pad), (0, 0), (0, 0)))

    def band(t):
        tp = jnp.pad(t, ((0, 0), (BLOCK, 0), (0, 0), (0, 0)))
        prev = tp[:, :-BLOCK].reshape(Bd, nb, BLOCK, H, Dh)
        cur = t.reshape(Bd, nb, BLOCK, H, Dh)
        return jnp.concatenate([prev, cur], axis=2)

    qb = sub(q).reshape(Bd, nb, BLOCK, H, Dh)
    kb = band(sub(k))
    vb = band(sub(v))

    i = jnp.arange(BLOCK)[:, None]
    j = jnp.arange(2 * BLOCK)[None, :]
    dist = BLOCK + i - j
    band_ok = (dist >= 0) & (dist <= n_back)
    key_ok = (jnp.arange(nb)[:, None, None] * BLOCK - BLOCK + j[None]) >= 0
    mask = band_ok[None] & key_ok
    bucket = t5_bucket(jnp.clip(dist, 0, n_back) * dil)
    bias = jnp.transpose(bias_g[bucket].astype(jnp.float32), (2, 0, 1))

    logits = jnp.einsum('znqhd,znkhd->znhqk', qb, kb).astype(jnp.float32) * (HEAD_DIM ** -0.5)
    logits = jnp.where(mask[None, :, None], logits + bias[None, None], -jnp.inf)
    m = jnp.max(logits, axis=-1, keepdims=True)
    p = jnp.exp(logits - m)
    denom = jnp.sum(p, axis=-1)
    o = jnp.einsum('znhqk,znkhd->znqhd', p.astype(vb.dtype), vb).astype(jnp.float32)
    o = o / jnp.moveaxis(denom, 2, 3)[..., None]
    lse = jnp.moveaxis(m[..., 0] + jnp.log(denom), 2, 3)

    o = o.reshape(Bd, nb * BLOCK, H, Dh)[:, :L]
    lse = lse.reshape(Bd, nb * BLOCK, H)[:, :L]
    return from_sub(o, B, dil), from_sub(lse, B, dil)

def multiscale_pool(u):
    B, S, C = u.shape
    uf = u.astype(jnp.float32)
    csp = jnp.pad(jnp.cumsum(uf, axis=1), ((0, 0), (1, 0), (0, 0)))
    t = jnp.arange(S)
    outs = []
    for g, win in enumerate(POOL_WINDOWS):
        cg = csp[:, :, g * PGW:(g + 1) * PGW]
        lo = jnp.maximum(t + 1 - win, 0)
        s = cg[:, 1:] - cg[:, lo]
        cnt = jnp.minimum(t + 1, win).astype(jnp.float32)
        outs.append(s / cnt[None, :, None])
    return jnp.concatenate(outs, axis=-1) - uf

def second_inputs(seed: int = 0) -> dict:
    key = jax.random.key(seed)
    ks = jax.random.split(key, 14)
    f32 = jnp.float32
    nrm = lambda k, shape, s: (jax.random.normal(k, shape, f32) * s).astype(f32)
    return {
        "x": nrm(ks[0], (BATCH, SEQ, D_MODEL), 1.0),
        "c": nrm(ks[1], (BATCH, D_MODEL), 1.0),
        "norm_g": 1.0 + nrm(ks[2], (DEPTH, D_MODEL), 0.05),
        "w_ada": nrm(ks[3], (DEPTH, D_MODEL, 3 * D_MODEL), 0.5 * D_MODEL ** -0.5),
        "b_ada": nrm(ks[4], (DEPTH, 3 * D_MODEL), 0.01),
        "w_in": nrm(ks[5], (DEPTH, D_MODEL, IN_WIDTH), D_MODEL ** -0.5),
        "pool_w": nrm(ks[6], (DEPTH, POOL_GROUPS, PGW, PGW), PGW ** -0.5),
        "pool_scale": 1.0 + nrm(ks[7], (DEPTH, POOL_WIDTH), 0.1),
        "w_attn_br": nrm(ks[8], (DEPTH, ATTN_WIDTH, D_MODEL), ATTN_WIDTH ** -0.5),
        "w_pool_br": nrm(ks[9], (DEPTH, POOL_WIDTH, D_MODEL), POOL_WIDTH ** -0.5),
        "w_out": nrm(ks[10], (DEPTH, D_MODEL, D_MODEL), D_MODEL ** -0.5),
        "rel_bias": nrm(ks[11], (NUM_BUCKETS, N_ATTN_HEADS), 0.5),
        "final_g": 1.0 + nrm(ks[12], (D_MODEL,), 0.05),
    }

def second_block(x, c, norm_g, w_ada, b_ada, w_in, pool_w, pool_scale, w_attn_br, w_pool_br, w_out, rel_bias, final_g):
    B, S, D = x.shape
    for l in range(DEPTH):
        mod = c @ w_ada[l] + b_ada[l]
        shift, scale, gate = jnp.split(mod, 3, axis=-1)
        h = rmsnorm(x, norm_g[l]) * (1.0 + scale[:, None]) + shift[:, None]

        proj = h @ w_in[l]
        qkv, z_attn, u_pool, z_pool, g_attn, g_pool = jnp.split(proj, SPLIT_POINTS, axis=-1)
        qkv = qkv.reshape(B, S, N_GROUPS, 3, HEADS_PER_GROUP, HEAD_DIM)

        outs, lses = [], []
        for gi, (win, dil) in enumerate(ATTN_GROUPS):
            bias_g = rel_bias[:, gi * HEADS_PER_GROUP:(gi + 1) * HEADS_PER_GROUP]
            o, lse = dilated_window_attention(qkv[:, :, gi, 0], qkv[:, :, gi, 1], qkv[:, :, gi, 2],
                                              dil, win // dil, bias_g)
            outs.append(o)
            lses.append(lse)
        wts = jax.nn.softmax(jnp.stack(lses, axis=0), axis=0)
        attn = jnp.sum(wts[..., None] * jnp.stack(outs, axis=0), axis=0)
        attn = attn.reshape(B, S, ATTN_WIDTH).astype(x.dtype)
        y_attn = (attn * jax.nn.silu(z_attn)) @ w_attn_br[l]

        pooled = multiscale_pool(u_pool).reshape(B, S, POOL_GROUPS, PGW)
        mixed = jnp.einsum('bsgc,gce->bsge', pooled, pool_w[l].astype(jnp.float32))
        mixed = (mixed.reshape(B, S, POOL_WIDTH) * pool_scale[l]).astype(x.dtype)
        y_pool = (mixed * jax.nn.silu(z_pool)) @ w_pool_br[l]

        merged = jax.nn.sigmoid(g_attn) * y_attn + jax.nn.sigmoid(g_pool) * y_pool
        x = x + gate[:, None] * (merged @ w_out[l])
    return rmsnorm(x, final_g)


def setup_inputs(seed=0):
    out = dict(first_inputs(seed))
    for name, value in second_inputs(seed + 1).items():
        if name != "x":
            out[name + "_2"] = value
    return out


def reference(
    x, p, w_in_first, w_in_rest, rwkv_mu, rwkv_w0, rwkv_w2, rwkv_a0, rwkv_a2, rwkv_v0, rwkv_v2,
    rwkv_g2, rwkv_k_k, rwkv_k_a, rwkv_r_k, rwkv_lnx_g, rwkv_lnx_b, hgrn_lower_bounds,
    hgrn_norm_w, mlstm_conv_w, mlstm_conv_b, mlstm_i_bias, mlstm_f_bias, mlstm_norm_w,
    lru_conv_w, lru_conv_b, lru_wx, lru_bx, lru_wa, lru_ba, lru_lambda, w_branch, w_out, ln1_g,
    ln1_b, router_w, router_b, expert_w_gu, expert_b_gu, expert_w_down, expert_b_down,
    ple_gate_w, ple_proj_w, ln2_g, ln2_b, c_2, norm_g_2, w_ada_2, b_ada_2, w_in_2, pool_w_2,
    pool_scale_2, w_attn_br_2, w_pool_br_2, w_out_2, rel_bias_2, final_g_2,
):
    x = first_block(
        x, p, w_in_first, w_in_rest, rwkv_mu, rwkv_w0, rwkv_w2, rwkv_a0, rwkv_a2, rwkv_v0,
        rwkv_v2, rwkv_g2, rwkv_k_k, rwkv_k_a, rwkv_r_k, rwkv_lnx_g, rwkv_lnx_b,
        hgrn_lower_bounds, hgrn_norm_w, mlstm_conv_w, mlstm_conv_b, mlstm_i_bias, mlstm_f_bias,
        mlstm_norm_w, lru_conv_w, lru_conv_b, lru_wx, lru_bx, lru_wa, lru_ba, lru_lambda,
        w_branch, w_out, ln1_g, ln1_b, router_w, router_b, expert_w_gu, expert_b_gu,
        expert_w_down, expert_b_down, ple_gate_w, ple_proj_w, ln2_g, ln2_b,
    )
    return second_block(
        x, c_2, norm_g_2, w_ada_2, b_ada_2, w_in_2, pool_w_2, pool_scale_2, w_attn_br_2,
        w_pool_br_2, w_out_2, rel_bias_2, final_g_2,
    )


_drawn_inputs = setup_inputs


def setup_inputs(seed=0):
    import zlib

    import numpy as np

    out = dict(_drawn_inputs(seed))
    spreads = {}
    factors = {'rwkv_w2': 4.174,
     'rwkv_a0': 3.367,
     'rwkv_k_k': 3.4,
     'rwkv_k_a': 3.491,
     'rwkv_lnx_g': 4.004,
     'rwkv_lnx_b': 6.003,
     'hgrn_norm_w': 3.9,
     'mlstm_conv_b': 5.312,
     'mlstm_i_bias': 200.0,
     'mlstm_norm_w': 3.444,
     'lru_bx': 22.247,
     'lru_ba': 37.956,
     'router_b': 2.779,
     'expert_b_gu': 8.0,
     'expert_b_down': 6.397,
     'ln2_b': 2.947,
     'norm_g_2': 3.534,
     'b_ada_2': 8.0,
     'pool_scale_2': 2.982}
    for name, (base, spread) in spreads.items():
        noise = np.random.default_rng([zlib.crc32(name.encode()), seed]).standard_normal(out[name].shape)
        drawn = base * np.exp(spread * noise) if base else spread * noise
        out[name] = jnp.asarray(drawn.astype(out[name].dtype))
    for name, factor in factors.items():
        out[name] = (out[name] * factor).astype(out[name].dtype)
    return out
```

```python
import numpy as np
import concourse.bass as bass
from concourse import mybir
from contextlib import ExitStack

F32 = mybir.dt.float32
I32 = mybir.dt.int32
ALU = mybir.AluOpType
ACT = mybir.ActivationFunctionType
AX = mybir.AxisListType

P = 128
T = 256
TT = T // P
D = 1024
KD = D // P
W = 512
KW = W // P
CH = 64
A_COL, B_COL, C_COL, D_COL, G_COL = 0, 1792, 3840, 5896, 6920
ALPHA = 2.0 ** 0.25
E_HALF = float(np.exp(np.float64(-0.5)))
NEG = -1e30
EXPERTS = 32
CAP = 64
GU = 2 * D
HEADS = 8
UNUSED = ("hgrn_lower_bounds",)
GROUPS = 3

CONST = {}


def _place():
    at = 0
    for name, n in (("ident", 128), ("headsum", 128), ("level", 7 * 128), ("strict64", 128), ("upper64", 128),
                    ("upper", 128), ("strict", 128), ("ones", 256), ("flip", 128), ("slot", 64), ("reset64", 256),
                    ("poolcnt", 1024), ("headrow", 1024)):
        CONST[name] = (at, n)
        at += n
    return at


NCONST = _place()
BKT = 384


def constants():
    c = np.zeros((P, NCONST), np.float32)
    s, t = np.arange(P)[:, None], np.arange(P)[None, :]

    def put(name, v):
        at, n = CONST[name]
        c[:, at:at + n] = np.broadcast_to(v, (P, n))

    put("ident", s == t)
    put("headsum", s // CH == t // CH)
    put("level", np.concatenate([(s // (2 * h) == t // (2 * h)) & (s % (2 * h) < h) & (t % (2 * h) >= h)
                                 for h in (1, 2, 4, 8, 16, 32, 64)], 1))
    put("strict64", (s // CH == t // CH) & (s < t))
    put("upper64", (s // CH == t // CH) & (s <= t))
    put("upper", s <= t)
    put("strict", s < t)
    put("ones", 1.0)
    put("flip", s + t == P - 1)
    put("slot", np.arange(64)[None, :])
    put("reset64", (np.arange(256) % CH != 0)[None, :])
    put("poolcnt", np.concatenate([1.0 / np.minimum(np.arange(T) + 1, w) for w in (2, 4, 8, 16)])[None, :])
    put("headrow", np.arange(1024)[None, :] // P == s)
    return c


def bias_tables():
    n = 255 - np.arange(BKT)
    m = np.clip(n, 0, 255)
    nf = np.maximum(m, 1).astype(np.float32)
    large = 16 + (np.log(nf / np.float32(16)) / np.float32(np.log(2048 / 16)) * np.float32(16)).astype(np.int32)
    bucket = np.where(m < 16, m, np.minimum(large, 31))
    hot = (bucket[None, :] == np.arange(32)[:, None]) * 8.0 * (n >= 0)
    mask = np.zeros((24, BKT), np.float32)
    for h in range(24):
        dil = (1, 4, 16)[h // 8]
        ok = (n >= 0) & (n % dil == 0) & (n <= 128 * dil)
        mask[h] = np.where(ok, 0.0, NEG)
    return hot.astype(np.float32), mask

VEC = {}


def _place_vectors():
    at = 0
    for name, n in (("rwkv_mu", 14), ("rwkv_w0", 4), ("rwkv_a0", 4), ("rwkv_k_k", 4), ("rwkv_k_a", 4), ("rwkv_r_k", 4),
                    ("rwkv_lnx_g", 4), ("rwkv_lnx_b", 4), ("hgrn_norm_w", 4), ("mlstm_conv_w", 32),
                    ("mlstm_conv_b", 8), ("mlstm_norm_w", 4), ("lru_conv_w", 16), ("lru_conv_b", 4), ("lru_bx", 4),
                    ("lru_ba", 4), ("lru_lambda", 4), ("pool_scale_2", 4)):
        VEC[name] = (at, n)
        at += n
    return at


NVEC = _place_vectors()

UNITS = (["D xr", "D gate", "C q", "C k", "C v", "C o", "C if", "B q", "B f", "B i", "B g",
          "G D 0", "G D 1", "Wb D", "A r", "A k", "A v", "A x",
          "G C 0", "G C 1", "Wb C", "G B 0", "G B 1", "Wb B", "G A 0", "G A 1", "Wb A", "out 0", "out 1", "ada 0", "ada 1", "ada 2", "ada 3", "ada 4", "ada 5",
          "ple 0", "ple 1", "pp"])
QKV = [f"{c}{g}" for g in range(GROUPS) for c in "QKV"]
UNITS2 = QKV + ["Z", "U", "ZP", "g2a 0", "g2a 1", "Wb2a", "g2p 0", "g2p 1", "Wb2p", "out2 0", "out2 1"]
COL2 = {n: i * W for i, n in enumerate(QKV + ["Z", "U", "ZP", "g2a 0", "g2a 1", "g2p 0", "g2p 1"])}
PROJ = (["D xr 0", "D xr 1", "D gate 0", "D gate 1", "C q 0", "C q 1", "C k 0", "C k 1", "C v 0", "C v 1",
         "C o 0", "C o 1", "C if", "B q 0", "B q 1", "B f 0", "B f 1", "B i 0", "B i 1", "B g 0", "B g 1",
         "G D 0", "G D 1", "G D 2", "G D 3", "A r 0", "A r 1", "A k 0", "A k 1", "A v 0", "A v 1", "A x",
         "G C 0", "G C 1", "G C 2", "G C 3", "G B 0", "G B 1", "G B 2", "G B 3", "G A 0", "G A 1", "G A 2", "G A 3"]
        + [f"{n} {i}" for n in QKV for i in range(2)] + ["L 0 0", "L 0 1", "L 0 2"]
        + [x for h in range(HEADS) for x in
           ([f"L {h + 1} {i}" for i in range(3)] if h < 7 else [])
           + [f"{n} {i}" for n in {0: ["Z"], 1: ["U"], 2: ["ZP"]}.get(h, []) for i in range(2)]]
        + [f"{n} {i}" for n in ("g2a", "g2p") for i in range(4)])
SMALL = (["vectors"] + [f"x {i}" for i in range(4)]
         + ["D gx 0", "D gx 1", "D ga 0", "D ga 1"]
         + ["C row 0", "C row 1", "C col"] + [f"C S {h}" for h in range(4)]
         + ["C num 0", "C num 1", "C den", "C yT 0", "C yT 1"]
         + [f"Wb D {i}" for i in range(4)]
         + ["B diag 0", "B diag 1"] + [f"B level {l} {j}" for l in range(7) for j in range(2)] + ["B cross"]
         + ["B o 0", "B o 1", "B yT 0", "B yT 1"]
         + ["A w 0", "A w 1", "A a 0", "A a 1", "A g 0", "A g 1", "A kk 0", "A kk 1"]
         + [f"A V {i}" for i in range(2)] + ["A bonus 0", "A bonus 1"]
         + [f"A {n} {i}" for n in ("At", "Bt", "Kt") for i in range(2)]
         + [f"A NT {i}" for i in range(4)] + [f"A X0 {i}" for i in range(4)]
         + [f"Wb C {i}" for i in range(4)]
         + [f"A {n}{l} {i}" for l in range(1, 6) for n in ("X", "D", "DT") if (n, l) != ("D", 5) for i in range(4)]
         + [f"Wb B {i}" for i in range(4)]
         + [f"A AkT {i}" for i in range(4)]
         + ["A GT 0", "A GT 1", "A W 0", "A W 1", "A U0 0", "A U0 1"]
         + ["A S 0", "A U 1 0", "A U 1 1", "A S 1", "A U 2 0", "A U 2 1", "A S 2", "A U 3 0", "A U 3 1"]
         + [f"A RbT {i}" for i in range(4)] + [f"A RkT {i}" for i in range(4)]
         + ["A Y 0", "A Y 1", "A Y 2", "A Y 3", "A yT 0", "A yT 1"]
         + [f"Wb A {i}" for i in range(4)] + [f"mix {i}" for i in range(4)]
         + ["vectors2"] + [f"ada {i}" for i in range(6)] + ["gate8", "gateB 0", "gateB 1", "bias"]
         + [f"x1 {i}" for i in range(4)] + ["logits", "gateT", "rank", "pT"]
         + [f"ple {i}" for i in range(4)] + [f"pp {i}" for i in range(4)]
         + [f"h {i}" for i in range(4)]
         + [f"{n} {h}" + s_ for h in range(HEADS) for n, s_ in (("T", " 0"), ("T", " 1"), ("T", " 2"), ("O", ""))]
         + ["aT 0", "aT 1", "pool 0", "pool 1"]
         + [f"{n} {i}" for n in ("Wb2a", "Wb2p", "mix2") for i in range(4)])

ARENA = 53200
UNIT = 4096
RING = ARENA - 6 * UNIT
HIGH = RING + 3 * UNIT


def unit_no(name):
    return UNITS.index(name)


def unit2_no(name):
    return UNITS2.index(name)


def proj_no(name):
    return PROJ.index(name)


def small_no(name):
    return SMALL.index(name)


def build(nc, ins, consts, outs):
    stack = ExitStack()
    with stack:
        arena = stack.enter_context(nc.sbuf_tensor("arena", [P, ARENA], F32))
        proj_bank = [stack.enter_context(nc.psum_tensor(f"proj{i}", [P, 512], F32)) for i in range(4)]
        small_bank = [stack.enter_context(nc.psum_tensor(f"small{i}", [P, 512], F32)) for i in range(4)]
        scratch = nc.dram_tensor("bias_rows", (24, BKT), F32).ap()
        signals = {}

        def sig(name):
            if name not in signals:
                signals[name] = stack.enter_context(nc.semaphore(name.replace(" ", "_")))
            return signals[name]

        def room(at, *shape):
            n = int(np.prod(shape))
            v = arena[:, at:at + n]
            if len(shape) == 2:
                v = v.rearrange("p (a b) -> p a b", b=shape[1])
            if len(shape) == 3:
                v = v.rearrange("p (a b c) -> p a b c", b=shape[1], c=shape[2])
            return v

        def over(v, n):
            return v.unsqueeze(len(v.shape)).to_broadcast(list(v.shape) + [n])

        def along(v, n):
            return v.unsqueeze(1).to_broadcast([v.shape[0], n, v.shape[1]])

        at = 0
        CO = room(at, NCONST); at += NCONST
        PV = room(at, P); at += P
        XTOK = room(at, TT, D); at += TT * D
        XT = room(at, KD, T); at += KD * T
        MERGED = room(at, KD, T); at += KD * T
        SG = room(at, KD, T)
        PROW = room(at, P)
        at += KD * T
        YT = {}
        for n in "DCBA":
            YT[n] = room(at, KW, T); at += KW * T
        WA2 = room(at - 1024, W)
        G2 = room(at - 512, W)
        LOW = at
        assert LOW + 11790 <= RING, (LOW, RING)

        def c(name, lo=0, hi=None):
            a, n = CONST[name]
            return CO[:, a + lo:a + (n if hi is None else hi)]

        def pv(name, lo=0, hi=None):
            a, n = VEC[name]
            return PV[:, a + lo:a + (n if hi is None else hi)]

        ident = c("ident")

        at = HIGH
        xr = room(at, KW, T + 3); at += KW * (T + 3)
        lgate = room(at, KW, T); at += 1024
        xc = room(at, KW, T); at += 1024
        gx = room(at, KW, T); at += 1024
        ga = room(at, KW, T); at += 1024
        lt1 = room(at, KW, T); at += 1024
        lt2 = room(at, KW, T); at += 1024
        WX = room(at, KW, P); at += 512
        WAD = room(at, KW, P); at += 512
        lam = room(at, 5, 4); at += 20
        assert at <= HIGH + 3 * UNIT

        at = LOW
        cz = room(at, 8, T + 3); hC = room(at, 8, P); hC2 = room(at + 1024, 8, P); at += 8 * (T + 3)
        qk = room(at, 8, T); at += 2048
        vC = room(at, TT, W); at += 1024
        oC = room(at, KW, T); at += 1024
        wC = room(at, 4, 384); at += 1536
        sC = room(at, 4, 384); at += 1536
        rows = room(at, 8, T); at += 2048
        iC, fC, uC, gC, mC = (rows[0:4, n, :] for n in range(5))
        e1C, e2C = rows[0:4, 5, :], rows[0:4, 6, :]
        colC = room(at, 2, 8); at += 16
        emC = room(at, 8); at += 8
        denC = room(at, 8); at += 8
        stC = room(at, 4, 8); at += 32
        ifb = room(at, 2); at += 2
        assert at <= RING

        at = HIGH
        qB = room(at, KW, T); at += 1024
        fB = room(at, KW, T); at += 1024
        vB = room(at, TT, W); at += 1024
        gB = room(at, KW, T); at += 1024
        kB = room(at, KW, T); at += 1024
        cB = room(at, KW, T); at += 1024
        eB = room(at, KW, T); at += 1024
        aB = room(at, 8, P); at += 1024
        aX = room(at, 4, P); at += 512
        tB = room(at, KW, T); at += 1024
        tB2 = room(at, KW, T); at += 1024
        stB = room(at, 2, 8); at += 16
        assert at <= HIGH + 3 * UNIT

        at = LOW
        zA = room(at, 14, T + 1); zmix = zA[:, :, 1:T + 1]; at += 14 * (T + 1)
        dA = room(at, 14, T)
        sl = [at + 1024 * i for i in range(8)]
        NTm = room(sl[0], 16, P)
        cumA, aA, kkA, bA, gA, bonusA, e1A, e2A = (room(s, KW, T) for s in sl)
        rA, kA, vA = zmix[:, 0:4], zmix[:, 4:8], zmix[:, 8:12]
        assert sl[7] + 1024 <= RING
        S_all = room(LOW + 8 * (T + 1), 4, 256)
        e3A = aA
        at = HIGH
        Vt = room(at, TT, W); At = room(at + 1024, TT, W)
        Bt = room(at + 2048, TT, W); Kt = room(at + 3072, TT, W); at += 4096
        DTa = room(at, 16, P); at += 2048
        NT = room(at, 16, P); AkT = NT; at += 2048
        X = room(at, 16, P); WU = room(at, TT, W); Ut = room(at + 1024, TT, W); at += 2048
        Da = room(at, 16, P); RbT = Da; at += 2048
        RkT = NTm
        GT = room(sl[7], KW, T)
        Ysum = room(sl[2], TT * 8, CH)
        Ysq = room(sl[3], TT * 8, CH)
        tmpA = room(sl[2], KW, T)
        stA = room(LOW + 12 * (T + 1), 3, 16)

        x1 = XTOK
        mixv = room(HIGH, TT, D)
        bcg = room(HIGH + 2048, D)
        bcb = room(HIGH + 3072, D)
        st1 = room(HIGH + 4096, 2, 12)
        mv1 = room(HIGH + 4096 + 24, 2, 2)
        rs1 = room(HIGH + 4096 + 28, 2)

        base = MERGED.rearrange("p k t -> p (k t)").rearrange("p (j d) -> p j d", j=TT)
        at = LOW
        YSB = room(at, W); at += W
        ESEL = room(at, CAP); at += CAP
        RW = room(at, KD, EXPERTS); at += KD * EXPERTS
        RB = room(at, EXPERTS); at += EXPERTS
        (lg, above, tie, cum, ex, sel, gates_, rank, tmp_r) = (room(at + 64 * n, TT, EXPERTS) for n in range(9)); at += 9 * 64
        mx8 = room(at, TT, 8); at += 16
        few = room(at, 8, TT); at += 16
        load = room(at, EXPERTS); at += EXPERTS
        top = room(at, 4); at += 4
        total = room(at, 1).bitcast(I32); at += 4
        BD = room(at, D)[0:EXPERTS]; at += D
        GTT = room(at, T)[0:EXPERTS]; at += T
        BGU = room(at, GU); at += GU
        PTOK = room(at, TT, T); at += TT * T
        PTT = room(at, TT, T); at += TT * T
        PG = room(at, TT, D)
        ln2g, ln2b = room(at, D), room(at + D, D); at += TT * D
        XG = room(at, 8, CAP); at += 512
        PICK = room(at, TT, CAP); at += TT * CAP
        PICKW = room(at, TT, P); at += TT * P
        PTW = room(at, T); at += T
        GH = room(at, W); at += W
        UH = room(at, W); at += W
        SGH = room(at, W); at += W
        assert at <= RING, (at, RING)
        HM = PTOK.rearrange("p j d -> p (j d)").rearrange("p (m s c) -> p m s c", m=4, s=2)
        gate_bank, up_bank, y_bank, x_bank = small_bank
        acc_bank = proj_bank
        slots = [3, 4, 5, 0, 1, 2]

        at = LOW - 4 * 1024
        PROW2 = room(at, P); at += P
        PV2 = room(at, 40); at += 40
        MODT = room(at, 24); at += 24
        G8 = room(at, P)[0:8]; at += P
        RELB = room(at, 24)[0:32]; at += 24
        HOT = room(at, BKT)[0:32]; at += BKT
        assert at <= LOW - 3 * 1024
        BM = room(at, BKT)[0:24]; at += BKT
        TAB = room(at, BKT)[0:24]; at += BKT
        assert at <= LOW - 2 * 1024
        st2 = room(at, 2, 12); mv2 = room(at + 24, 2, 2); rs2 = room(at + 28, 2); ss2 = room(at + 30, 2)
        rs3 = room(at + 32, 2); ss3 = room(at + 34, 2)
        mod_a = room(at + 36, 8); den = room(at + 44, 2, 4); nmax = room(at + 52, 2, 4)
        gateB = room(LOW - 2 * 1024 + 64, D)
        assert at + 60 <= LOW - 2 * 1024 + 64

        x2 = XTOK
        HT = XT
        at = LOW
        qT, kT, vK = [], [], []
        for g in range(GROUPS):
            qT.append(room(at, KW, T)); kT.append(room(at + 1024, KW, T)); vK.append(room(at + 2048, TT, W)); at += 3072
        u0 = room(at, 4, T + 16); at += 4 * (T + 16)
        zp = room(at, KW, T); at += 1024
        assert at <= RING
        at = HIGH
        HK = room(at, 24, T); at += 24 * T
        PB = [room(at, 1152), room(at + 1152, 1152)]; at += 2304
        PTr = room(at, 1152); at += 1152
        attn = room(at, TT, W); at += 1024
        zat = room(at, TT, W); at += 1024
        assert at <= HIGH + 3 * UNIT
        uA, uB = room(HIGH, 4, T + 16), room(HIGH + 1088, 4, T + 16)
        pooled = room(HIGH + 2176, KW, T)
        attnT = room(HIGH + 3200, KW, T)
        poolT = room(HIGH + 4224, KW, T)
        POOLW = room(HIGH + 5248, 4, P)
        zsig = room(HIGH + 6144, TT, W)
        zpsig = room(HIGH + 7168, KW, T)
        x3 = room(LOW, TT, D)
        MERGED2 = MERGED
        fing = room(LOW + 2048, D)

        def mat(j, h):
            return 8 * j + 4 * (h % 2) + h // 2

        def ring(n):
            return RING + (n % 3) * UNIT

        w_in = ins["w_in_first"]

        def unit_source(name):
            col = {"D xr": D_COL, "D gate": D_COL + W, "C q": C_COL, "C k": C_COL + W, "C v": C_COL + 2 * W,
                   "C o": C_COL + 3 * W, "B q": B_COL, "B f": B_COL + W, "B i": B_COL + 2 * W, "B g": B_COL + 3 * W,
                   "A r": 0, "A k": W, "A v": 2 * W}
            for n, b in enumerate("ABCD"):
                col[f"G {b} 0"] = G_COL + n * D
                col[f"G {b} 1"] = G_COL + n * D + W
            if name in col:
                return w_in[:, col[name]:col[name] + W].rearrange("(k p) n -> p k n", p=P), (KD, W)
            if name == "C if":
                return w_in[:, C_COL + 4 * W:C_COL + 4 * W + 8].rearrange("(k p) n -> p k n", p=P), (KD, 8)
            if name == "A x":
                return w_in[:, 3 * W:3 * W + 256].rearrange("(k p) n -> p k n", p=P), (KD, 256)
            if name.startswith("Wb"):
                return ins["w_branch"][0, "ABCD".index(name[-1])].rearrange("(k p) n -> p k n", p=P), (KW, D)
            half = int(name[-1]) if name != "pp" else 0
            if name.startswith("ada"):
                return ins["w_ada_2"][0, :, half * W:half * W + W].rearrange("(k p) n -> p k n", p=P), (KD, W)
            if name.startswith("ple"):
                return ins["ple_gate_w"][0, :, half * W:half * W + W].rearrange("(k p) n -> p k n", p=P), (KD, W)
            if name == "pp":
                return ins["ple_proj_w"][0].rearrange("(k p) n -> p k n", p=P), (TT, D)
            return ins["w_out"][0, :, half * W:half * W + W].rearrange("(k p) n -> p k n", p=P), (KD, W)

        def weights(name):
            return room(ring(unit_no(name)), *unit_source(name)[1])

        def unit2_source(name):
            if name.startswith("Wb2"):
                src = ins["w_attn_br_2" if name[-1] == "a" else "w_pool_br_2"][0]
                return src.rearrange("(k p) n -> p k n", p=P), (KW, D)
            if name.startswith("out2"):
                half = int(name[-1])
                return ins["w_out_2"][0, :, half * W:half * W + W].rearrange("(k p) n -> p k n", p=P), (KD, W)
            return ins["w_in_2"][0, :, COL2[name]:COL2[name] + W].rearrange("(k p) n -> p k n", p=P), (KD, W)

        def weights2(name):
            return room(ring(unit2_no(name)), *unit2_source(name)[1])

        def unit2_used(name):
            if name.startswith("Wb2"):
                return sig("small_full"), small_no(f"{name} 3") + 1
            if name.startswith("out2"):
                return sig("small_full"), small_no(f"mix2 {2 * int(name[-1]) + 1}") + 1
            if name.startswith("g2"):
                return sig("proj_full"), proj_no(f"{name[:-1]}{2 * int(name[-1]) + 1}") + 1
            return sig("proj_full"), proj_no(f"{name} 1") + 1

        def expert_unit(e, u):
            if u < 4:
                src = ins["expert_w_gu"][0, bass.ds(e, 1), u * 2 * P:(u + 1) * 2 * P, :]
                return src.rearrange("e (k p) n -> p (e k) n", p=P), (2, GU)
            src = ins["expert_w_down"][0, bass.ds(e, 1), (u - 4) * 4 * P:(u - 3) * 4 * P, :]
            return src.rearrange("e (k p) n -> p (e k) n", p=P), (4, D)

        def expert_room(u):
            return room(RING + slots[u] * UNIT, *expert_unit(0, u)[1])

        named = dict(XT=XT, x1=x1, MERGED=MERGED, YA=YT["A"], YB=YT["B"], YC=YT["C"], YD=YT["D"])

        def unit_used(name):
            if name.startswith("Wb"):
                return sig("small_full"), small_no(f"{name} 3") + 1
            if name.startswith("out"):
                return sig("small_full"), small_no(f"mix {2 * int(name[-1]) + 1}") + 1
            if name.startswith("ada"):
                return sig("small_full"), small_no(name) + 1
            if name.startswith("ple"):
                return sig("small_full"), small_no(f"ple {2 * int(name[-1]) + 1}") + 1
            if name == "pp":
                return sig("small_full"), small_no("pp 3") + 1
            if name in ("C if", "A x"):
                return sig("proj_full"), proj_no(name) + 1
            if name.startswith("G"):
                return sig("proj_full"), proj_no(f"{name[:-1]}{2 * int(name[-1]) + 1}") + 1
            return sig("proj_full"), proj_no(f"{name} 1") + 1

        block = stack.enter_context(nc.Block())

        @block.sync
        def _(sp):
            sp.dma_start(XTOK, ins["x"][0].rearrange("(j p) d -> p j d", p=P)).then_inc(sig("x_loaded"), 16)
            for n, name in enumerate(UNITS):
                if n >= 3:
                    sp.wait_ge(*unit_used(UNITS[n - 3]))
                src, _ = unit_source(name)
                sp.dma_start(weights(name), src).then_inc(sig(f"unit_in_{n % 3}"), 16)
            sp.wait_ge(sig("x1_done"), 2)
            sp.wait_ge(*unit_used("pp"))
            for u in range(6):
                sp.dma_start(expert_room(u), expert_unit(0, u)[0]).then_inc(sig(f"expert_in_{u}"), 16)
            sp.wait_ge(sig("total_ready"), 1)
            n_steps = sp.value_load(total[0:1, 0:1], min_val=EXPERTS, max_val=EXPERTS * T // CAP)
            with sp.Fori(1, n_steps) as i:
                for u in range(6):
                    if u < 4:
                        sp.wait_ge(sig("gu_used"), 4 * i + (u - 3))
                    elif u == 4:
                        sp.wait_ge(sig("down_used"), i)
                    else:
                        sp.wait_ge(sig("y_full"), i)
                    sp.dma_start(expert_room(u), expert_unit(i % EXPERTS, u)[0]).then_inc(sig(f"expert_in_{u}"), 16)
            sp.wait_ge(sig("experts_done"), 1)
            for n, name in enumerate(UNITS2):
                if n >= 3:
                    sp.wait_ge(*unit2_used(UNITS2[n - 3]))
                if n == 3:
                    sp.wait_ge(sig("table_stored"), 16)
                    tab = bass.AP(tensor=scratch.tensor, offset=0, ap=[[1, P], [BKT, 24], [1, T]])
                    sp.dma_start(HK, tab).then_inc(sig("hankel_loaded"), 16)
                sp.dma_start(weights2(name), unit2_source(name)[0]).then_inc(sig(f"unit2_in_{n % 3}"), 16)
            for j in range(TT):
                sp.wait_ge(sig("final"), j + 1)
                sp.dma_start(outs[0][0, j * P:(j + 1) * P, :], x3[:, j, :]).then_inc(sig("stored"), 16)
            sp.wait_ge(sig("stored"), 16 * TT)

        @block.gpsimd
        def _(pool):
            pool.dma_start(CO, consts["consts"]).then_inc(sig("const_loaded"), 16)
            n = 0
            for name, (row, cnt) in VEC.items():
                src = ins[name]
                src = src.flatten().rearrange("(a b) -> a b", b=P)
                pool.dma_start(PROW[row:row + cnt, :], src).then_inc(sig("prow_loaded"), 16)
                n += 1
            assert n == len(VEC)
            pool.dma_start(ifb[0:4, 0:1], ins["mlstm_i_bias"].rearrange("a b -> b a")).then_inc(sig("ifb_loaded"), 16)
            pool.dma_start(ifb[0:4, 1:2], ins["mlstm_f_bias"].rearrange("a b -> b a")).then_inc(sig("ifb_loaded"), 16)
            pool.memset(WX, 0.0).then_inc(sig("wx_zero"), 1)
            pool.memset(WAD, 0.0).then_inc(sig("wx_zero"), 1)
            pool.wait_ge(sig("wx_zero"), 2)
            for t_, name in ((WX, "lru_wx"), (WAD, "lru_wa")):
                for odd in range(2):
                    pool.dma_start(t_[64 * odd:64 * odd + 64, :, 64 * odd:64 * odd + 64],
                                   ins[name][0, odd::2].rearrange("g i j -> i g j")).then_inc(sig("wx_loaded"), 16)
            pool.dma_start(WA2[0:64, :], ins["rwkv_w2"][0]).then_inc(sig("w2_loaded"), 16)
            pool.dma_start(WA2[64:128, :], ins["rwkv_a2"][0]).then_inc(sig("w2_loaded"), 16)
            pool.dma_start(G2, ins["rwkv_g2"][0]).then_inc(sig("w2_loaded"), 16)
            for l in range(6):
                if l == 0:
                    pool.wait_ge(sig("small_out"), small_no("A NT 3") + 1)
                elif l == 1:
                    pool.wait_ge(sig("small_out"), small_no("A X0 3") + 1)
                else:
                    pool.wait_ge(sig("small_full"), small_no(f"A X{l - 1} 3") + 1)
                pool.tensor_tensor(NTm, NT, along(c("level", l * P, l * P + P), 16), ALU.mult).then_inc(sig("NTm_ready"), 1)
            pool.wait_ge(sig("A_states_done"), 1)
            pool.wait_ge(sig("small_full"), small_no("A Y 3") + 1)
            pool.dma_start(bcg, ins["ln1_g"][0].partition_broadcast(P)).then_inc(sig("ln1_loaded"), 16)
            pool.dma_start(bcb, ins["ln1_b"][0].partition_broadcast(P)).then_inc(sig("ln1_loaded"), 16)
            pool.wait_ge(sig("merged"), 4)
            for n, (lo, src) in enumerate(((0, ins["c_2"][0]), (8, ins["norm_g_2"][0]), (16, ins["b_ada_2"][0]))):
                cnt = 24 if n == 2 else 8
                pool.dma_start(PROW2[lo:lo + cnt, :], src.rearrange("(a b) -> a b", b=P)).then_inc(sig("prow2_loaded"), 16)
            for dst, src in ((RELB, ins["rel_bias_2"]), (HOT, consts["hot"]), (BM, consts["mask"])):
                pool.dma_start(dst, src).then_inc(sig("table_loaded"), 16)
            pool.memset(BGU, 0.0).then_inc(sig("bgu_zero"), 1)
            pool.wait_ge(sig("bgu_zero"), 1)
            for dst, src in ((RW, ins["router_w"][0].rearrange("(k p) e -> p k e", p=P)),
                             (RB, ins["router_b"][0].partition_broadcast(P)),
                             (BD, ins["expert_b_down"][0]), (BGU[0:EXPERTS], ins["expert_b_gu"][0]),
                             (PTOK, ins["p"][0, 0].rearrange("(j p) d -> p j d", p=P))):
                pool.dma_start(dst, src).then_inc(sig("router_loaded"), 16)
            pool.wait_ge(sig("table_done"), 1)
            pool.dma_start(scratch, TAB).then_inc(sig("table_stored"), 16)
            pool.wait_ge(sig("base_done"), 1)
            pool.dma_start(ln2g, ins["ln2_g"][0].partition_broadcast(P)).then_inc(sig("ln2_loaded"), 16)
            pool.dma_start(ln2b, ins["ln2_b"][0].partition_broadcast(P)).then_inc(sig("ln2_loaded"), 16)
            pool.wait_ge(sig("small_full"), small_no("O 7") + 1)
            pool.dma_start(POOLW, ins["pool_w_2"][0].rearrange("g c e -> c g e")).then_inc(sig("poolw_loaded"), 16)
            pool.dma_start(fing, ins["final_g_2"].partition_broadcast(P)).then_inc(sig("fing_loaded"), 16)

        @block.tensor
        def _(pe):
            def unit(name):
                n = unit_no(name)
                pe.wait_ge(sig(f"unit_in_{n % 3}"), 16 * (n // 3 + 1))
                return weights(name)

            def proj(name):
                n = proj_no(name)
                if n >= 4:
                    pe.wait_ge(sig("proj_out"), n - 3)
                return proj_bank[n % 4]

            def small(name):
                n = small_no(name)
                if n >= 4:
                    pe.wait_ge(sig("small_out"), n - 3)
                return small_bank[n % 4]

            def ones_channels(what, banks=2, last=True):
                w = unit(what)
                for b in range(banks):
                    name = f"{what} {b}" if not what.startswith("G") else f"{what[:-1]}{int(what[-1]) * 2 + b}"
                    if what == "A x":
                        name = what
                    ps = proj(name)
                    for m in range(2):
                        for k in range(KD):
                            mm = pe.matmul(ps[:, m * T:m * T + T], w[:, k, (2 * b + m) * P:(2 * b + m + 1) * P],
                                           XT[:, k, :], start=k == 0, stop=k == KD - 1)
                    mm.then_inc(sig("proj_full"), 1)

            def ones_tokens(what):
                w = unit(what)
                for j in range(TT):
                    ps = proj(f"{what} {j}")
                    for k in range(KD):
                        mm = pe.matmul(ps[:, :], XT[:, k, j * P:j * P + P], w[:, k, :], start=k == 0, stop=k == KD - 1)
                    mm.then_inc(sig("proj_full"), 1)

            def merge(b):
                pe.wait_ge(sig(f"{b}_done"), 1)
                w = unit(f"Wb {b}")
                for i in range(4):
                    ps = small(f"Wb {b} {i}")
                    for m in range(2):
                        for k in range(KW):
                            mm = pe.matmul(ps[:, m * T:m * T + T], w[:, k, (2 * i + m) * P:(2 * i + m + 1) * P],
                                           YT[b][:, k, :], start=k == 0, stop=k == KW - 1)
                    mm.then_inc(sig("small_full"), 1)

            pe.wait_ge(sig("const_loaded"), 16)
            pe.wait_ge(sig("prow_loaded"), 16 * len(VEC))
            pe.transpose(small("vectors")[:, 0:NVEC], PROW[0:NVEC, :], ident[0:NVEC, 0:NVEC]).then_inc(sig("small_full"), 1)
            pe.wait_ge(sig("x_loaded"), 16)
            for g in range(4):
                ps = small(f"x {g}")
                for k in range(2):
                    for j in range(TT):
                        mm = pe.transpose(ps[:, k * T + j * P:k * T + j * P + P], XTOK[:, j, (2 * g + k) * P:(2 * g + k + 1) * P], ident)
                mm.then_inc(sig("small_full"), 1)
            pe.wait_ge(sig("small_out"), small_no("x 3") + 1)

            ones_channels("D xr")
            ones_channels("D gate")
            ones_channels("C q")
            ones_channels("C k")
            ones_tokens("C v")
            ones_channels("C o")
            w = unit("C if")
            ps = proj("C if")
            for m in range(2):
                for k in range(KD):
                    mm = pe.matmul(ps[0:4, m * T:m * T + T], w[:, k, 4 * m:4 * m + 4], XT[:, k, :], start=k == 0, stop=k == KD - 1)
            mm.then_inc(sig("proj_full"), 1)

            pe.wait_ge(sig("wx_loaded"), 64)
            pe.wait_ge(sig("D_conv"), 1)
            for nm, wt in (("gx", WX), ("ga", WAD)):
                for i in range(2):
                    ps = small(f"D {nm} {i}")
                    for m in range(2):
                        mm = pe.matmul(ps[:, m * T:m * T + T], wt[:, 2 * i + m, :], xc[:, 2 * i + m, :], start=True, stop=True)
                    mm.then_inc(sig("small_full"), 1)
            ones_channels("B q")
            ones_channels("B f")
            ones_tokens("B i")
            ones_channels("B g")

            pe.wait_ge(sig("C_rows"), 1)
            for i in range(2):
                ps = small(f"C row {i}")
                for m in range(2):
                    mm = pe.matmul(ps[:, m * T:m * T + T], c("headrow", (2 * i + m) * P, (2 * i + m + 1) * P)[0:4, :], gC, start=True, stop=True)
                mm.then_inc(sig("small_full"), 1)
            ps = small("C col")
            for n, r in enumerate((uC, mC)):
                for j in range(TT):
                    mm = pe.transpose(ps[:, 8 * n + 4 * j:8 * n + 4 * j + 4], r[:, j * P:j * P + P], ident[0:4, 0:4])
            mm.then_inc(sig("small_full"), 1)
            pe.wait_ge(sig("C_qk"), 1)
            for h in range(4):
                ps = small(f"C S {h}")
                pe.matmul(ps[:, 0:T], qk[:, 4 + h, 0:P], qk[:, h, :], start=True, stop=True)
                pe.matmul(ps[:, T:T + P], qk[:, 4 + h, P:T], qk[:, h, P:T], start=True, stop=True).then_inc(sig("small_full"), 1)
            ones_channels("G D 0")
            ones_channels("G D 1")
            pe.wait_ge(sig("C_weights"), 1)
            pe.wait_ge(sig("proj_out"), proj_no("C v 1") + 1)
            for j in range(TT):
                ps = small(f"C num {j}")
                for h in range(4):
                    if j == 0:
                        mm = pe.matmul(ps[:, h * P:h * P + P], sC[:, h, 0:P], vC[:, 0, h * P:h * P + P], start=True, stop=True)
                    else:
                        pe.matmul(ps[:, h * P:h * P + P], sC[:, h, P:T], vC[:, 0, h * P:h * P + P], start=True, stop=False)
                        mm = pe.matmul(ps[:, h * P:h * P + P], sC[:, h, T:T + P], vC[:, 1, h * P:h * P + P], start=False, stop=True)
                mm.then_inc(sig("small_full"), 1)
            ps = small("C den")
            for h in range(4):
                pe.matmul(ps[:, h:h + 1], sC[:, h, 0:P], c("ones", 0, 1), start=True, stop=True)
                pe.matmul(ps[:, 4 + h:5 + h], sC[:, h, P:T], c("ones", 0, 1), start=True, stop=False)
                mm = pe.matmul(ps[:, 4 + h:5 + h], sC[:, h, T:T + P], c("ones", 0, 1), start=False, stop=True)
            mm.then_inc(sig("small_full"), 1)

            def turned(b, src, done):
                pe.wait_ge(sig(done), 1)
                for i in range(2):
                    ps = small(f"{b} {i}")
                    for m in range(2):
                        for j in range(TT):
                            mm = pe.transpose(ps[:, m * T + j * P:m * T + j * P + P], src[:, j, (2 * i + m) * P:(2 * i + m + 1) * P], ident)
                    mm.then_inc(sig("small_full"), 1)

            turned("C yT", hC.rearrange("p (j h) e -> p j (h e)", j=TT), "C_normed")
            merge("D")

            pe.wait_ge(sig("B_qk"), 1)
            for j in range(TT):
                ps = small(f"B diag {j}")
                for h in range(4):
                    mm = pe.matmul(ps[:, h * P:h * P + P], kB[:, h, j * P:j * P + P], qB[:, h, j * P:j * P + P], start=True, stop=True)
                mm.then_inc(sig("small_full"), 1)
            fill = {0: "A r", 2: "A k", 4: "A v", 6: "A x"}
            for l in range(8):
                pe.wait_ge(sig("B_level"), l + 1)
                if l < 7:
                    for j in range(TT):
                        ps = small(f"B level {l} {j}")
                        for h in range(4):
                            e = eB[:, h, j * P:j * P + P]
                            mm = pe.matmul(ps[:, h * P:h * P + P], e, e, start=True, stop=True)
                        mm.then_inc(sig("small_full"), 1)
                else:
                    ps = small("B cross")
                    for h in range(4):
                        mm = pe.matmul(ps[:, h * P:h * P + P], eB[:, h, 0:P], eB[:, h, P:T], start=True, stop=True)
                    mm.then_inc(sig("small_full"), 1)
                if l in fill:
                    ones_channels(fill[l], 2 if fill[l] != "A x" else 1)
            pe.wait_ge(sig("proj_out"), proj_no("B i 1") + 1)
            pe.wait_ge(sig("small_out"), small_no("B cross") + 1)
            for j in range(TT):
                ps = small(f"B o {j}")
                for h in range(4):
                    mm = pe.matmul(ps[:, h * P:h * P + P], aB[:, 4 * j + h, :], vB[:, j, h * P:h * P + P], start=True, stop=j == 0)
                    if j == 1:
                        mm = pe.matmul(ps[:, h * P:h * P + P], aX[:, h, :], vB[:, 0, h * P:h * P + P], start=False, stop=True)
                mm.then_inc(sig("small_full"), 1)
            ones_channels("G C 0")
            ones_channels("G C 1")
            turned("B yT", tB2.rearrange("p a b -> p (a b)").rearrange("p (j n) -> p j n", j=TT), "B_normed")

            pe.wait_ge(sig("w2_loaded"), 48)
            pe.wait_ge(sig("A_tanh"), 1)
            for nm, lo, hi, wt in (("w", 0, 64, WA2), ("a", 64, 128, WA2), ("g", 0, 128, G2)):
                for i in range(2):
                    ps = small(f"A {nm} {i}")
                    for m in range(2):
                        rhs = zmix[lo:hi, 13 if nm == "g" else 12, :]
                        mm = pe.matmul(ps[:, m * T:m * T + T], wt[lo:hi, (2 * i + m) * P:(2 * i + m + 1) * P], rhs, start=True, stop=True)
                    mm.then_inc(sig("small_full"), 1)
            pe.wait_ge(sig("A_kksq"), 1)
            for i in range(2):
                ps = small(f"A kk {i}")
                pe.matmul(ps[:, :], c("headsum"), bA[:, 2 * i:2 * i + 2, :], start=True, stop=True).then_inc(sig("small_full"), 1)

            def to_tokens(name, src):
                for i in range(2):
                    ps = small(f"A {name} {i}")
                    for m in range(4):
                        mm = pe.transpose(ps[:, m * P:m * P + P], src[:, m, i * P:i * P + P], ident)
                    mm.then_inc(sig("small_full"), 1)

            pe.wait_ge(sig("A_mixed"), 1)
            to_tokens("V", vA)
            pe.wait_ge(sig("A_rk"), 1)
            for i in range(2):
                ps = small(f"A bonus {i}")
                pe.matmul(ps[:, :], c("headsum"), bonusA[:, 2 * i:2 * i + 2, :], start=True, stop=True).then_inc(sig("small_full"), 1)
            pe.wait_ge(sig("A_tilde"), 1)
            to_tokens("At", kkA)
            to_tokens("Bt", bA)
            to_tokens("Kt", kA)

            def head(v, h, lo, hi):
                return v[64 * (h % 2):64 * (h % 2) + 64, h // 2, lo:hi]

            def pairs(name, lhs, rhs):
                for i in range(4):
                    ps = small(f"A {name} {i}")
                    for m in range(4):
                        j, h = i // 2, 2 * m + i % 2
                        mm = pe.matmul(ps[:, m * P:m * P + P], head(lhs, h, j * P, j * P + P), head(rhs, h, j * P, j * P + P), start=True, stop=True)
                    mm.then_inc(sig("small_full"), 1)

            def products(name, lhs, rhs):
                for i in range(4):
                    ps = small(f"A {name} {i}")
                    for m in range(4):
                        n = 4 * i + m
                        mm = pe.matmul(ps[:, m * P:m * P + P], lhs[:, n, :], rhs[:, n, :], start=True, stop=True)
                    mm.then_inc(sig("small_full"), 1)

            pairs("NT", bA, kkA)
            pe.wait_ge(sig("NTm_ready"), 1)
            for i in range(4):
                ps = small(f"A X0 {i}")
                for m in range(4):
                    mm = pe.transpose(ps[:, m * P:m * P + P], NTm[:, 4 * i + m, :], ident)
                mm.then_inc(sig("small_full"), 1)
            merge("C")
            fill = {1: "G B 0", 2: "G B 1", 3: "Wb B", 4: "G A 0"}
            for l in range(1, 6):
                pe.wait_ge(sig("NTm_ready"), l + 1)
                pe.wait_ge(sig("small_out"), (small_no("A X0 3") if l == 1 else small_no(f"A DT{l - 1} 3")) + 1)
                products(f"X{l}", NTm, Da)
                if l in (1, 2):
                    ones_channels(fill[l])
                pe.wait_ge(sig("small_out"), small_no(f"A X{l} 3") + 1)
                if l < 5:
                    products(f"D{l}", DTa, X)
                products(f"DT{l}", X, DTa)
            merge("B")
            pairs("AkT", kA, kkA)
            ones_channels("G A 0")
            ones_channels("G A 1")
            pe.wait_ge(sig("small_out"), small_no("A AkT 3") + 1)
            for j in range(TT):
                ps = small(f"A GT {j}")
                for h in range(8):
                    mm = pe.matmul(ps[64 * (h % 2):64 * (h % 2) + 64, (h // 2) * P:(h // 2 + 1) * P], At[:, j, h * CH:h * CH + CH], DTa[:, mat(j, h), :], start=True, stop=True)
                mm.then_inc(sig("small_full"), 1)
            for j in range(TT):
                ps = small(f"A W {j}")
                for h in range(8):
                    mm = pe.matmul(ps[:, h * CH:h * CH + CH], AkT[:, mat(j, h), :], Vt[:, j, h * CH:h * CH + CH], start=True, stop=True)
                mm.then_inc(sig("small_full"), 1)
            pe.wait_ge(sig("small_out"), small_no("A W 1") + 1)
            for j in range(TT):
                ps = small(f"A U0 {j}")
                for h in range(8):
                    mm = pe.matmul(ps[:, h * CH:h * CH + CH], DTa[:, mat(j, h), :], WU[:, j, h * CH:h * CH + CH], start=True, stop=True)
                mm.then_inc(sig("small_full"), 1)
            for ch in range(4):
                j, po = ch // 2, 64 * (ch % 2)
                if ch > 0:
                    pe.wait_ge(sig("A_state"), ch)
                    for h in (0, 2, 4, 6, 1, 3, 5, 7):
                        ho = 64 * (h % 2)
                        if h < 2:
                            ps = small(f"A U {ch} {h}")
                        mm = pe.matmul(ps[po:po + 64, (h // 2) * CH:(h // 2 + 1) * CH], GT[ho:ho + 64, h // 2, ch * CH:ch * CH + CH],
                                       S_all[ho:ho + 64, ch, (h // 2) * CH:(h // 2 + 1) * CH], start=True, stop=True)
                        if h > 5:
                            mm.then_inc(sig("small_full"), 1)
                if ch < 3:
                    pe.wait_ge(sig("A_u"), ch + 1)
                    ps = small(f"A S {ch}")
                    for h in range(8):
                        ho = 64 * (h % 2)
                        o = ps[ho:ho + 64, (h // 2) * CH:(h // 2 + 1) * CH]
                        pe.matmul(o, Bt[po:po + 64, j, h * CH:h * CH + CH], Ut[po:po + 64, j, h * CH:h * CH + CH], start=True, stop=False)
                        mm = pe.matmul(o, Kt[po:po + 64, j, h * CH:h * CH + CH], Vt[po:po + 64, j, h * CH:h * CH + CH], start=False, stop=True)
                    mm.then_inc(sig("small_full"), 1)
            pe.wait_ge(sig("A_u"), 4)
            pairs("RbT", bA, rA)
            pairs("RkT", kA, rA)
            pe.wait_ge(sig("small_out"), small_no("A RkT 3") + 1)
            for i in range(4):
                j, odd = divmod(i, 2)
                ps = small(f"A Y {i}")
                for pair in range(4):
                    h = 2 * pair + odd
                    o = ps[:, pair * CH:pair * CH + CH]
                    pe.matmul(o, RbT[:, mat(j, h), :], Ut[:, j, h * CH:h * CH + CH], start=True, stop=False, skip_group_check=True)
                    mm = pe.matmul(o, RkT[:, mat(j, h), :], Vt[:, j, h * CH:h * CH + CH], start=False, stop=True, skip_group_check=True)
                    for cp in range(2):
                        ch = 2 * j + cp
                        if ch > 0:
                            mm = pe.matmul(ps[64 * cp:64 * cp + 64, pair * CH:pair * CH + CH], head(rA, h, ch * CH, ch * CH + CH),
                                           S_all[64 * odd:64 * odd + 64, ch, pair * CH:pair * CH + CH], start=False, stop=True,
                                           skip_group_check=True)
                mm.then_inc(sig("small_full"), 1)
            turned("A yT", Ysum.rearrange("p (j h) e -> p j (h e)", j=TT), "A_normed")
            merge("A")
            pe.wait_ge(sig("merged"), 4)
            for half in range(2):
                w = unit(f"out {half}")
                for j in range(TT):
                    ps = small(f"mix {2 * half + j}")
                    for k in range(KD):
                        mm = pe.matmul(ps[:, :], MERGED[:, k, j * P:j * P + P], w[:, k, :], start=k == 0, stop=k == KD - 1)
                    mm.then_inc(sig("small_full"), 1)

            pe.wait_ge(sig("prow2_loaded"), 48)
            pe.transpose(small("vectors2")[:, 0:40], PROW2[0:40, :], ident[0:40, 0:40]).then_inc(sig("small_full"), 1)
            pe.wait_ge(sig("small_out"), small_no("vectors2") + 1)
            for i in range(6):
                w = unit(f"ada {i}")
                ps = small(f"ada {i}")
                for m in range(4):
                    for k in range(KD):
                        mm = pe.matmul(ps[:, m:m + 1], w[:, k, m * P:m * P + P], PV2[:, k:k + 1], start=k == 0, stop=k == KD - 1)
                mm.then_inc(sig("small_full"), 1)
            pe.wait_ge(sig("small_out"), small_no("ada 5") + 1)
            pe.transpose(small("gate8")[0:8, 0:P], MODT[:, 16:24], ident).then_inc(sig("small_full"), 1)
            pe.wait_ge(sig("small_out"), small_no("gate8") + 1)
            for i in range(2):
                ps = small(f"gateB {i}")
                for m in range(4):
                    k = 4 * i + m
                    mm = pe.matmul(ps[:, m * P:m * P + P], c("headrow", k * P, k * P + P)[0:8, :], G8, start=True, stop=True)
                mm.then_inc(sig("small_full"), 1)
            pe.wait_ge(sig("table_loaded"), 48)
            pe.matmul(small("bias")[0:24, 0:BKT], RELB, HOT, start=True, stop=True).then_inc(sig("small_full"), 1)
            pe.wait_ge(sig("x1_done"), 2)
            for g in range(4):
                ps = small(f"x1 {g}")
                for k in range(2):
                    for j in range(TT):
                        mm = pe.transpose(ps[:, k * T + j * P:k * T + j * P + P], x1[:, j, (2 * g + k) * P:(2 * g + k + 1) * P], ident)
                mm.then_inc(sig("small_full"), 1)
            pe.wait_ge(sig("router_loaded"), 80)
            pe.wait_ge(sig("small_out"), small_no("x1 3") + 1)
            ps = small("logits")
            for j in range(TT):
                for k in range(KD):
                    mm = pe.matmul(ps[:, j * EXPERTS:(j + 1) * EXPERTS], XT[:, k, j * P:j * P + P], RW[:, k, :], start=k == 0, stop=k == KD - 1)
            mm.then_inc(sig("small_full"), 1)
            pe.wait_ge(sig("gates_ready"), 1)
            ps = small("gateT")
            for j in range(TT):
                mm = pe.transpose(ps[0:EXPERTS, j * P:j * P + P], gates_[:, j, :], ident)
            mm.then_inc(sig("small_full"), 1)
            ps = small("rank")
            pe.matmul(ps[:, 0:32], c("strict"), sel[:, 0, :], start=True, stop=True)
            pe.matmul(ps[:, 32:64], c("ones", 0, P), sel[:, 0, :], start=True, stop=False)
            pe.matmul(ps[:, 32:64], c("strict"), sel[:, 1, :], start=False, stop=True)
            pe.matmul(ps[:, 64:96], c("ones", 0, P), sel[:, 0, :], start=True, stop=False)
            pe.matmul(ps[:, 64:96], c("ones", 0, P), sel[:, 1, :], start=False, stop=True).then_inc(sig("small_full"), 1)
            ps = small("pT")
            for k in range(2):
                for j in range(TT):
                    mm = pe.transpose(ps[:, k * T + j * P:k * T + j * P + P], PTOK[:, j, k * P:k * P + P], ident)
            mm.then_inc(sig("small_full"), 1)
            for half in range(2):
                w = unit(f"ple {half}")
                for j in range(TT):
                    ps = small(f"ple {2 * half + j}")
                    for k in range(KD):
                        mm = pe.matmul(ps[:, :], XT[:, k, j * P:j * P + P], w[:, k, :], start=k == 0, stop=k == KD - 1)
                    mm.then_inc(sig("small_full"), 1)
            w = unit("pp")
            for i in range(4):
                half, j = divmod(i, 2)
                ps = small(f"pp {i}")
                for k in range(2):
                    mm = pe.matmul(ps[:, :], PTT[:, k, j * P:j * P + P], w[:, k, half * W:half * W + W], start=k == 0, stop=k == 1)
                mm.then_inc(sig("small_full"), 1)

            pe.wait_ge(sig("proj_out"), proj_no("G A 3") + 1)
            pe.wait_ge(sig("small_out"), small_no("pp 3") + 1)
            for j in range(TT):
                for half in range(2):
                    pe.matmul(acc_bank[2 * j + half][:, :], GTT[:, j * P:j * P + P], BD[:, half * W:half * W + W], start=True, stop=False, skip_group_check=True)

            def gather():
                for k in range(KD):
                    for j in range(TT):
                        mm = pe.matmul(x_bank[:, k * CAP:(k + 1) * CAP], x1[:, j, k * P:k * P + P], PICK[:, j, :], start=j == 0, stop=j == 1)
                mm.then_inc(sig("gathered"), 1)

            def scatter():
                for j in range(TT):
                    for half in range(2):
                        lo = CAP * half
                        mm = pe.matmul(acc_bank[2 * j + half][:, :], PTW[lo:lo + CAP, j * P:j * P + P], YSB[lo:lo + CAP, :],
                                       start=False, stop=False, skip_group_check=True)
                return mm

            pe.wait_ge(sig("pick_ready"), 1)
            gather()
            pe.nop().then_inc(sig("ptw_full"), 1)
            pe.wait_ge(sig("total_ready"), 1)
            n_steps = pe.value_load(total[0:1, 0:1], min_val=EXPERTS, max_val=EXPERTS * T // CAP)
            with pe.Fori(0, n_steps) as i:
                pe.wait_ge(sig("xg_ready"), i + 1)
                for k in range(KD):
                    if k % 2 == 0:
                        pe.wait_ge(sig(f"expert_in_{k // 2}"), 16 * i + 16)
                        w = expert_room(k // 2)
                    for n, bank in enumerate((gate_bank, up_bank)):
                        for half in range(2):
                            mm = pe.matmul(bank[CAP * half:CAP * half + CAP, :], XG[:, k, :], w[:, k % 2, n * D + half * W:n * D + half * W + W],
                                           start=k == 0, stop=False, skip_group_check=True)
                    if k % 2:
                        mm.then_inc(sig("gu_used"), 1)
                pe.wait_ge(sig("esel_ready"), i + 1)
                for n, bank in enumerate((gate_bank, up_bank)):
                    for half in range(2):
                        mm = pe.matmul(bank[CAP * half:CAP * half + CAP, :], ESEL, BGU[:, n * D + half * W:n * D + half * W + W],
                                       start=False, stop=True, skip_group_check=True)
                mm.then_inc(sig("gu_full"), 1)
                pe.wait_ge(sig("y_ready"), i + 1)
                pe.wait_ge(sig("ptw_ready"), i + 1)
                scatter()
                pe.wait_ge(sig("pickw_ready"), i + 1)
                for j in range(TT):
                    mm = pe.transpose(y_bank[:, j * P:j * P + P], PICKW[:, j, :], ident)
                mm.then_inc(sig("ptw_full"), 1)
                pe.wait_ge(sig("pick_ready"), i + 2)
                gather()
                pe.wait_ge(sig("h_ready"), i + 1)
                for m in range(4):
                    mm = pe.transpose(gate_bank[:, m * P:m * P + P], GH[:, m * P:m * P + P], ident)
                mm.then_inc(sig("ht_full"), 1)
                pe.wait_ge(sig("ptw_ready"), i + 2)
                pe.wait_ge(sig("hm_ready"), i + 1)
                for u in range(2):
                    pe.wait_ge(sig(f"expert_in_{4 + u}"), 16 * i + 16)
                    w = expert_room(4 + u)
                    for m in range(4):
                        for half in range(2):
                            mm = pe.matmul(y_bank[CAP * half:CAP * half + CAP, :], HM[:, m, u, :], w[:, m, half * W:half * W + W],
                                           start=u == 0 and m == 0, stop=u == 1 and m == 3, skip_group_check=True)
                    if u == 0:
                        mm.then_inc(sig("down_used"), 1)
                mm.then_inc(sig("y_full"), 1)
            pe.wait_ge(sig("last_y_ready"), 1)
            scatter().then_inc(sig("experts_done"), 1)

            def unit2(name):
                n = unit2_no(name)
                pe.wait_ge(sig(f"unit2_in_{n % 3}"), 16 * (n // 3 + 1))
                return weights2(name)

            def channels2(what):
                w = unit2(what)
                for b in range(2):
                    name = f"{what} {b}" if what[:2] != "g2" else f"{what[:-1]}{int(what[-1]) * 2 + b}"
                    ps = proj(name)
                    for m in range(2):
                        for k in range(KD):
                            mm = pe.matmul(ps[:, m * T:m * T + T], w[:, k, (2 * b + m) * P:(2 * b + m + 1) * P], HT[:, k, :],
                                           start=k == 0, stop=k == KD - 1)
                    mm.then_inc(sig("proj_full"), 1)

            def tokens2(what):
                w = unit2(what)
                for j in range(TT):
                    ps = proj(f"{what} {j}")
                    for k in range(KD):
                        mm = pe.matmul(ps[:, :], HT[:, k, j * P:j * P + P], w[:, k, :], start=k == 0, stop=k == KD - 1)
                    mm.then_inc(sig("proj_full"), 1)

            def merge2(what, y):
                w = unit2(what)
                for i in range(4):
                    ps = small(f"{what} {i}")
                    for m in range(2):
                        for k in range(KW):
                            mm = pe.matmul(ps[:, m * T:m * T + T], w[:, k, (2 * i + m) * P:(2 * i + m + 1) * P], y[:, k, :],
                                           start=k == 0, stop=k == KW - 1)
                    mm.then_inc(sig("small_full"), 1)

            pe.wait_ge(sig("acc_read"), 1)
            pe.wait_ge(sig("x2n_done"), 2)
            for g in range(4):
                ps = small(f"h {g}")
                for k in range(2):
                    for j in range(TT):
                        mm = pe.transpose(ps[:, k * T + j * P:k * T + j * P + P], base[:, j, (2 * g + k) * P:(2 * g + k + 1) * P], ident)
                mm.then_inc(sig("small_full"), 1)
            pe.wait_ge(sig("small_out"), small_no("h 3") + 1)
            for n in QKV:
                (tokens2 if n[0] == "V" else channels2)(n)

            def scores(h):
                ho = 64 * (h % 2)
                for b, parts in enumerate((((0, 1, 0), (1, 1, 256)), ((2, 1, 0),), ((0, 0, 0), (1, 0, 128), (2, 0, 256)))):
                    ps = proj(f"L {h} {b}")
                    for g, j, at_ in parts:
                        n = T if j else P
                        pe.matmul(ps[:, at_:at_ + n], c("flip"), HK[:, g * HEADS + h, T - n:T], start=True, stop=False)
                        mm = pe.matmul(ps[:, at_:at_ + n], qT[g][ho:ho + 64, h // 2, j * P:j * P + P], kT[g][ho:ho + 64, h // 2, 0:n],
                                       start=False, stop=True)
                    mm.then_inc(sig("proj_full"), 1)

            pe.wait_ge(sig("hankel_loaded"), 16)
            pe.wait_ge(sig("proj_out"), proj_no("V2 1") + 1)
            scores(0)
            for h in range(HEADS):
                if h < HEADS - 1:
                    scores(h + 1)
                if h == 0:
                    tokens2("Z")
                if h == 1:
                    channels2("U")
                if h == 2:
                    channels2("ZP")
                pe.wait_ge(sig("proj_out"), proj_no(f"L {h} 2") + 1)
                for b in range(3):
                    ps = small(f"T {h} {b}")
                    for m in range(4 if b < 2 else 1):
                        mm = pe.transpose(ps[:, m * P:m * P + P], PB[h % 2][:, (4 * b + m) * P:(4 * b + m + 1) * P], ident)
                    mm.then_inc(sig("small_full"), 1)
                ps = small(f"O {h}")
                pe.wait_ge(sig("small_out"), small_no(f"T {h} 2") + 1)
                for n in range(6):
                    pe.matmul(ps[:, CH:2 * CH], PTr[:, n * P:n * P + P], vK[n // 2][:, n % 2, h * CH:h * CH + CH], start=n == 0, stop=n == 5)
                for n in range(3):
                    mm = pe.matmul(ps[:, 0:CH], PTr[:, (6 + n) * P:(7 + n) * P], vK[n][:, 0, h * CH:h * CH + CH], start=n == 0, stop=n == 2)
                mm.then_inc(sig("small_full"), 1)
            channels2("g2a 0")
            channels2("g2a 1")
            pe.wait_ge(sig("attn_done"), 1)
            for i in range(2):
                ps = small(f"aT {i}")
                for m in range(2):
                    for j in range(TT):
                        mm = pe.transpose(ps[:, m * T + j * P:m * T + j * P + P], attn[:, j, (2 * i + m) * P:(2 * i + m + 1) * P], ident)
                mm.then_inc(sig("small_full"), 1)
            pe.wait_ge(sig("poolw_loaded"), 16)
            pe.wait_ge(sig("pooled"), 1)
            for i in range(2):
                ps = small(f"pool {i}")
                for m in range(2):
                    mm = pe.matmul(ps[:, m * T:m * T + T], POOLW[:, 2 * i + m, :], pooled[:, 2 * i + m, :], start=True, stop=True)
                mm.then_inc(sig("small_full"), 1)
            pe.wait_ge(sig("small_out"), small_no("aT 1") + 1)
            merge2("Wb2a", attnT)
            channels2("g2p 0")
            channels2("g2p 1")
            pe.wait_ge(sig("pool_done"), 1)
            merge2("Wb2p", poolT)
            pe.wait_ge(sig("merged2"), 2)
            for half in range(2):
                w = unit2(f"out2 {half}")
                for j in range(TT):
                    ps = small(f"mix2 {2 * half + j}")
                    for k in range(KD):
                        mm = pe.matmul(ps[:, :], MERGED2[:, k, j * P:j * P + P], w[:, k, :], start=k == 0, stop=k == KD - 1)
                    mm.then_inc(sig("small_full"), 1)

        @block.scalar
        def _(act):
            count = {}

            def do(ins_, s="act_chain"):
                count[s] = count.get(s, 0) + 1
                ins_.then_inc(sig(s), 1)
                act.wait_ge(sig(s), count[s])

            def out(name, dst, func=ACT.Copy, src=None):
                n = proj_no(name)
                act.wait_ge(sig("proj_full"), n + 1)
                ps = proj_bank[n % 4]
                v = ps[:, :] if src is None else src(ps)
                if len(dst.shape) == 3 and src is None:
                    v = ps[:, :].rearrange("p (a b) -> p a b", b=dst.shape[2])
                act.activation(dst, v, func).then_inc(sig("proj_out"), 1)

            def channels(what, dst, func=ACT.Copy):
                for b in range(2):
                    out(f"{what} {b}", dst[:, 2 * b:2 * b + 2, :], func)

            def gates(b, before):
                if before:
                    act.wait_ge(sig("merged"), before)
                for i in range(4):
                    out(f"G {b} {i}", SG[:, 2 * i:2 * i + 2, :], ACT.Sigmoid)

            act.wait_ge(sig("lam_abs"), 1)
            do(act.activation(lam[:, 1], lam[:, 0], ACT.Exp), "lam_exp")
            act.wait_ge(sig("lam_u"), 1)
            do(act.activation(lam[:, 3], lam[:, 2], ACT.Ln), "lam_ln")
            channels("D xr", xr[:, :, 3:])
            channels("D gate", lgate)
            channels("C q", cz[:, 0:4, 3:])
            channels("C k", cz[:, 4:8, 3:])
            for j in range(TT):
                out(f"C v {j}", vC[:, j, :])
            channels("C o", oC, ACT.Sigmoid)
            out("C if", rows[0:4, 0:2, :], src=lambda ps: ps[0:4, :].rearrange("p (a b) -> p a b", b=T))
            act.wait_ge(sig("D_gates"), 1)
            do(act.activation(gx, gx, ACT.Sigmoid), "D_sig")
            do(act.activation(ga, ga, ACT.Sigmoid), "D_sig")
            act.wait_ge(sig("D_gelu"), 1)
            do(act.activation(lt1, lt1, ACT.Sigmoid, scale=2.0 * float(np.sqrt(2.0 / np.pi))), "D_gelu_sig")
            act.wait_ge(sig("D_loga"), 1)
            do(act.activation(lt2, ga, ACT.Tanh, scale=-1.0), "D_tanh")
            do(act.activation(ga, ga, ACT.Exp), "D_a")
            act.wait_ge(sig("D_m2"), 1)
            do(act.activation(lt2, lt2, ACT.Sqrt), "D_mult")
            act.wait_ge(sig("D_done"), 1)
            channels("B q", qB)
            channels("B f", fB)
            for j in range(TT):
                out(f"B i {j}", vB[:, j, :])
            channels("B g", gB)
            act.wait_ge(sig("C_absf"), 1)
            do(act.activation(e1C, e1C, ACT.Exp, scale=-1.0), "C_exp")
            act.wait_ge(sig("C_u1"), 1)
            do(act.activation(e2C, e2C, ACT.Ln), "C_ln")
            act.wait_ge(sig("C_conv"), 1)
            do(act.activation(cz[:, :, 0:T], qk, ACT.Sigmoid), "C_silu")
            act.wait_ge(sig("C_dist"), 1)
            do(act.activation(wC, wC, ACT.Exp, scale=-1.0), "C_w")
            do(act.activation(emC, colC[:, 1, :], ACT.Exp, scale=-1.0), "C_em")
            gates("D", 0)

            def rsqrt(v, wait, s):
                act.wait_ge(sig(wait), 1)
                do(act.activation(v, v, ACT.Ln))
                do(act.activation(v, v, ACT.Exp, scale=-0.5), s)

            rsqrt(stC[:, 2, :], "C_var", "C_rstd")
            act.wait_ge(sig("C_done"), 1)
            act.wait_ge(sig("B_start"), 1)
            do(act.activation(tB, qB, ACT.Sigmoid))
            do(act.activation(kB, fB, ACT.Sigmoid, scale=-1.0))
            do(act.activation(eB, gB, ACT.Sigmoid), "B_sig")
            act.wait_ge(sig("B_absf"), 1)
            do(act.activation(cB, cB, ACT.Exp, scale=-1.0))
            do(act.activation(cB, cB, ACT.Ln, bias=1.0), "B_ln")
            fill = {0: "A r", 2: "A k", 4: "A v", 6: "A x"}
            for l in range(8):
                act.wait_ge(sig("B_diff"), l + 1)
                do(act.activation(eB, eB, ACT.Exp), "B_exp")
                if l in fill:
                    if l < 6:
                        channels(fill[l], zA[:, 2 * l:2 * l + 4, 1:])
                    else:
                        out("A x", zA[:, 12:14, 1:])
            gates("C", 1)
            rsqrt(stB[:, 1, :], "B_var", "B_rstd")
            act.wait_ge(sig("A_mixed"), 1)
            do(act.activation(zmix[0:64, 12, :], zmix[0:64, 12, :], ACT.Tanh))
            do(act.activation(zmix[:, 13, :], zmix[:, 13, :], ACT.Sigmoid), "A_tanh")
            act.wait_ge(sig("A_lowrank"), 1)
            do(act.activation(e2A, e2A, ACT.Sigmoid))
            do(act.activation(aA, aA, ACT.Sigmoid), "A_sig")
            act.wait_ge(sig("A_kksum"), 1)
            do(act.activation(e1A, e1A, ACT.Sqrt), "A_norm")
            act.wait_ge(sig("A_cum"), 1)
            do(act.activation(e1A, cumA, ACT.Exp, scale=-E_HALF))
            do(act.activation(e3A, e2A, ACT.Exp, scale=-E_HALF))
            do(act.activation(e2A, cumA, ACT.Exp, scale=E_HALF), "A_exps")
            gates("B", 2)
            gates("A", 3)
            rsqrt(stA[:, 1, :], "A_var", "A_rstd")
            rsqrt(rs1, "ln1_var", "ln1_rstd")
            act.wait_ge(sig("logits_ready"), 1)
            do(act.activation(ex, ex, ACT.Exp), "router_exp")
            act.wait_ge(sig("ple_ready"), 1)
            do(act.activation(PG, PG, ACT.Sigmoid), "ple_sig")
            act.wait_ge(sig("gathered"), 1)
            act.activation(XG, x_bank[:, :].rearrange("p (a b) -> p a b", b=CAP), ACT.Copy).then_inc(sig("xg_ready"), 1)
            act.wait_ge(sig("total_ready"), 1)
            n_steps = act.value_load(total[0:1, 0:1], min_val=EXPERTS, max_val=EXPERTS * T // CAP)
            with act.Fori(0, n_steps) as i:
                act.wait_ge(sig("g_ready"), i + 1)
                act.activation(SGH, GH, ACT.Sigmoid, scale=1.702).then_inc(sig("sig_ready"), 1)
                act.wait_ge(sig("gathered"), i + 2)
                act.activation(XG, x_bank[:, :].rearrange("p (a b) -> p a b", b=CAP), ACT.Copy).then_inc(sig("xg_ready"), 1)
                act.wait_ge(sig("ht_full"), i + 1)
                act.activation(HM.rearrange("p m s c -> p (m s c)"), gate_bank[:, :], ACT.Copy).then_inc(sig("hm_ready"), 1)
                act.wait_ge(sig("y_full"), i + 1)
                act.activation(YSB, y_bank[:, :], ACT.Copy).then_inc(sig("y_ready"), 1)
            act.wait_ge(sig("y_ready"), n_steps + 1)
            act.nop().then_inc(sig("last_y_ready"), 1)
            rsqrt(rs2, "ln2_var", "ln2_rstd")
            for n, (src, ss, rs, wait) in enumerate(((x2, ss2, rs3, "x2_done"),)):
                act.wait_ge(sig(wait), 2)
                for j in range(TT):
                    do(act.activation(base[:, j, :], src[:, j, :], ACT.Square, accum_out=ss[:, j:j + 1]), "squares2")
            rsqrt(ss2, "rms2_var", "rms2_rstd")
            for g in range(GROUPS):
                for b in range(2):
                    out(f"Q{g} {b}", qT[g][:, 2 * b:2 * b + 2, :])
                for b in range(2):
                    out(f"K{g} {b}", kT[g][:, 2 * b:2 * b + 2, :])
                for j in range(TT):
                    out(f"V{g} {j}", vK[g][:, j, :])

            def exponentials(h):
                act.wait_ge(sig("max_ready"), h + 1)
                for b, (lo, n) in enumerate(((0, 512), (512, 256), (768, 384))):
                    j = 1 if b < 2 else 0
                    act.activation(PB[h % 2][:, lo:lo + n], proj_bank[proj_no(f"L {h} {b}") % 4][:, 0:n], ACT.Exp, scale=0.125,
                                   bias=nmax[:, h % 2, j:j + 1], accum_out=den[:, h % 2, b:b + 1]).then_inc(sig("proj_out"), 1)

            exponentials(0)
            for h in range(HEADS):
                if h < HEADS - 1:
                    if h >= 1:
                        act.wait_ge(sig("small_full"), small_no(f"T {h - 1} 2") + 1)
                        act.wait_ge(sig("small_out"), small_no(f"O {h - 1}") + 1)
                    exponentials(h + 1)
                if h == 0:
                    for j in range(TT):
                        out(f"Z {j}", zat[:, j, :])
                if h == 1:
                    for b in range(2):
                        out(f"U {b}", u0[:, 2 * b:2 * b + 2, 16:])
                if h == 2:
                    for b in range(2):
                        out(f"ZP {b}", zp[:, 2 * b:2 * b + 2, :])
            act.wait_ge(sig("small_full"), small_no("T 7 2") + 1)
            act.wait_ge(sig("proj_out"), proj_no("ZP 1") + 1)
            do(act.activation(zsig, zat, ACT.Sigmoid), "zsig")
            do(act.activation(zpsig, zp, ACT.Sigmoid), "zpsig")
            for n, before in (("g2a", 0), ("g2p", 1)):
                if before:
                    act.wait_ge(sig("merged2"), before)
                for i in range(4):
                    out(f"{n} {i}", SG[:, 2 * i:2 * i + 2, :], ACT.Sigmoid)
            act.wait_ge(sig("x3_ready"), 2)
            for j in range(TT):
                do(act.activation(base[:, j, :], x3[:, j, :], ACT.Square, accum_out=ss3[:, j:j + 1]), "squares3")
            rsqrt(ss3, "rms3_var", "rms3_rstd")

        @block.vector
        def _(dve):
            count = {}

            def do(ins_, s="dve_chain"):
                count[s] = count.get(s, 0) + 1
                ins_.then_inc(sig(s), 1)
                dve.wait_ge(sig(s), count[s])

            def full(name):
                n = small_no(name)
                dve.wait_ge(sig("small_full"), n + 1)
                assert count.get("small_out", 0) == n, (name, n, count.get("small_out", 0))
                return small_bank[n % 4]

            def tiles(ps, n=T):
                return ps[:, :].rearrange("p (a b) -> p a b", b=n)

            TTn, TS, STT = dve.tensor_tensor, dve.tensor_scalar, dve.scalar_tensor_tensor

            def merge(b, first):
                for i in range(4):
                    ps = full(f"Wb {b} {i}")
                    g, m = SG[:, 2 * i:2 * i + 2, :], MERGED[:, 2 * i:2 * i + 2, :]
                    dve.wait_ge(sig("proj_out"), proj_no(f"G {b} {i}") + 1)
                    if first:
                        do(TTn(m, tiles(ps), g, ALU.mult), "small_out")
                    else:
                        do(TTn(g, tiles(ps), g, ALU.mult), "small_out")
                        do(TTn(m, m, g, ALU.add))
                dve.nop().then_inc(sig("merged"), 1)

            dve.wait_ge(sig("const_loaded"), 16)
            do(dve.tensor_copy(PV[:, 0:NVEC], full("vectors")[:, 0:NVEC]), "small_out")
            for g in range(4):
                do(dve.tensor_copy(XT[:, 2 * g:2 * g + 2, :], tiles(full(f"x {g}"))), "small_out")

            do(dve.memset(xr[:, :, 0:3], 0.0))
            do(dve.memset(cz[:, :, 0:3], 0.0))
            LAM = pv("lru_lambda")
            do(STT(lam[:, 0], LAM, -1.0, LAM, ALU.mult, ALU.min), "lam_abs")
            dve.wait_ge(sig("lam_exp"), 1)
            do(TS(lam[:, 2], lam[:, 1], 1.0, None, ALU.add), "lam_u")
            do(STT(lam[:, 4], lam[:, 2], -1.0, lam[:, 1], ALU.add, ALU.subtract))
            do(dve.reciprocal(lam[:, 0], lam[:, 2]))
            do(TTn(lam[:, 4], lam[:, 4], lam[:, 0], ALU.mult))
            dve.wait_ge(sig("lam_ln"), 1)
            do(TTn(lam[:, 4], lam[:, 3], lam[:, 4], ALU.subtract))
            do(STT(lam[:, 4], LAM, 0.0, lam[:, 4], ALU.min, ALU.subtract))
            do(TS(lam[:, 4], lam[:, 4], 8.0, None, ALU.mult))
            dve.wait_ge(sig("proj_out"), proj_no("D xr 1") + 1)

            def conv(dst, src, w, b, tiles_):
                for m in range(tiles_):
                    do(TS(dst[:, m, :], src[:, m, 0:T], w(0, m), b(m), ALU.mult, ALU.add))
                    for tap in range(1, 4):
                        do(STT(dst[:, m, :], src[:, m, tap:tap + T], w(tap, m), dst[:, m, :], ALU.mult, ALU.add))

            conv(xc, xr, lambda tap, m: pv("lru_conv_w", 4 * tap + m, 4 * tap + m + 1), lambda m: pv("lru_conv_b", m, m + 1), 4)
            dve.nop().then_inc(sig("D_conv"), 1)
            for nm, dst in (("gx", gx), ("ga", ga)):
                bias = "lru_bx" if nm == "gx" else "lru_ba"
                for i in range(2):
                    do(TTn(dst[:, 2 * i:2 * i + 2, :], tiles(full(f"D {nm} {i}")), over(pv(bias, 2 * i, 2 * i + 2), T), ALU.add), "small_out")
            dve.nop().then_inc(sig("D_gates"), 1)
            dve.wait_ge(sig("proj_out"), proj_no("D gate 1") + 1)
            do(TTn(lt1, lgate, lgate, ALU.mult))
            do(TS(lt1, lt1, 0.044715, 1.0, ALU.mult, ALU.add))
            do(TTn(lt1, lt1, lgate, ALU.mult), "D_gelu")
            dve.wait_ge(sig("D_sig"), 2)
            do(TTn(ga, ga, over(lam[:, 4], T), ALU.mult), "D_loga")
            do(TTn(gx, gx, xc, ALU.mult))
            dve.wait_ge(sig("D_gelu_sig"), 1)
            do(TTn(lgate, lgate, lt1, ALU.mult))
            dve.wait_ge(sig("D_a"), 1)
            do(TTn(lt1, ga, ga, ALU.mult))
            do(STT(lt2, lt1, 1.0, lt2, ALU.add, ALU.mult), "D_m2")
            dve.wait_ge(sig("D_mult"), 1)
            do(dve.memset(lt2[:, :, 0:1], 1.0))
            do(TTn(gx, gx, lt2, ALU.mult))
            for m in range(KW):
                do(dve.tensor_tensor_scan(lt1[:, m, :], ga[:, m, :], gx[:, m, :], 0.0, ALU.mult, ALU.add))
            do(TTn(YT["D"], lt1, lgate, ALU.mult), "D_done")

            def log_sigmoid(dst, f, e1, e2, absf, u1, ln, exp, tmp, tmp2):
                do(STT(e1, f, -1.0, f, ALU.mult, ALU.max), absf)
                dve.wait_ge(sig(exp), 1)
                do(TS(e2, e1, 1.0, None, ALU.add), u1)
                do(TS(tmp, e1, 1.0, None, ALU.add))
                do(STT(tmp2, tmp, -1.0, e1, ALU.add, ALU.subtract))
                do(dve.reciprocal(tmp, tmp))
                do(TTn(tmp, tmp, tmp2, ALU.mult))
                dve.wait_ge(sig(ln), 1)
                do(TTn(tmp, e2, tmp, ALU.subtract))
                do(STT(dst, f, 0.0, tmp, ALU.min, ALU.subtract))

            dve.wait_ge(sig("proj_out"), proj_no("C if") + 1)
            dve.wait_ge(sig("ifb_loaded"), 32)
            do(TS(iC, iC, ifb[0:4, 0:1], None, ALU.add))
            do(TS(fC, fC, ifb[0:4, 1:2], None, ALU.add))
            log_sigmoid(fC, fC, e1C, e2C, "C_absf", "C_u1", "C_ln", "C_exp", uC, gC)
            on = c("ones")[0:4, :]
            do(dve.tensor_tensor_scan(mC, on, fC, 0.0, ALU.mult, ALU.add))
            do(TTn(uC, iC, mC, ALU.subtract))
            do(dve.tensor_tensor_scan(gC, on, uC, NEG, ALU.mult, ALU.max))
            do(TTn(mC, mC, gC, ALU.add), "C_rows")
            conv(qk, cz, lambda tap, m: pv("mlstm_conv_w", 8 * tap + m, 8 * tap + m + 1), lambda m: pv("mlstm_conv_b", m, m + 1), 8)
            dve.nop().then_inc(sig("C_conv"), 1)
            dve.wait_ge(sig("C_silu"), 1)
            do(TTn(qk[:, 0:4], qk[:, 0:4], cz[:, 0:4, 0:T], ALU.mult))
            do(STT(qk[:, 4:8], qk[:, 4:8], float(P) ** -0.5, cz[:, 4:8, 0:T], ALU.mult, ALU.mult), "C_qk")
            for i in range(2):
                n = small_no(f"C row {i}")
                dve.wait_ge(sig("small_full"), n + 1)
            dve.wait_ge(sig("small_full"), small_no("C col") + 1)
            cps = small_bank[small_no("C col") % 4]
            do(dve.tensor_copy(colC.rearrange("p a b -> p (a b)"), cps[:, 0:16]))
            for i in range(2):
                ps = full(f"C row {i}")
                for m in range(2):
                    h = 2 * i + m
                    do(TS(wC[:, h, 0:T], ps[:, m * T:m * T + T], colC[:, 0, h:h + 1], 0.0, ALU.subtract, ALU.max))
                    do(TS(wC[:, h, T:T + P], ps[:, m * T + P:m * T + T], colC[:, 0, 4 + h:5 + h], 0.0, ALU.subtract, ALU.max),
                       "small_out" if m == 1 else "dve_chain")
            full("C col")
            do(TS(emC, colC[:, 1, :], 0.0, None, ALU.add), "small_out")
            dve.nop().then_inc(sig("C_dist"), 1)
            dve.wait_ge(sig("C_w"), 1)
            do(TTn(wC[:, :, 0:P], wC[:, :, 0:P], along(c("upper"), 4), ALU.mult))
            do(TTn(wC[:, :, T:T + P], wC[:, :, T:T + P], along(c("upper"), 4), ALU.mult))
            for h in range(4):
                do(TTn(sC[:, h, :], full(f"C S {h}")[:, 0:384], wC[:, h, :], ALU.mult), "small_out")
            dve.nop().then_inc(sig("C_weights"), 1)
            for j in range(TT):
                do(dve.tensor_copy(hC[:, 4 * j:4 * j + 4, :], tiles(full(f"C num {j}"), P)), "small_out")
            do(dve.tensor_copy(denC, full("C den")[:, 0:8]), "small_out")
            dve.wait_ge(sig("C_em"), 1)
            do(STT(stC[:, 0, :], denC, -1.0, denC, ALU.mult, ALU.max))
            do(TTn(stC[:, 0, :], stC[:, 0, :], emC, ALU.max))
            do(dve.reciprocal(stC[:, 0, :], stC[:, 0, :]))
            do(TTn(hC, hC, over(stC[:, 0, :], P), ALU.mult))

            def centre(v, sq, mean, var, n, eps):
                do(dve.tensor_reduce(mean, v, AX.X, ALU.add))
                do(TS(mean, mean, 1.0 / n, None, ALU.mult))
                do(TTn(v, v, over(mean, n), ALU.subtract))
                do(TTn(sq, v, v, ALU.mult))
                do(dve.tensor_reduce(var, sq, AX.X, ALU.add))

            centre(hC, hC2, stC[:, 1, :], stC[:, 2, :], P, 1e-6)
            do(TS(stC[:, 2, :], stC[:, 2, :], 1.0 / P, 1e-6, ALU.mult, ALU.add), "C_var")
            dve.wait_ge(sig("C_rstd"), 1)
            do(TTn(hC, hC, over(stC[:, 2, :], P), ALU.mult), "C_normed")
            for i in range(2):
                ps = full(f"C yT {i}")
                for m in range(2):
                    ct = 2 * i + m
                    do(STT(YT["C"][:, ct, :], ps[:, m * T:m * T + T], pv("mlstm_norm_w", ct, ct + 1), oC[:, ct, :], ALU.mult, ALU.mult),
                       "small_out" if m == 1 else "dve_chain")
            dve.nop().then_inc(sig("C_done"), 1)
            do(dve.memset(zA[:, :, 0:1], 0.0))
            merge("D", True)

            dve.wait_ge(sig("proj_out"), proj_no("B g 1") + 1)
            dve.nop().then_inc(sig("B_start"), 1)
            do(STT(cB, fB, -1.0, fB, ALU.mult, ALU.max), "B_absf")
            dve.wait_ge(sig("B_sig"), 1)
            do(TTn(qB, qB, tB, ALU.mult), "B_qk")
            do(TTn(gB, gB, eB, ALU.mult))
            dve.wait_ge(sig("B_ln"), 1)
            do(STT(fB, fB, 0.0, cB, ALU.min, ALU.subtract))
            for m in range(KW):
                do(dve.tensor_tensor_scan(cB[:, m, :], c("ones"), fB[:, m, :], 0.0, ALU.mult, ALU.add))
            for j in range(TT):
                do(TTn(aB[:, 4 * j:4 * j + 4, :], tiles(full(f"B diag {j}"), P), along(ident, 4), ALU.mult), "small_out")
            for l in range(8):
                h = 1 << l

                def half(v, right):
                    return v.rearrange("p a (n r i) -> p (a n) r i", r=2, i=h)[:, :, right, :]

                ref = half(cB, 0)[:, :, h - 1:h].to_broadcast([P, 4 * T // (2 * h), h])
                if l > 0:
                    dve.wait_ge(sig("small_full"), small_no(f"B level {l - 1} 1") + 1)
                do(TTn(half(eB, 1), half(cB, 1), ref, ALU.subtract))
                do(TTn(half(eB, 0), ref, half(cB, 0), ALU.subtract), "B_diff")
                dve.wait_ge(sig("B_exp"), l + 1)
                do(TTn(half(eB, 1), half(eB, 1), half(qB, 1), ALU.mult))
                do(TTn(half(eB, 0), half(eB, 0), half(kB, 0), ALU.mult), "B_level")
                if l < 7:
                    for j in range(TT):
                        t_ = tB.rearrange("p a b -> p (a b)")[:, 0:512].rearrange("p (a b) -> p a b", b=P)
                        do(TTn(t_, tiles(full(f"B level {l} {j}"), P), along(c("level", l * P, l * P + P), 4), ALU.mult), "small_out")
                        do(TTn(aB[:, 4 * j:4 * j + 4, :], aB[:, 4 * j:4 * j + 4, :], t_, ALU.add))
                else:
                    do(dve.tensor_copy(aX, tiles(full("B cross"), P)), "small_out")
            o2 = tB2.rearrange("p a b -> p (a b)").rearrange("p (a b) -> p a b", b=P)
            sq = tB.rearrange("p a b -> p (a b)").rearrange("p (a b) -> p a b", b=P)
            for j in range(TT):
                do(dve.tensor_copy(o2[:, 4 * j:4 * j + 4, :], tiles(full(f"B o {j}"), P)), "small_out")
            do(TTn(sq, o2, o2, ALU.mult))
            do(dve.tensor_reduce(stB[:, 1, :], sq, AX.X, ALU.add))
            do(TS(stB[:, 1, :], stB[:, 1, :], 1.0 / P, 1e-6, ALU.mult, ALU.add), "B_var")
            dve.wait_ge(sig("proj_out"), proj_no("A x") + 1)
            do(TTn(dA, zA[:, :, 0:T], zmix, ALU.subtract))
            for m in range(14):
                do(STT(zmix[:, m, :], dA[:, m, :], pv("rwkv_mu", m, m + 1), zmix[:, m, :], ALU.mult, ALU.add))
            dve.nop().then_inc(sig("A_mixed"), 1)
            dve.wait_ge(sig("B_rstd"), 1)
            do(TTn(o2, o2, over(stB[:, 1, :], P), ALU.mult), "B_normed")
            for i in range(2):
                ps = full(f"B yT {i}")
                for m in range(2):
                    ct = 2 * i + m
                    do(STT(YT["B"][:, ct, :], ps[:, m * T:m * T + T], pv("hgrn_norm_w", ct, ct + 1), gB[:, ct, :], ALU.mult, ALU.mult),
                       "small_out" if m == 1 else "dve_chain")
            dve.nop().then_inc(sig("B_done"), 1)

            for nm, dst in (("w", e2A), ("a", aA), ("g", gA)):
                for i in range(2):
                    d = dst[:, 2 * i:2 * i + 2, :]
                    ps = tiles(full(f"A {nm} {i}"))
                    if nm == "g":
                        do(dve.tensor_copy(d, ps), "small_out")
                    else:
                        do(TTn(d, ps, over(pv("rwkv_w0" if nm == "w" else "rwkv_a0", 2 * i, 2 * i + 2), T), ALU.add), "small_out")
                if nm == "a":
                    dve.nop().then_inc(sig("A_lowrank"), 1)
            do(TTn(kkA, kA, over(pv("rwkv_k_k"), T), ALU.mult))
            do(TTn(bA, kkA, kkA, ALU.mult), "A_kksq")
            for i in range(2):
                do(dve.tensor_copy(e1A[:, 2 * i:2 * i + 2, :], tiles(full(f"A kk {i}"))), "small_out")
            dve.nop().then_inc(sig("A_kksum"), 1)
            for i in range(2):
                do(dve.tensor_copy(Vt[:, i, :], full(f"A V {i}")[:, :]), "small_out")
            dve.wait_ge(sig("A_sig"), 1)
            do(STT(bonusA, aA, -1.0, over(pv("rwkv_k_a"), T), ALU.add, ALU.mult))
            do(STT(kA, bonusA, 1.0, kA, ALU.add, ALU.mult))
            do(TTn(bonusA, rA, kA, ALU.mult))
            do(TTn(bonusA, bonusA, over(pv("rwkv_r_k"), T), ALU.mult), "A_rk")
            dve.wait_ge(sig("A_norm"), 1)
            do(TS(e1A, e1A, 1e-12, None, ALU.max))
            do(dve.reciprocal(e1A, e1A))
            do(TTn(kkA, kkA, e1A, ALU.mult))
            do(TTn(bA, kkA, aA, ALU.mult))
            for m in range(KW):
                do(dve.tensor_tensor_scan(cumA[:, m, :], c("reset64"), e2A[:, m, :], 0.0, ALU.mult, ALU.add))
            do(TTn(e2A, cumA, e2A, ALU.subtract), "A_cum")
            for i in range(2):
                do(TTn(bonusA[:, 2 * i:2 * i + 2, :], tiles(full(f"A bonus {i}")), vA[:, 2 * i:2 * i + 2, :], ALU.mult), "small_out")
            dve.wait_ge(sig("A_exps"), 1)
            do(STT(kkA, kkA, -1.0, e3A, ALU.mult, ALU.mult))
            do(TTn(bA, bA, e2A, ALU.mult))
            do(TTn(kA, kA, e2A, ALU.mult))
            do(TTn(rA, rA, e1A, ALU.mult), "A_tilde")
            for nm, dst in (("At", At), ("Bt", Bt), ("Kt", Kt)):
                for i in range(2):
                    do(dve.tensor_copy(dst[:, i, :], full(f"A {nm} {i}")[:, :]), "small_out")

            def masked(name, dst, mask):
                for i in range(4):
                    do(TTn(dst[:, 4 * i:4 * i + 4, :], tiles(full(f"A {name} {i}"), P), along(c(mask), 4), ALU.mult), "small_out")

            masked("NT", NT, "strict64")
            dve.wait_ge(sig("NTm_ready"), 1)
            do(TTn(DTa, NTm, along(ident, 16), ALU.add))
            for i in range(4):
                do(TTn(Da[:, 4 * i:4 * i + 4, :], tiles(full(f"A X0 {i}"), P), along(ident, 4), ALU.add), "small_out")
            merge("C", False)
            for l in range(1, 6):
                for i in range(4):
                    do(dve.tensor_copy(X[:, 4 * i:4 * i + 4, :], tiles(full(f"A X{l} {i}"), P)), "small_out")
                for nm, m in (("D", Da), ("DT", DTa)):
                    if (nm, l) == ("D", 5):
                        continue
                    for i in range(4):
                        do(TTn(m[:, 4 * i:4 * i + 4, :], tiles(full(f"A {nm}{l} {i}"), P), m[:, 4 * i:4 * i + 4, :], ALU.add), "small_out")
            merge("B", False)
            masked("AkT", AkT, "strict64")
            for j in range(TT):
                do(dve.tensor_copy(GT[:, :, j * P:j * P + P], tiles(full(f"A GT {j}"), P)), "small_out")
            for j in range(TT):
                do(dve.tensor_copy(WU[:, j, :], full(f"A W {j}")[:, :]), "small_out")
            for j in range(TT):
                do(dve.tensor_copy(Ut[:, j, :], full(f"A U0 {j}")[:, :]), "small_out")
            dve.nop().then_inc(sig("A_u"), 1)
            for ch in range(4):
                j, po = ch // 2, 64 * (ch % 2)
                if ch > 0:
                    for odd in range(2):
                        u = Ut[po:po + 64, j, :].rearrange("p (a r v) -> p a r v", r=2, v=CH)[:, :, odd, :]
                        ps = full(f"A U {ch} {odd}")[po:po + 64, 0:256].rearrange("p (a v) -> p a v", v=CH)
                        do(TTn(u, ps, u, ALU.add), "small_out")
                    dve.nop().then_inc(sig("A_u"), 1)
                if ch < 3:
                    s = S_all[:, ch + 1, :].rearrange("p (a b) -> p a b", b=CH)
                    decay = over(e1A[:, :, ch * CH + CH - 1], CH)
                    ps = full(f"A S {ch}")[:, 0:256].rearrange("p (a b) -> p a b", b=CH)
                    if ch == 0:
                        do(TTn(s, ps, decay, ALU.mult), "small_out")
                    else:
                        do(TTn(s, ps, S_all[:, ch, :].rearrange("p (a b) -> p a b", b=CH), ALU.add), "small_out")
                        do(TTn(s, s, decay, ALU.mult))
                    dve.nop().then_inc(sig("A_state"), 1)
            dve.nop().then_inc(sig("A_states_done"), 1)
            masked("RbT", RbT, "upper64")
            masked("RkT", RkT, "upper64")
            for i in range(4):
                j, odd = divmod(i, 2)
                ps = full(f"A Y {i}")[:, 0:256].rearrange("p (a v) -> p a v", v=CH)
                do(dve.tensor_copy(Ysum[:, 8 * j + odd:8 * j + 8:2, :], ps), "small_out")
            centre(Ysum, Ysq, stA[:, 0, :], stA[:, 1, :], CH, 64e-5)
            do(TS(stA[:, 1, :], stA[:, 1, :], 1.0 / CH, 64e-5, ALU.mult, ALU.add), "A_var")
            dve.wait_ge(sig("A_rstd"), 1)
            do(TTn(Ysum, Ysum, over(stA[:, 1, :], CH), ALU.mult), "A_normed")
            for i in range(2):
                ps = full(f"A yT {i}")
                for m in range(2):
                    ct = 2 * i + m
                    do(TS(YT["A"][:, ct, :], ps[:, m * T:m * T + T], pv("rwkv_lnx_g", ct, ct + 1), pv("rwkv_lnx_b", ct, ct + 1), ALU.mult, ALU.add),
                       "small_out" if m == 1 else "dve_chain")
            do(TTn(YT["A"], YT["A"], bonusA, ALU.add))
            do(TTn(YT["A"], YT["A"], gA, ALU.mult), "A_done")
            merge("A", False)

            for half_ in range(2):
                for j in range(TT):
                    do(STT(mixv[:, j, half_ * W:half_ * W + W], XTOK[:, j, half_ * W:half_ * W + W], ALPHA,
                           full(f"mix {2 * half_ + j}")[:, :], ALU.mult, ALU.add), "small_out")

            def stats(v, st, mv, rs, eps, wait):
                for j in range(TT):
                    for half_ in range(2):
                        do(dve.bn_stats(st[:, j, 6 * half_:6 * half_ + 6], v[:, j, half_ * W:half_ * W + W]))
                    do(dve.bn_aggr(mv[:, j, :], st[:, j, :]))
                do(TS(rs, mv[:, :, 1], eps, None, ALU.add), wait)

            stats(mixv, st1, mv1, rs1, 1e-5, "ln1_var")
            dve.wait_ge(sig("ln1_rstd"), 1)
            dve.wait_ge(sig("ln1_loaded"), 32)
            for j in range(TT):
                do(TS(x1[:, j, :], mixv[:, j, :], mv1[:, j, 0:1], rs1[:, j:j + 1], ALU.subtract, ALU.mult))
                do(TTn(x1[:, j, :], x1[:, j, :], bcg, ALU.mult))
                do(TTn(x1[:, j, :], x1[:, j, :], bcb, ALU.add), "x1_done")

            do(dve.tensor_copy(PV2, full("vectors2")[:, 0:40]), "small_out")
            for i in range(6):
                do(TTn(MODT[:, 4 * i:4 * i + 4], full(f"ada {i}")[:, 0:4], PV2[:, 16 + 4 * i:20 + 4 * i], ALU.add), "small_out")
            do(STT(mod_a, MODT[:, 8:16], 1.0, PV2[:, 8:16], ALU.add, ALU.mult))
            do(dve.tensor_copy(G8, full("gate8")[0:8, 0:P]), "small_out")
            for i in range(2):
                do(dve.tensor_copy(gateB[:, i * W:i * W + W], full(f"gateB {i}")[:, :]), "small_out")
            dve.wait_ge(sig("table_loaded"), 48)
            do(TTn(TAB, full("bias")[0:24, 0:BKT], BM, ALU.add), "small_out")
            dve.nop().then_inc(sig("table_done"), 1)

            for g in range(4):
                do(dve.tensor_copy(XT[:, 2 * g:2 * g + 2, :], tiles(full(f"x1 {g}"))), "small_out")
            dve.wait_ge(sig("router_loaded"), 80)
            do(TTn(lg, full("logits")[:, 0:64].rearrange("p (a b) -> p a b", b=EXPERTS), along(RB, TT), ALU.add), "small_out")
            for j in range(TT):
                do(dve.max(mx8[:, j, :], lg[:, j, :]))
                do(TS(ex[:, j, :], lg[:, j, :], mx8[:, j, 0:1], None, ALU.subtract), "logits_ready" if j == 1 else "dve_chain")
                do(TS(above[:, j, :], lg[:, j, :], mx8[:, j, 3:4], None, ALU.is_gt))
                do(TS(tie[:, j, :], lg[:, j, :], mx8[:, j, 3:4], None, ALU.is_equal))
                do(dve.tensor_tensor_scan(cum[:, j, :], c("ones", 0, EXPERTS), tie[:, j, :], 0.0, ALU.mult, ALU.add))
            do(dve.tensor_reduce(few[:, 0, :], above, AX.X, ALU.add))
            do(TS(few[:, 1, :], few[:, 0, :], -1.0, 4.0, ALU.mult, ALU.add))
            do(TTn(cum, cum, over(few[:, 1, :], EXPERTS), ALU.is_le))
            do(TTn(cum, cum, tie, ALU.mult))
            do(TTn(sel, above, cum, ALU.add))
            dve.wait_ge(sig("router_exp"), 1)
            do(TTn(gates_, ex, sel, ALU.mult))
            do(dve.tensor_reduce(few[:, 2, :], gates_, AX.X, ALU.add))
            do(dve.reciprocal(few[:, 3, :], few[:, 2, :]))
            do(TTn(gates_, gates_, over(few[:, 3, :], EXPERTS), ALU.mult), "gates_ready")
            do(dve.tensor_copy(GTT, full("gateT")[0:EXPERTS, 0:T]), "small_out")
            ps = full("rank")
            do(dve.tensor_reduce(top[:, 0:1], ps[:, 64:96], AX.X, ALU.max))
            do(STT(rank, ps[:, 0:64].rearrange("p (a b) -> p a b", b=EXPERTS), 4096.0, sel, ALU.add, ALU.mult), "small_out")
            do(TS(rank, rank, -4096.0, None, ALU.add))
            do(TS(top[:, 1:2], top[:, 0:1], float(CAP), 1.0, ALU.is_gt, ALU.add))
            for n in (2, 3):
                do(STT(top[:, 1:2], top[:, 0:1], float(n * CAP), top[:, 1:2], ALU.is_gt, ALU.add))
            do(TS(total, top[:, 1:2], float(EXPERTS), None, ALU.mult), "total_ready")
            do(dve.tensor_copy(PTT, tiles(full("pT"))), "small_out")
            for i in range(4):
                half_, j = divmod(i, 2)
                do(dve.tensor_copy(PG[:, j, half_ * W:half_ * W + W], full(f"ple {i}")[:, :]), "small_out")
            dve.nop().then_inc(sig("ple_ready"), 1)
            dve.wait_ge(sig("ple_sig"), 1)
            for i in range(4):
                half_, j = divmod(i, 2)
                do(TTn(base[:, j, half_ * W:half_ * W + W], full(f"pp {i}")[:, :], PG[:, j, half_ * W:half_ * W + W], ALU.mult), "small_out")
            do(STT(base, x1, ALPHA, base, ALU.mult, ALU.add), "base_done")

            def pick(dst, e, ready, weight):
                for j in range(TT):
                    if weight:
                        op = TS(dst[:, j, :].rearrange("p (s c) -> p s c", s=2), along(c("slot"), 2), rank[:, j, bass.ds(e, 1)], gates_[:, j, bass.ds(e, 1)], ALU.is_equal, ALU.mult)
                    else:
                        op = TS(dst[:, j, :], c("slot"), rank[:, j, bass.ds(e, 1)], None, ALU.is_equal)
                op.then_inc(sig(ready), 1)

            do(dve.memset(YSB, 0.0), "y_ready")
            do(dve.memset(PTW, 0.0), "ptw_ready")
            do(dve.tensor_copy(ESEL, c("ident", 0, 1).to_broadcast([P, CAP])), "esel_ready")
            pick(PICK, 0, "pick_ready", False)
            n_steps = dve.value_load(total[0:1, 0:1], min_val=EXPERTS, max_val=EXPERTS * T // CAP)
            LINKS = 3
            with dve.Fori(0, n_steps) as i:
                link = [0]

                def then(ins_):
                    link[0] += 1
                    ins_.then_inc(sig("expert_chain"), 1)
                    dve.wait_ge(sig("expert_chain"), LINKS * i + link[0])

                e, nxt = i % EXPERTS, (i + 1) % EXPERTS
                dve.wait_ge(sig("ptw_full"), i + 1)
                pick(PICKW, e, "pickw_ready", True)
                dve.wait_ge(sig("pickw_ready"), i + 1)
                then(TS(rank[:, :, bass.ds(e, 1)], rank[:, :, bass.ds(e, 1)], -float(CAP), None, ALU.add))
                dve.wait_ge(sig("gathered"), i + 1)
                pick(PICK, nxt, "pick_ready", False)
                dve.wait_ge(sig("gu_full"), i + 1)
                TS(GH, gate_bank[:, :], 7.0, None, ALU.min).then_inc(sig("g_ready"), 1)
                then(TS(UH, up_bank[:, :], 7.0, -7.0, ALU.min, ALU.max))
                dve.tensor_copy(ESEL, c("ident", 0, EXPERTS)[:, bass.ds(nxt, 1)].to_broadcast([P, CAP])).then_inc(sig("esel_ready"), 1)
                dve.wait_ge(sig("sig_ready"), i + 1)
                then(TTn(GH, GH, SGH, ALU.mult))
                STT(GH, UH, 1.0, GH, ALU.add, ALU.mult).then_inc(sig("h_ready"), 1)
                dve.wait_ge(sig("ptw_full"), i + 2)
                dve.tensor_copy(PTW, y_bank[:, 0:T]).then_inc(sig("ptw_ready"), 1)
                assert link[0] == LINKS
            dve.wait_ge(sig("experts_done"), 1)
            for i in range(4):
                j, half_ = divmod(i, 2)
                v = base[:, j, half_ * W:half_ * W + W]
                do(TTn(v, acc_bank[i][:, :], v, ALU.add))
            dve.nop().then_inc(sig("acc_read"), 1)
            stats(base, st2, mv2, rs2, 1e-5, "ln2_var")
            dve.wait_ge(sig("ln2_rstd"), 1)
            dve.wait_ge(sig("ln2_loaded"), 32)
            for j in range(TT):
                do(TS(x2[:, j, :], base[:, j, :], mv2[:, j, 0:1], rs2[:, j:j + 1], ALU.subtract, ALU.mult))
                do(TTn(x2[:, j, :], x2[:, j, :], ln2g, ALU.mult))
                do(TTn(x2[:, j, :], x2[:, j, :], ln2b, ALU.add), "x2_done")

            dve.wait_ge(sig("squares2"), 2)
            do(TS(ss2, ss2, 1.0 / D, 1e-6, ALU.mult, ALU.add), "rms2_var")
            dve.wait_ge(sig("rms2_rstd"), 1)
            for j in range(TT):
                do(TS(base[:, j, :], x2[:, j, :], ss2[:, j:j + 1], None, ALU.mult), "x2n_done")
            for g in range(4):
                ps = full(f"h {g}")
                for m in range(2):
                    k = 2 * g + m
                    do(TS(HT[:, k, :], ps[:, m * T:m * T + T], mod_a[:, k:k + 1], MODT[:, k:k + 1], ALU.mult, ALU.add),
                       "small_out" if m else "dve_chain")
            do(dve.memset(u0[:, :, 0:16], 0.0))

            def maxima(h):
                for b in range(3):
                    n = proj_no(f"L {h} {b}")
                    dve.wait_ge(sig("proj_full"), n + 1)
                    do(dve.tensor_reduce(nmax[:, h % 2, 1 + b:2 + b] if b < 2 else nmax[:, h % 2, 0:1],
                                         proj_bank[n % 4][:, 0:(512, 256, 384)[b]], AX.X, ALU.max))
                do(TTn(nmax[:, h % 2, 1:2], nmax[:, h % 2, 1:2], nmax[:, h % 2, 2:3], ALU.max))
                do(TS(nmax[:, h % 2, 0:2], nmax[:, h % 2, 0:2], -0.125, None, ALU.mult), "max_ready")

            maxima(0)
            for h in range(HEADS):
                if h < HEADS - 1:
                    maxima(h + 1)
                for b in range(3):
                    n = 512 if b < 2 else P
                    do(dve.tensor_copy(PTr[:, 512 * b:512 * b + n], full(f"T {h} {b}")[:, 0:n]), "small_out")
                d = den[:, h % 2, :]
                do(TTn(d[:, 1:2], d[:, 0:1], d[:, 1:2], ALU.add))
                do(dve.reciprocal(d[:, 1:3], d[:, 1:3]))
                ps = full(f"O {h}")
                do(TS(attn[:, 1, h * CH:h * CH + CH], ps[:, CH:2 * CH], d[:, 1:2], None, ALU.mult))
                do(TS(attn[:, 0, h * CH:h * CH + CH], ps[:, 0:CH], d[:, 2:3], None, ALU.mult), "small_out")
            dve.wait_ge(sig("zsig"), 1)
            do(TTn(attn, attn, zat, ALU.mult))
            do(TTn(attn, attn, zsig, ALU.mult), "attn_done")
            src = u0
            for n in range(4):
                w_, dst = 1 << n, (uA, uB)[n % 2]
                do(TTn(dst[:, n:, w_:], src[:, n:, w_:], src[:, n:, 0:T + 16 - w_], ALU.add))
                if n < 3:
                    do(dve.tensor_copy(dst[:, n:, 0:w_], src[:, n:, 0:w_]))
                do(TTn(pooled[:, n, :], dst[:, n, 16:], c("poolcnt", n * T, n * T + T), ALU.mult))
                do(TTn(pooled[:, n, :], pooled[:, n, :], u0[:, n, 16:], ALU.subtract))
                src = dst
            dve.nop().then_inc(sig("pooled"), 1)
            for i in range(2):
                do(dve.tensor_copy(attnT[:, 2 * i:2 * i + 2, :], tiles(full(f"aT {i}"))), "small_out")
            dve.wait_ge(sig("zpsig"), 1)
            do(TTn(zp, zp, zpsig, ALU.mult))
            for i in range(2):
                ps = full(f"pool {i}")
                for m in range(2):
                    ct = 2 * i + m
                    do(STT(poolT[:, ct, :], ps[:, m * T:m * T + T], pv("pool_scale_2", ct, ct + 1), zp[:, ct, :], ALU.mult, ALU.mult),
                       "small_out" if m else "dve_chain")
            dve.nop().then_inc(sig("pool_done"), 1)
            for n, name in enumerate(("a", "p")):
                for i in range(4):
                    ps = full(f"Wb2{name} {i}")
                    g, m = SG[:, 2 * i:2 * i + 2, :], MERGED2[:, 2 * i:2 * i + 2, :]
                    dve.wait_ge(sig("proj_out"), proj_no(f"g2{name} {i}") + 1)
                    do(TTn(g if n else m, tiles(ps), g, ALU.mult), "small_out")
                    if n:
                        do(TTn(m, m, g, ALU.add))
                dve.nop().then_inc(sig("merged2"), 1)
            for i in range(4):
                half_, j = divmod(i, 2)
                cols = slice(half_ * W, half_ * W + W)
                do(TTn(x3[:, j, cols], full(f"mix2 {i}")[:, :], gateB[:, cols], ALU.mult), "small_out")
                do(TTn(x3[:, j, cols], x3[:, j, cols], x2[:, j, cols], ALU.add), "x3_ready" if half_ else "dve_chain")
            dve.wait_ge(sig("squares3"), 2)
            do(TS(ss3, ss3, 1.0 / D, 1e-6, ALU.mult, ALU.add), "rms3_var")
            dve.wait_ge(sig("rms3_rstd"), 1)
            dve.wait_ge(sig("fing_loaded"), 16)
            for j in range(TT):
                do(STT(x3[:, j, :], x3[:, j, :], ss3[:, j:j + 1], fing, ALU.mult, ALU.mult), "final")


def kernel(**inputs):
    import numpy as _np
    import concourse.bacc as _bacc
    from concourse import mybir as _mybir
    from concourse.bass_utils import run_bass_kernel_spmd as _run

    nc = _bacc.Bacc("TRN2", target_bir_lowering=False, num_devices=1)
    arrays, ins, consts = {}, {}, {}
    for name, a in inputs.items():
        a = _np.ascontiguousarray(a)
        if not a.size or name in UNUSED:
            continue
        arrays[f"in_{name}"] = a
        ins[name] = nc.dram_tensor(f"in_{name}", a.shape, _mybir.dt.from_np(a.dtype), kind="ExternalInput").ap()
    hot, mask = bias_tables()
    for name, a in (("consts", constants()), ("hot", hot), ("mask", mask)):
        arrays[f"shape_{name}"] = a
        consts[name] = nc.dram_tensor(f"shape_{name}", a.shape, F32, kind="ExternalInput").ap()
    out = nc.dram_tensor("out", (1, T, D), F32, kind="ExternalOutput").ap()
    build(nc, ins, consts, [out])
    r = _run(nc, [arrays], core_ids=[0])
    return r.results[0]["out"]
```

```python
import numpy as np
import concourse.bass as bass
from concourse import mybir
from contextlib import ExitStack

F32 = mybir.dt.float32
I32 = mybir.dt.int32
ALU = mybir.AluOpType
ACT = mybir.ActivationFunctionType
AX = mybir.AxisListType

P = 128
T = 256
TT = T // P
D = 1024
KD = D // P
W = 512
KW = W // P
CH = 64
A_COL, B_COL, C_COL, D_COL, G_COL = 0, 1792, 3840, 5896, 6920
ALPHA = 2.0 ** 0.25
E_HALF = float(np.exp(np.float64(-0.5)))
NEG = -1e30
EXPERTS = 32
CAP = 64
GU = 2 * D
HEADS = 8
UNUSED = ("hgrn_lower_bounds",)
GROUPS = 3

CONST = {}


def _place():
    at = 0
    for name, n in (("ident", 128), ("headsum", 128), ("level", 7 * 128), ("strict64", 128), ("upper64", 128),
                    ("upper", 128), ("strict", 128), ("ones", 256), ("slot", 64), ("reset64", 256),
                    ("poolcnt", 1024), ("headrow", 1024)):
        CONST[name] = (at, n)
        at += n
    return at


NCONST = _place()
BKT = 384


def constants():
    c = np.zeros((P, NCONST), np.float32)
    s, t = np.arange(P)[:, None], np.arange(P)[None, :]

    def put(name, v):
        at, n = CONST[name]
        c[:, at:at + n] = np.broadcast_to(v, (P, n))

    put("ident", s == t)
    put("headsum", s // CH == t // CH)
    put("level", np.concatenate([(s // (2 * h) == t // (2 * h)) & (s % (2 * h) < h) & (t % (2 * h) >= h)
                                 for h in (1, 2, 4, 8, 16, 32, 64)], 1))
    put("strict64", (s // CH == t // CH) & (s < t))
    put("upper64", (s // CH == t // CH) & (s <= t))
    put("upper", s <= t)
    put("strict", s < t)
    put("ones", 1.0)
    put("slot", np.arange(64)[None, :])
    put("reset64", (np.arange(256) % CH != 0)[None, :])
    put("poolcnt", np.concatenate([1.0 / np.minimum(np.arange(T) + 1, w) for w in (2, 4, 8, 16)])[None, :])
    put("headrow", np.arange(1024)[None, :] // P == s)
    return c


def bias_tables():
    n = 255 - np.arange(BKT)
    m = np.clip(n, 0, 255)
    nf = np.maximum(m, 1).astype(np.float32)
    large = 16 + (np.log(nf / np.float32(16)) / np.float32(np.log(2048 / 16)) * np.float32(16)).astype(np.int32)
    bucket = np.where(m < 16, m, np.minimum(large, 31))
    hot = (bucket[None, :] == np.arange(32)[:, None]) * 8.0 * (n >= 0)
    mask = np.zeros((24, BKT), np.float32)
    for h in range(24):
        dil = (1, 4, 16)[h // 8]
        ok = (n >= 0) & (n % dil == 0) & (n <= 128 * dil)
        mask[h] = np.where(ok, 0.0, NEG)
    return hot.astype(np.float32), mask

VEC = {}


def _place_vectors():
    at = 0
    for name, n in (("rwkv_mu", 14), ("rwkv_w0", 4), ("rwkv_a0", 4), ("rwkv_k_k", 4), ("rwkv_k_a", 4), ("rwkv_r_k", 4),
                    ("rwkv_lnx_g", 4), ("rwkv_lnx_b", 4), ("hgrn_norm_w", 4), ("mlstm_conv_w", 32),
                    ("mlstm_conv_b", 8), ("mlstm_norm_w", 4), ("lru_conv_w", 16), ("lru_conv_b", 4), ("lru_bx", 4),
                    ("lru_ba", 4), ("lru_lambda", 4), ("pool_scale_2", 4)):
        VEC[name] = (at, n)
        at += n
    return at


NVEC = _place_vectors()

UNITS = (["D xr", "D gate", "C q", "C k", "C if", "C v", "C o", "B q", "B f", "B i", "B g",
          "G D 0", "G D 1", "Wb D", "A r", "A k", "A v", "A x",
          "G C 0", "G C 1", "ada 0", "ada 1", "ada 2", "ada 3", "Wb C", "G B 0", "G B 1", "Wb B", "G A 0", "G A 1", "Wb A", "out 0", "out 1", "ada 4", "ada 5",
          "ple 0", "ple 1", "pp"])
QKV = [f"{c}{g}" for g in range(GROUPS) for c in "QKV"]
UNITS2 = QKV + ["Z", "U", "ZP", "g2a 0", "g2a 1", "Wb2a", "g2p 0", "g2p 1", "Wb2p", "out2 0", "out2 1"]
COL2 = {n: i * W for i, n in enumerate(QKV + ["Z", "U", "ZP", "g2a 0", "g2a 1", "g2p 0", "g2p 1"])}
PROJ = (["D xr 0", "D xr 1", "D gate 0", "D gate 1", "C q 0", "C q 1", "C k 0", "C k 1", "C if",
         "C v 0", "C v 1", "C o 0", "C o 1", "B q 0", "B q 1", "B f 0", "B f 1", "B i 0", "B i 1", "B g 0", "B g 1",
         "G D 0", "G D 1", "G D 2", "G D 3", "A r 0", "A r 1", "A k 0", "A k 1", "A v 0", "A v 1", "A x",
         "G C 0", "G C 1", "G C 2", "G C 3", "G B 0", "G B 1", "G B 2", "G B 3", "G A 0", "G A 1", "G A 2", "G A 3"]
        + [f"{n} {i}" for n in QKV for i in range(2)] + ["L 0 0", "L 0 1", "L 0 2"]
        + [x for h in range(HEADS) for x in
            ([f"L {h + 1} {i}" for i in range(3)] if h < 7 else []) + [f"{('Z', 'U', 'ZP', 'g2a')[h // 2]} {h % 2}"]]
         + ["g2a 2", "g2a 3"] + [f"g2p {i}" for i in range(4)])
SMALL = ([f"x {i}" for i in range(4)] + ["vectors"]
         + ["D gx 0", "D gx 1", "D ga 0", "D ga 1"]
         + ["C row 0", "C row 1", "C col"] + [f"C S {h}" for h in range(4)]
         + ["C num 0", "C num 1", "C den", "C yT 0", "C yT 1"]
         + [f"Wb D {i}" for i in range(4)]
         + ["B diag 0", "B diag 1"] + [f"B level {l} {j}" for l in range(7) for j in range(2)] + ["B cross"]
         + ["B o 0", "B o 1", "vectors2"]
         + ["A w 0", "A w 1", "A a 0", "A a 1", "A g 0", "A g 1", "A kk 0", "A kk 1", "B yT 0", "B yT 1"]
         + ["A V 0", "A V 1", "ada rows 0", "A bonus 0", "A bonus 1", "ada 0", "ada rows 1"]
         + [f"A {n} {i}" for n in ("At", "Bt", "Kt") for i in range(2)] + ["ada 1", "ada rows 2"]
         + [f"A NT {i}" for i in range(4)] + ["ada 2", "ada rows 3"] + [f"A X0 {i}" for i in range(4)] + ["ada 3"]
         + [f"Wb C {i}" for i in range(4)]
         + [f"A {n}{l} {i}" for l in range(1, 6) for n in ("X", "D", "DT") if (n, l) != ("D", 5) for i in range(4)]
         + [f"Wb B {i}" for i in range(4)]
         + [f"A AkT {i}" for i in range(4)]
         + ["A GT 0", "A GT 1", "A W 0", "A W 1", "A U0 0", "A U0 1"]
         + ["A S 0", "A U 1 0", "A U 1 1", "A S 1", "A U 2 0", "A U 2 1", "A S 2", "A U 3 0", "A U 3 1"]
         + [f"A RbT {i}" for i in range(4)] + [f"A RkT {i}" for i in range(4)]
         + ["A Y 0", "A Y 1", "A Y 2", "A Y 3", "A yT 0", "A yT 1"]
         + [f"Wb A {i}" for i in range(4)] + [f"mix {i}" for i in range(4)]
         + ["bias", "ada rows 4", "ada rows 5", "ada 4", "ada 5", "gate8"] + [f"x1 {i}" for i in range(4)] + ["gateB 0", "gateB 1"]
         + ["logits", "pT", "ple 0", "ple 1", "gateT", "rank", "ple 2", "ple 3"] + [f"pp {i}" for i in range(4)]
         + [f"h {i}" for i in range(4)]
         + [f"{n} {h}" + s_ for h in range(HEADS) for n, s_ in (("T", " 0"), ("T", " 1"), ("T", " 2"), ("O", ""))]
         + ["aT 0", "aT 1", "pool 0", "pool 1"]
         + [f"{n} {i}" for n in ("Wb2a", "Wb2p", "mix2") for i in range(4)])

ARENA = 53200
UNIT = 4096
RING = ARENA - 6 * UNIT
HIGH = RING + 3 * UNIT


def unit_no(name):
    return UNITS.index(name)


def unit2_no(name):
    return UNITS2.index(name)


def proj_no(name):
    return PROJ.index(name)


def small_no(name):
    return SMALL.index(name)


def build(nc, ins, consts, outs):
    stack = ExitStack()
    with stack:
        arena = stack.enter_context(nc.sbuf_tensor("arena", [P, ARENA], F32))
        proj_bank = [stack.enter_context(nc.psum_tensor(f"proj{i}", [P, 512], F32)) for i in range(4)]
        small_bank = [stack.enter_context(nc.psum_tensor(f"small{i}", [P, 512], F32)) for i in range(4)]
        scratch = nc.dram_tensor("bias_rows", (P, 24, BKT), F32).ap()
        signals = {}

        def sig(name):
            if name not in signals:
                signals[name] = stack.enter_context(nc.semaphore(name.replace(" ", "_")))
            return signals[name]

        def room(at, *shape):
            n = int(np.prod(shape))
            v = arena[:, at:at + n]
            if len(shape) == 2:
                v = v.rearrange("p (a b) -> p a b", b=shape[1])
            if len(shape) == 3:
                v = v.rearrange("p (a b c) -> p a b c", b=shape[1], c=shape[2])
            return v

        def over(v, n):
            return v.unsqueeze(len(v.shape)).to_broadcast(list(v.shape) + [n])

        def along(v, n):
            return v.unsqueeze(1).to_broadcast([v.shape[0], n, v.shape[1]])

        at = 0
        CO = room(at, NCONST); at += NCONST
        PV = room(at, P); at += P
        XTOK = room(at, TT, D); at += TT * D
        XT = room(at, KD, T); at += KD * T
        MERGED = room(at, KD, T); at += KD * T
        SG = room(at, KD, T)
        PROW = room(at, P)
        at += KD * T
        YT = {}
        for n in "DCBA":
            YT[n] = room(at, KW, T); at += KW * T
        WA2 = room(at - 1024, W)
        G2 = room(at - 512, W)
        LOW = at
        assert LOW + 11790 <= RING, (LOW, RING)

        def c(name, lo=0, hi=None):
            a, n = CONST[name]
            return CO[:, a + lo:a + (n if hi is None else hi)]

        def pv(name, lo=0, hi=None):
            a, n = VEC[name]
            return PV[:, a + lo:a + (n if hi is None else hi)]

        ident = c("ident")

        at = HIGH
        xr = room(at, KW, T + 3); at += KW * (T + 3)
        lgate = room(at, KW, T); at += 1024
        xc = room(at, KW, T); at += 1024
        gx = room(at, KW, T); at += 1024
        ga = room(at, KW, T); at += 1024
        lt1 = room(at, KW, T); at += 1024
        lt2 = room(at, KW, T); at += 1024
        WX = room(at, KW, P); at += 512
        WAD = room(at, KW, P); at += 512
        lam = room(at, 5, 4); at += 20
        assert at <= HIGH + 3 * UNIT

        at = LOW
        cz = room(at, 8, T + 3); hC = room(at, 8, P); hC2 = room(at + 1024, 8, P); at += 8 * (T + 3)
        qk = room(at, 8, T); at += 2048
        vC = room(at, TT, W); at += 1024
        oC = room(at, KW, T); at += 1024
        wC = room(at, 4, 384); at += 1536
        sC = room(at, 4, 384); at += 1536
        rows = room(at, 8, T); at += 2048
        iC, fC, uC, gC, mC = (rows[0:4, n, :] for n in range(5))
        e1C, e2C = rows[0:4, 5, :], rows[0:4, 6, :]
        colC = room(at, 2, 8); at += 16
        emC = room(at, 8); at += 8
        denC = room(at, 8); at += 8
        stC = room(at, 4, 8); at += 32
        ifb = room(at, 2); at += 2
        assert at <= RING

        at = HIGH
        qB = room(at, KW, T); at += 1024
        fB = room(at, KW, T); at += 1024
        vB = room(at, TT, W); at += 1024
        gB = room(at, KW, T); at += 1024
        kB = room(at, KW, T); at += 1024
        cB = room(at, KW, T); at += 1024
        eBs = [room(at, KW, T), room(at + 1024, KW, T)]; at += 2048
        eB = eBs[1]
        aB = room(at, 8, P); at += 1024
        aX = room(at, 4, P); at += 512
        tB = room(at, KW, T); at += 1024
        tB2 = room(at, KW, T); at += 1024
        stB = room(at, 2, 8); at += 16
        assert at <= HIGH + 3 * UNIT

        at = LOW
        zA = room(at, 14, T + 1); zmix = zA[:, :, 1:T + 1]; at += 14 * (T + 1)
        dA = room(at, 14, T)
        sl = [at + 1024 * i for i in range(8)]
        NTm = room(sl[0], 16, P)
        cumA, aA, kkA, bA, gA, bonusA, e1A, e2A = (room(s, KW, T) for s in sl)
        rA, kA, vA = zmix[:, 0:4], zmix[:, 4:8], zmix[:, 8:12]
        assert sl[7] + 1024 <= RING
        S_all = room(LOW + 8 * (T + 1), 4, 256)
        e3A = aA
        at = HIGH
        Vt = room(at, TT, W); At = room(at + 1024, TT, W)
        Bt = room(at + 2048, TT, W); Kt = room(at + 3072, TT, W); at += 4096
        DTa = room(at, 16, P); at += 2048
        NT = room(at, 16, P); AkT = NT; at += 2048
        X = room(at, 16, P); WU = room(at, TT, W); Ut = room(at + 1024, TT, W); at += 2048
        Da = room(at, 16, P); RbT = Da; at += 2048
        RkT = NTm
        GT = room(sl[7], KW, T)
        Ysum = room(sl[2], TT * 8, CH)
        Ysq = room(sl[3], TT * 8, CH)
        stA = room(LOW + 12 * (T + 1), 3, 16)

        x1 = XTOK
        mixv = room(HIGH, TT, D)
        bcg = room(HIGH + 2048, D)
        bcb = room(HIGH + 3072, D)
        st1 = room(HIGH + 4096, 2, 12)
        mv1 = room(HIGH + 4096 + 24, 2, 2)
        rs1 = room(HIGH + 4096 + 28, 2)

        base = MERGED.rearrange("p k t -> p (k t)").rearrange("p (j d) -> p j d", j=TT)
        at = LOW
        YSB = room(at, W); at += W
        ESEL = room(at, CAP); at += CAP
        RW = room(at, KD, EXPERTS); at += KD * EXPERTS
        RB = room(at, EXPERTS); at += EXPERTS
        (lg, above, tie, cum, ex, sel, gates_, rank) = (room(at + 64 * n, TT, EXPERTS) for n in range(8)); at += 8 * 64
        mx8 = room(at, TT, 8); at += 16
        n_above, n_ties, gate_sum, gate_scale = (room(at + TT * n, TT) for n in range(4)); at += 4 * TT
        top = room(at, 4); at += 4
        total = room(at, 1).bitcast(I32); at += 4
        BD = room(at, D)[0:EXPERTS]; at += D
        GTT = room(at, T)[0:EXPERTS]; at += T
        BGU = room(at, GU); at += GU
        PTOK = room(at, TT, T); at += TT * T
        PTT = room(at, TT, T); at += TT * T
        PG = room(at, TT, D)
        ln2g, ln2b = room(at, D), room(at + D, D); at += TT * D
        XG = room(at, 8, CAP); at += 512
        PICK = room(at, TT, CAP); at += TT * CAP
        PICKW = room(at, TT, P); at += TT * P
        PTW = room(at, T); at += T
        GH = room(at, W); at += W
        UH = room(at, W); at += W
        SGH = room(at, W); at += W
        assert at <= RING, (at, RING)
        HM = PTOK.rearrange("p j d -> p (j d)").rearrange("p (m s c) -> p m s c", m=4, s=2)
        gate_bank, up_bank, y_bank, x_bank = small_bank
        acc_bank = proj_bank
        slots = [3, 4, 5, 0, 1, 2]

        at = LOW - 4 * 1024
        PROW2 = room(at, P); at += P
        PV2 = room(at, 40); at += 40
        MODT = room(at, 24); at += 24
        G8 = room(at, P)[0:8]; at += P
        RELB = room(at, 24)[0:32]; at += 24
        HOT = room(at, BKT)[0:32]; at += BKT
        CB = room(at, KD, 32); at += KD * 32
        SEL = room(at, 1); at += 1
        assert at <= LOW - 3 * 1024
        BM = room(at, BKT)[0:24]; at += BKT
        TAB = room(at, BKT)[0:24]; at += BKT
        assert at <= LOW - 2 * 1024
        st2 = room(at, 2, 12); mv2 = room(at + 24, 2, 2); rs2 = room(at + 28, 2); ss2 = room(at + 30, 2)
        rs3 = room(at + 32, 2); ss3 = room(at + 34, 2)
        mod_a = room(at + 36, 8); den = room(at + 44, 2, 4); nmax = room(at + 52, 2, 4)
        gateB = room(LOW - 2 * 1024 + 64, D)
        ADAROW = [room(HIGH + 8192, 2, W)] * 4 + [gateB.rearrange("p (a b) -> p a b", b=W)] * 2
        assert at + 60 <= LOW - 2 * 1024 + 64

        x2 = XTOK
        HT = XT
        at = LOW
        qT, kT, vK = [], [], []
        for g in range(GROUPS):
            qT.append(room(at, KW, T)); kT.append(room(at + 1024, KW, T)); vK.append(room(at + 2048, TT, W)); at += 3072
        u0 = room(at, 4, T + 16); at += 4 * (T + 16)
        zp = room(at, KW, T); at += 1024
        assert at <= RING
        at = HIGH
        HK = room(at, 24, T); at += 24 * T
        PB = [room(at, 1152), room(at + 1152, 1152)]; at += 2304
        PTr = room(at, 1152); at += 1152
        attn = room(at, TT, W); at += 1024
        zat = room(at, TT, W); at += 1024
        assert at <= HIGH + 3 * UNIT
        uA, uB = room(HIGH, 4, T + 16), room(HIGH + 1088, 4, T + 16)
        pooled = room(HIGH + 2176, KW, T)
        attnT = room(HIGH + 3200, KW, T)
        poolT = room(HIGH + 4224, KW, T)
        POOLW = room(HIGH + 5248, 4, P)
        zsig = room(HIGH + 6144, TT, W)
        zpsig = room(HIGH + 7168, KW, T)
        x3 = room(LOW, TT, D)
        MERGED2 = MERGED
        fing = room(LOW + 2048, D)
        squares = SG.rearrange("p k t -> p (k t)").rearrange("p (j d) -> p j d", j=TT)

        def mat(j, h):
            return 8 * j + 4 * (h % 2) + h // 2

        def ring(n):
            return RING + (n % 3) * UNIT

        w_in = ins["w_in_first"]

        def unit_source(name):
            col = {"D xr": D_COL, "D gate": D_COL + W, "C q": C_COL, "C k": C_COL + W, "C v": C_COL + 2 * W,
                   "C o": C_COL + 3 * W, "B q": B_COL, "B f": B_COL + W, "B i": B_COL + 2 * W, "B g": B_COL + 3 * W,
                   "A r": 0, "A k": W, "A v": 2 * W}
            for n, b in enumerate("ABCD"):
                col[f"G {b} 0"] = G_COL + n * D
                col[f"G {b} 1"] = G_COL + n * D + W
            if name in col:
                return w_in[:, col[name]:col[name] + W].rearrange("(k p) n -> p k n", p=P), (KD, W)
            if name == "C if":
                return w_in[:, C_COL + 4 * W:C_COL + 4 * W + 8].rearrange("(k p) n -> p k n", p=P), (KD, 8)
            if name == "A x":
                return w_in[:, 3 * W:3 * W + 256].rearrange("(k p) n -> p k n", p=P), (KD, 256)
            if name.startswith("Wb"):
                return ins["w_branch"][0, "ABCD".index(name[-1])].rearrange("(k p) n -> p k n", p=P), (KW, D)
            half = int(name[-1]) if name != "pp" else 0
            if name.startswith("ada"):
                return ins["w_ada_2"][0, :, half * W:half * W + W].rearrange("(k p) n -> p k n", p=P), (KD, W)
            if name.startswith("ple"):
                return ins["ple_gate_w"][0, :, half * W:half * W + W].rearrange("(k p) n -> p k n", p=P), (KD, W)
            if name == "pp":
                return ins["ple_proj_w"][0].rearrange("(k p) n -> p k n", p=P), (TT, D)
            return ins["w_out"][0, :, half * W:half * W + W].rearrange("(k p) n -> p k n", p=P), (KD, W)

        def weights(name):
            return room(ring(unit_no(name)), *unit_source(name)[1])

        def unit2_source(name):
            if name.startswith("Wb2"):
                src = ins["w_attn_br_2" if name[-1] == "a" else "w_pool_br_2"][0]
                return src.rearrange("(k p) n -> p k n", p=P), (KW, D)
            if name.startswith("out2"):
                half = int(name[-1])
                return ins["w_out_2"][0, :, half * W:half * W + W].rearrange("(k p) n -> p k n", p=P), (KD, W)
            return ins["w_in_2"][0, :, COL2[name]:COL2[name] + W].rearrange("(k p) n -> p k n", p=P), (KD, W)

        def weights2(name):
            return room(ring(unit2_no(name)), *unit2_source(name)[1])

        def unit2_used(name):
            if name.startswith("Wb2"):
                return sig("small_full"), small_no(f"{name} 3") + 1
            if name.startswith("out2"):
                return sig("small_full"), small_no(f"mix2 {2 * int(name[-1]) + 1}") + 1
            if name.startswith("g2"):
                return sig("proj_full"), proj_no(f"{name[:-1]}{2 * int(name[-1]) + 1}") + 1
            return sig("proj_full"), proj_no(f"{name} 1") + 1

        def expert_unit(e, u):
            if u < 4:
                src = ins["expert_w_gu"][0, bass.ds(e, 1), u * 2 * P:(u + 1) * 2 * P, :]
                return src.rearrange("e (k p) n -> p (e k) n", p=P), (2, GU)
            src = ins["expert_w_down"][0, bass.ds(e, 1), (u - 4) * 4 * P:(u - 3) * 4 * P, :]
            return src.rearrange("e (k p) n -> p (e k) n", p=P), (4, D)

        def expert_room(u):
            return room(RING + slots[u] * UNIT, *expert_unit(0, u)[1])

        def unit_used(name):
            if name.startswith("Wb"):
                return sig("small_full"), small_no(f"{name} 3") + 1
            if name.startswith("out"):
                return sig("small_full"), small_no(f"mix {2 * int(name[-1]) + 1}") + 1
            if name.startswith("ada"):
                return sig("small_full"), small_no(name) + 1
            if name.startswith("ple"):
                return sig("small_full"), small_no(f"ple {2 * int(name[-1]) + 1}") + 1
            if name == "pp":
                return sig("small_full"), small_no("pp 3") + 1
            if name in ("C if", "A x"):
                return sig("proj_full"), proj_no(name) + 1
            if name.startswith("G"):
                return sig("proj_full"), proj_no(f"{name[:-1]}{2 * int(name[-1]) + 1}") + 1
            return sig("proj_full"), proj_no(f"{name} 1") + 1

        block = stack.enter_context(nc.Block())

        @block.sync
        def _(sp):
            sp.dma_start(XTOK, ins["x"][0].rearrange("(j p) d -> p j d", p=P)).then_inc(sig("x_loaded"), 16)
            for n, name in enumerate(UNITS):
                if n >= 3:
                    sp.wait_ge(*unit_used(UNITS[n - 3]))
                src, _ = unit_source(name)
                sp.dma_start(weights(name), src).then_inc(sig(f"unit_in_{n % 3}"), 16)
                if n == 0:
                    sp.dma_start(CO[:, P:], consts["consts"][:, P:]).then_inc(sig("const_loaded"), 16)
            sp.wait_ge(sig("x1_done"), 2)
            sp.wait_ge(*unit_used("pp"))
            for u in range(6):
                sp.dma_start(expert_room(u), expert_unit(0, u)[0]).then_inc(sig(f"expert_in_{u}"), 16)
            sp.wait_ge(sig("total_ready"), 1)
            n_steps = sp.value_load(total[0:1, 0:1], min_val=EXPERTS, max_val=EXPERTS * T // CAP)
            with sp.Fori(1, n_steps) as i:
                for u in range(6):
                    if u < 4:
                        sp.wait_ge(sig("gu_used"), 4 * i + (u - 3))
                    elif u == 4:
                        sp.wait_ge(sig("down_used"), i)
                    else:
                        sp.wait_ge(sig("y_full"), i)
                    sp.dma_start(expert_room(u), expert_unit(i % EXPERTS, u)[0]).then_inc(sig(f"expert_in_{u}"), 16)
            sp.wait_ge(sig("experts_done"), 1)
            for n, name in enumerate(UNITS2):
                if n >= 3:
                    sp.wait_ge(*unit2_used(UNITS2[n - 3]))
                if n == 3:
                    sp.wait_ge(sig("table_stored"), 16)
                    tab = bass.AP(tensor=scratch.tensor, offset=P - 1, ap=[[24 * BKT - 1, P], [BKT, 24], [1, T]])
                    sp.dma_start(HK, tab).then_inc(sig("hankel_loaded"), 16)
                sp.dma_start(weights2(name), unit2_source(name)[0]).then_inc(sig(f"unit2_in_{n % 3}"), 16)
            for j in range(TT):
                sp.wait_ge(sig("final"), j + 1)
                sp.dma_start(outs[0][0, j * P:(j + 1) * P, :], x3[:, j, :]).then_inc(sig("stored"), 16)
            sp.wait_ge(sig("stored"), 16 * TT)

        @block.gpsimd
        def _(pool):
            pool.dma_start(ifb[0:4, 0:1], ins["mlstm_i_bias"].rearrange("a b -> b a")).then_inc(sig("ifb_loaded"), 16)
            pool.dma_start(ifb[0:4, 1:2], ins["mlstm_f_bias"].rearrange("a b -> b a")).then_inc(sig("ifb_loaded"), 16)
            pool.memset(WX, 0.0).then_inc(sig("wx_zero"), 1)
            pool.memset(WAD, 0.0).then_inc(sig("wx_zero"), 1)
            pool.wait_ge(sig("wx_zero"), 2)
            for t_, name in ((WX, "lru_wx"), (WAD, "lru_wa")):
                for odd in range(2):
                    pool.dma_start(t_[64 * odd:64 * odd + 64, :, 64 * odd:64 * odd + 64],
                                   ins[name][0, odd::2].rearrange("g i j -> i g j")).then_inc(sig("wx_loaded"), 16)
            pool.dma_start(WA2[0:64, :], ins["rwkv_w2"][0]).then_inc(sig("w2_loaded"), 16)
            pool.dma_start(WA2[64:128, :], ins["rwkv_a2"][0]).then_inc(sig("w2_loaded"), 16)
            pool.dma_start(G2, ins["rwkv_g2"][0]).then_inc(sig("w2_loaded"), 16)
            pool.wait_ge(sig("merged"), 1)
            for n, (lo, src) in enumerate(((0, ins["c_2"][0]), (8, ins["norm_g_2"][0]), (16, ins["b_ada_2"][0]))):
                cnt = 24 if n == 2 else 8
                pool.dma_start(PROW2[lo:lo + cnt, :], src.rearrange("(a b) -> a b", b=P)).then_inc(sig("prow2_loaded"), 16)
            for l in range(6):
                if l == 0:
                    pool.wait_ge(sig("small_out"), small_no("A NT 3") + 1)
                elif l == 1:
                    pool.wait_ge(sig("small_out"), small_no("A X0 3") + 1)
                else:
                    pool.wait_ge(sig("small_full"), small_no(f"A X{l - 1} 3") + 1)
                pool.tensor_tensor(NTm, NT, along(c("level", l * P, l * P + P), 16), ALU.mult).then_inc(sig("NTm_ready"), 1)
            pool.wait_ge(sig("merged"), 2)
            for dst, src in ((RELB, ins["rel_bias_2"]), (HOT, consts["hot"]), (BM, consts["mask"])):
                pool.dma_start(dst, src).then_inc(sig("table_loaded"), 16)
            pool.wait_ge(sig("A_states_done"), 1)
            pool.wait_ge(sig("small_full"), small_no("A Y 3") + 1)
            pool.dma_start(bcg, ins["ln1_g"][0].partition_broadcast(P)).then_inc(sig("ln1_loaded"), 16)
            pool.dma_start(bcb, ins["ln1_b"][0].partition_broadcast(P)).then_inc(sig("ln1_loaded"), 16)
            pool.wait_ge(sig("merged"), 4)
            pool.memset(BGU, 0.0).then_inc(sig("bgu_zero"), 1)
            pool.wait_ge(sig("bgu_zero"), 1)
            for dst, src in ((RW, ins["router_w"][0].rearrange("(k p) e -> p k e", p=P)),
                             (RB, ins["router_b"][0].partition_broadcast(P)),
                             (BD, ins["expert_b_down"][0]), (BGU[0:EXPERTS], ins["expert_b_gu"][0]),
                             (PTOK, ins["p"][0, 0].rearrange("(j p) d -> p j d", p=P))):
                pool.dma_start(dst, src).then_inc(sig("router_loaded"), 16)
            pool.wait_ge(sig("base_done"), 1)
            pool.dma_start(ln2g, ins["ln2_g"][0].partition_broadcast(P)).then_inc(sig("ln2_loaded"), 16)
            pool.dma_start(ln2b, ins["ln2_b"][0].partition_broadcast(P)).then_inc(sig("ln2_loaded"), 16)
            pool.wait_ge(sig("small_full"), small_no("O 7") + 1)
            pool.dma_start(POOLW, ins["pool_w_2"][0].rearrange("g c e -> c g e")).then_inc(sig("poolw_loaded"), 16)
            pool.dma_start(fing, ins["final_g_2"].partition_broadcast(P)).then_inc(sig("fing_loaded"), 16)

        @block.tensor
        def _(pe):
            def unit(name):
                n = unit_no(name)
                pe.wait_ge(sig(f"unit_in_{n % 3}"), 16 * (n // 3 + 1))
                return weights(name)

            def proj(name):
                n = proj_no(name)
                if n >= 4:
                    pe.wait_ge(sig("proj_out"), n - 3)
                return proj_bank[n % 4]

            def small(name):
                n = small_no(name)
                if n >= 4:
                    pe.wait_ge(sig("small_out"), n - 3)
                return small_bank[n % 4]

            def by_channels(what, banks=(0, 1)):
                w = unit(what)
                for b in banks:
                    name = f"{what} {b}" if not what.startswith("G") else f"{what[:-1]}{int(what[-1]) * 2 + b}"
                    if what == "A x":
                        name = what
                    ps = proj(name)
                    for m in range(2):
                        for k in range(KD):
                            mm = pe.matmul(ps[:, m * T:m * T + T], w[:, k, (2 * b + m) * P:(2 * b + m + 1) * P],
                                           XT[:, k, :], start=k == 0, stop=k == KD - 1)
                    mm.then_inc(sig("proj_full"), 1)

            def by_tokens(what):
                w = unit(what)
                for j in range(TT):
                    ps = proj(f"{what} {j}")
                    for k in range(KD):
                        mm = pe.matmul(ps[:, :], XT[:, k, j * P:j * P + P], w[:, k, :], start=k == 0, stop=k == KD - 1)
                    mm.then_inc(sig("proj_full"), 1)

            def merge(b):
                pe.wait_ge(sig(f"{b}_done"), 1)
                w = unit(f"Wb {b}")
                for i in range(4):
                    ps = small(f"Wb {b} {i}")
                    for m in range(2):
                        for k in range(KW):
                            mm = pe.matmul(ps[:, m * T:m * T + T], w[:, k, (2 * i + m) * P:(2 * i + m + 1) * P],
                                           YT[b][:, k, :], start=k == 0, stop=k == KW - 1)
                    mm.then_inc(sig("small_full"), 1)

            pe.wait_ge(sig("ident_loaded"), 16)
            pe.wait_ge(sig("x_loaded"), 16)
            for g in range(4):
                ps = small(f"x {g}")
                for k in range(2):
                    for j in range(TT):
                        mm = pe.transpose(ps[:, k * T + j * P:k * T + j * P + P], XTOK[:, j, (2 * g + k) * P:(2 * g + k + 1) * P], ident)
                mm.then_inc(sig("small_full"), 1)
            pe.wait_ge(sig("small_out"), small_no("x 3") + 1)

            by_channels("D xr")
            by_channels("D gate")
            pe.wait_ge(sig("prow_loaded"), 16 * len(VEC))
            pe.transpose(small("vectors")[:, 0:NVEC], PROW[0:NVEC, :], ident[0:NVEC, 0:NVEC]).then_inc(sig("small_full"), 1)
            by_channels("C q")
            pe.wait_ge(sig("wx_loaded"), 64)
            pe.wait_ge(sig("D_conv"), 1)
            for nm, wt in (("gx", WX), ("ga", WAD)):
                for i in range(2):
                    ps = small(f"D {nm} {i}")
                    for m in range(2):
                        mm = pe.matmul(ps[:, m * T:m * T + T], wt[:, 2 * i + m, :], xc[:, 2 * i + m, :], start=True, stop=True)
                    mm.then_inc(sig("small_full"), 1)
            by_channels("C k")
            w = unit("C if")
            ps = proj("C if")
            for m in range(2):
                for k in range(KD):
                    mm = pe.matmul(ps[0:4, m * T:m * T + T], w[:, k, 4 * m:4 * m + 4], XT[:, k, :], start=k == 0, stop=k == KD - 1)
            mm.then_inc(sig("proj_full"), 1)

            by_tokens("C v")
            by_channels("C o")
            by_channels("B q")
            pe.wait_ge(sig("const_loaded"), 16)
            pe.wait_ge(sig("C_rows"), 1)
            for i in range(2):
                ps = small(f"C row {i}")
                for m in range(2):
                    mm = pe.matmul(ps[:, m * T:m * T + T], c("headrow", (2 * i + m) * P, (2 * i + m + 1) * P)[0:4, :], gC, start=True, stop=True)
                mm.then_inc(sig("small_full"), 1)
            ps = small("C col")
            for n, r in enumerate((uC, mC)):
                for j in range(TT):
                    mm = pe.transpose(ps[:, 8 * n + 4 * j:8 * n + 4 * j + 4], r[:, j * P:j * P + P], ident[0:4, 0:4])
            mm.then_inc(sig("small_full"), 1)
            by_channels("B f")
            pe.wait_ge(sig("C_qk"), 1)
            for h in range(4):
                ps = small(f"C S {h}")
                pe.matmul(ps[:, 0:T], qk[:, 4 + h, 0:P], qk[:, h, :], start=True, stop=True)
                pe.matmul(ps[:, T:T + P], qk[:, 4 + h, P:T], qk[:, h, P:T], start=True, stop=True).then_inc(sig("small_full"), 1)
            by_tokens("B i")
            by_channels("B g")

            pe.wait_ge(sig("C_weights"), 1)
            pe.wait_ge(sig("proj_out"), proj_no("C v 1") + 1)
            for j in range(TT):
                ps = small(f"C num {j}")
                for h in range(4):
                    if j == 0:
                        mm = pe.matmul(ps[:, h * P:h * P + P], sC[:, h, 0:P], vC[:, 0, h * P:h * P + P], start=True, stop=True)
                    else:
                        pe.matmul(ps[:, h * P:h * P + P], sC[:, h, P:T], vC[:, 0, h * P:h * P + P], start=True, stop=False)
                        mm = pe.matmul(ps[:, h * P:h * P + P], sC[:, h, T:T + P], vC[:, 1, h * P:h * P + P], start=False, stop=True)
                mm.then_inc(sig("small_full"), 1)
            ps = small("C den")
            for h in range(4):
                pe.matmul(ps[:, h:h + 1], sC[:, h, 0:P], c("ones", 0, 1), start=True, stop=True)
                pe.matmul(ps[:, 4 + h:5 + h], sC[:, h, P:T], c("ones", 0, 1), start=True, stop=False)
                mm = pe.matmul(ps[:, 4 + h:5 + h], sC[:, h, T:T + P], c("ones", 0, 1), start=False, stop=True)
            mm.then_inc(sig("small_full"), 1)

            by_channels("G D 0")
            by_channels("G D 1")
            def turned(b, src, done):
                pe.wait_ge(sig(done), 1)
                for i in range(2):
                    ps = small(f"{b} {i}")
                    for m in range(2):
                        for j in range(TT):
                            mm = pe.transpose(ps[:, m * T + j * P:m * T + j * P + P], src[:, j, (2 * i + m) * P:(2 * i + m + 1) * P], ident)
                    mm.then_inc(sig("small_full"), 1)

            turned("C yT", hC.rearrange("p (j h) e -> p j (h e)", j=TT), "C_normed")
            merge("D")

            pe.wait_ge(sig("B_qk"), 1)
            for j in range(TT):
                ps = small(f"B diag {j}")
                for h in range(4):
                    mm = pe.matmul(ps[:, h * P:h * P + P], kB[:, h, j * P:j * P + P], qB[:, h, j * P:j * P + P], start=True, stop=True)
                mm.then_inc(sig("small_full"), 1)
            fill = [(x, (b,)) for x in ("A r", "A k", "A v") for b in range(2)] + [("A x", (0,))]
            for l in range(8):
                pe.wait_ge(sig("B_level"), l + 1)
                if l < 7:
                    for j in range(TT):
                        ps = small(f"B level {l} {j}")
                        for h in range(4):
                            e = eBs[l % 2][:, h, j * P:j * P + P]
                            mm = pe.matmul(ps[:, h * P:h * P + P], e, e, start=True, stop=True)
                        mm.then_inc(sig("small_full"), 1)
                else:
                    ps = small("B cross")
                    for h in range(4):
                        mm = pe.matmul(ps[:, h * P:h * P + P], eBs[1][:, h, 0:P], eBs[1][:, h, P:T], start=True, stop=True)
                    mm.then_inc(sig("small_full"), 1)
                if l < 7:
                    by_channels(*fill[l])
            pe.wait_ge(sig("proj_out"), proj_no("B i 1") + 1)
            pe.wait_ge(sig("small_out"), small_no("B cross") + 1)
            for j in range(TT):
                ps = small(f"B o {j}")
                for h in range(4):
                    mm = pe.matmul(ps[:, h * P:h * P + P], aB[:, 4 * j + h, :], vB[:, j, h * P:h * P + P], start=True, stop=j == 0)
                    if j == 1:
                        mm = pe.matmul(ps[:, h * P:h * P + P], aX[:, h, :], vB[:, 0, h * P:h * P + P], start=False, stop=True)
                mm.then_inc(sig("small_full"), 1)
            by_channels("G C 0")
            pe.wait_ge(sig("prow2_loaded"), 48)
            pe.transpose(small("vectors2")[:, 0:40], PROW2[0:40, :], ident[0:40, 0:40]).then_inc(sig("small_full"), 1)
            pe.wait_ge(sig("w2_loaded"), 48)
            pe.wait_ge(sig("A_tanh"), 1)
            for nm, lo, hi, wt in (("w", 0, 64, WA2), ("a", 64, 128, WA2), ("g", 0, 128, G2)):
                for i in range(2):
                    ps = small(f"A {nm} {i}")
                    for m in range(2):
                        rhs = zmix[lo:hi, 13 if nm == "g" else 12, :]
                        mm = pe.matmul(ps[:, m * T:m * T + T], wt[lo:hi, (2 * i + m) * P:(2 * i + m + 1) * P], rhs, start=True, stop=True)
                    mm.then_inc(sig("small_full"), 1)
            pe.wait_ge(sig("A_kksq"), 1)
            for i in range(2):
                ps = small(f"A kk {i}")
                pe.matmul(ps[:, :], c("headsum"), bA[:, 2 * i:2 * i + 2, :], start=True, stop=True).then_inc(sig("small_full"), 1)
            turned("B yT", tB2.rearrange("p a b -> p (a b)").rearrange("p (j n) -> p j n", j=TT), "B_normed")

            def to_tokens(name, src):
                for i in range(2):
                    ps = small(f"A {name} {i}")
                    for m in range(4):
                        mm = pe.transpose(ps[:, m * P:m * P + P], src[:, m, i * P:i * P + P], ident)
                    mm.then_inc(sig("small_full"), 1)

            pe.wait_ge(sig("A_mixed"), 1)
            to_tokens("V", vA)
            by_channels("G C 1")

            def ada_rows(i):
                w = unit(f"ada {i}")
                ps = small(f"ada rows {i}")
                for k in range(KD):
                    g = k % 4
                    mm = pe.matmul(ps[32 * g:32 * g + 32, :], CB[:, k, :], w[:, k, :], start=k < 4, stop=k >= 4, skip_group_check=True)
                mm.then_inc(sig("small_full"), 1)

            def ada(i):
                pe.wait_ge(sig("small_out"), small_no(f"ada rows {i}") + 1)
                ps = small(f"ada {i}")
                for m in range(4):
                    mm = pe.matmul(ps[:, m:m + 1], ADAROW[i][:, i % 2, m * P:m * P + P], SEL, start=True, stop=True)
                mm.then_inc(sig("small_full"), 1)

            pe.wait_ge(sig("cond_ready"), 1)
            ada_rows(0)
            pe.wait_ge(sig("A_rk"), 1)
            for i in range(2):
                ps = small(f"A bonus {i}")
                pe.matmul(ps[:, :], c("headsum"), bonusA[:, 2 * i:2 * i + 2, :], start=True, stop=True).then_inc(sig("small_full"), 1)
            ada(0)
            ada_rows(1)
            for n, (name, src) in enumerate((("At", kkA), ("Bt", bA), ("Kt", kA))):
                pe.wait_ge(sig("A_tilde"), n + 1)
                to_tokens(name, src)
            ada(1)
            ada_rows(2)

            def head(v, h, lo, hi):
                return v[64 * (h % 2):64 * (h % 2) + 64, h // 2, lo:hi]

            def pairs(name, lhs, rhs):
                for i in range(4):
                    ps = small(f"A {name} {i}")
                    for m in range(4):
                        j, h = i // 2, 2 * m + i % 2
                        mm = pe.matmul(ps[:, m * P:m * P + P], head(lhs, h, j * P, j * P + P), head(rhs, h, j * P, j * P + P), start=True, stop=True)
                    mm.then_inc(sig("small_full"), 1)

            def products(name, lhs, rhs):
                for i in range(4):
                    ps = small(f"A {name} {i}")
                    for m in range(4):
                        n = 4 * i + m
                        mm = pe.matmul(ps[:, m * P:m * P + P], lhs[:, n, :], rhs[:, n, :], start=True, stop=True)
                    mm.then_inc(sig("small_full"), 1)

            pairs("NT", bA, kkA)
            ada(2)
            ada_rows(3)
            pe.wait_ge(sig("NTm_ready"), 1)
            for i in range(4):
                ps = small(f"A X0 {i}")
                for m in range(4):
                    mm = pe.transpose(ps[:, m * P:m * P + P], NTm[:, 4 * i + m, :], ident)
                mm.then_inc(sig("small_full"), 1)
            ada(3)
            merge("C")
            fill = {1: "G B 0", 2: "G B 1", 3: "Wb B", 4: "G A 0"}
            for l in range(1, 6):
                pe.wait_ge(sig("NTm_ready"), l + 1)
                pe.wait_ge(sig("small_out"), (small_no("A X0 3") if l == 1 else small_no(f"A DT{l - 1} 3")) + 1)
                products(f"X{l}", NTm, Da)
                if l in (1, 2):
                    by_channels(fill[l])
                pe.wait_ge(sig("small_out"), small_no(f"A X{l} 3") + 1)
                if l < 5:
                    products(f"D{l}", DTa, X)
                products(f"DT{l}", X, DTa)
            merge("B")
            pairs("AkT", kA, kkA)
            by_channels("G A 0")
            pe.wait_ge(sig("small_out"), small_no("A AkT 3") + 1)
            for j in range(TT):
                ps = small(f"A GT {j}")
                for h in range(8):
                    mm = pe.matmul(ps[64 * (h % 2):64 * (h % 2) + 64, (h // 2) * P:(h // 2 + 1) * P], At[:, j, h * CH:h * CH + CH], DTa[:, mat(j, h), :], start=True, stop=True)
                mm.then_inc(sig("small_full"), 1)
            for j in range(TT):
                ps = small(f"A W {j}")
                for h in range(8):
                    mm = pe.matmul(ps[:, h * CH:h * CH + CH], AkT[:, mat(j, h), :], Vt[:, j, h * CH:h * CH + CH], start=True, stop=True)
                mm.then_inc(sig("small_full"), 1)
            pe.wait_ge(sig("small_out"), small_no("A W 1") + 1)
            for j in range(TT):
                ps = small(f"A U0 {j}")
                for h in range(8):
                    mm = pe.matmul(ps[:, h * CH:h * CH + CH], DTa[:, mat(j, h), :], WU[:, j, h * CH:h * CH + CH], start=True, stop=True)
                mm.then_inc(sig("small_full"), 1)
            for ch in range(4):
                j, po = ch // 2, 64 * (ch % 2)
                if ch > 0:
                    pe.wait_ge(sig("A_state"), ch)
                    for h in (0, 2, 4, 6, 1, 3, 5, 7):
                        ho = 64 * (h % 2)
                        if h < 2:
                            ps = small(f"A U {ch} {h}")
                        mm = pe.matmul(ps[po:po + 64, (h // 2) * CH:(h // 2 + 1) * CH], GT[ho:ho + 64, h // 2, ch * CH:ch * CH + CH],
                                       S_all[ho:ho + 64, ch, (h // 2) * CH:(h // 2 + 1) * CH], start=True, stop=True)
                        if h > 5:
                            mm.then_inc(sig("small_full"), 1)
                if ch < 3:
                    pe.wait_ge(sig("A_u"), ch + 1)
                    ps = small(f"A S {ch}")
                    for h in range(8):
                        ho = 64 * (h % 2)
                        o = ps[ho:ho + 64, (h // 2) * CH:(h // 2 + 1) * CH]
                        pe.matmul(o, Bt[po:po + 64, j, h * CH:h * CH + CH], Ut[po:po + 64, j, h * CH:h * CH + CH], start=True, stop=False)
                        mm = pe.matmul(o, Kt[po:po + 64, j, h * CH:h * CH + CH], Vt[po:po + 64, j, h * CH:h * CH + CH], start=False, stop=True)
                    mm.then_inc(sig("small_full"), 1)
            pe.wait_ge(sig("A_u"), 4)
            pairs("RbT", bA, rA)
            pairs("RkT", kA, rA)
            pe.wait_ge(sig("small_out"), small_no("A RkT 3") + 1)
            for i in range(4):
                j, odd = divmod(i, 2)
                ps = small(f"A Y {i}")
                for pair in range(4):
                    h = 2 * pair + odd
                    o = ps[:, pair * CH:pair * CH + CH]
                    pe.matmul(o, RbT[:, mat(j, h), :], Ut[:, j, h * CH:h * CH + CH], start=True, stop=False, skip_group_check=True)
                    mm = pe.matmul(o, RkT[:, mat(j, h), :], Vt[:, j, h * CH:h * CH + CH], start=False, stop=True, skip_group_check=True)
                    for cp in range(2):
                        ch = 2 * j + cp
                        if ch > 0:
                            mm = pe.matmul(ps[64 * cp:64 * cp + 64, pair * CH:pair * CH + CH], head(rA, h, ch * CH, ch * CH + CH),
                                           S_all[64 * odd:64 * odd + 64, ch, pair * CH:pair * CH + CH], start=False, stop=True,
                                           skip_group_check=True)
                mm.then_inc(sig("small_full"), 1)
            by_channels("G A 1")
            turned("A yT", Ysum.rearrange("p (j h) e -> p j (h e)", j=TT), "A_normed")
            merge("A")
            pe.wait_ge(sig("merged"), 4)
            for half in range(2):
                w = unit(f"out {half}")
                for j in range(TT):
                    ps = small(f"mix {2 * half + j}")
                    for k in range(KD):
                        mm = pe.matmul(ps[:, :], MERGED[:, k, j * P:j * P + P], w[:, k, :], start=k == 0, stop=k == KD - 1)
                    mm.then_inc(sig("small_full"), 1)

            pe.wait_ge(sig("table_loaded"), 48)
            pe.matmul(small("bias")[0:24, 0:BKT], RELB, HOT, start=True, stop=True).then_inc(sig("small_full"), 1)
            ada_rows(4)
            ada_rows(5)
            ada(4)
            ada(5)
            pe.wait_ge(sig("small_out"), small_no("ada 5") + 1)
            pe.transpose(small("gate8")[0:8, 0:P], MODT[:, 16:24], ident).then_inc(sig("small_full"), 1)
            pe.wait_ge(sig("x1_done"), 2)
            for g in range(4):
                ps = small(f"x1 {g}")
                for k in range(2):
                    for j in range(TT):
                        mm = pe.transpose(ps[:, k * T + j * P:k * T + j * P + P], x1[:, j, (2 * g + k) * P:(2 * g + k + 1) * P], ident)
                mm.then_inc(sig("small_full"), 1)
            pe.wait_ge(sig("small_out"), small_no("gate8") + 1)
            for i in range(2):
                ps = small(f"gateB {i}")
                for m in range(4):
                    k = 4 * i + m
                    mm = pe.matmul(ps[:, m * P:m * P + P], c("headrow", k * P, k * P + P)[0:8, :], G8, start=True, stop=True)
                mm.then_inc(sig("small_full"), 1)
            pe.wait_ge(sig("router_loaded"), 80)
            pe.wait_ge(sig("small_out"), small_no("x1 3") + 1)
            ps = small("logits")
            for j in range(TT):
                for k in range(KD):
                    mm = pe.matmul(ps[:, j * EXPERTS:(j + 1) * EXPERTS], XT[:, k, j * P:j * P + P], RW[:, k, :], start=k == 0, stop=k == KD - 1)
            mm.then_inc(sig("small_full"), 1)
            ps = small("pT")
            for k in range(2):
                for j in range(TT):
                    mm = pe.transpose(ps[:, k * T + j * P:k * T + j * P + P], PTOK[:, j, k * P:k * P + P], ident)
            mm.then_inc(sig("small_full"), 1)

            def embed(half):
                w = unit(f"ple {half}")
                for j in range(TT):
                    ps = small(f"ple {2 * half + j}")
                    for k in range(KD):
                        mm = pe.matmul(ps[:, :], XT[:, k, j * P:j * P + P], w[:, k, :], start=k == 0, stop=k == KD - 1)
                    mm.then_inc(sig("small_full"), 1)

            embed(0)
            pe.wait_ge(sig("gates_ready"), 1)
            ps = small("gateT")
            for j in range(TT):
                mm = pe.transpose(ps[0:EXPERTS, j * P:j * P + P], gates_[:, j, :], ident)
            mm.then_inc(sig("small_full"), 1)
            ps = small("rank")
            pe.matmul(ps[:, 0:32], c("strict"), sel[:, 0, :], start=True, stop=True)
            pe.matmul(ps[:, 32:64], c("ones", 0, P), sel[:, 0, :], start=True, stop=False)
            pe.matmul(ps[:, 32:64], c("strict"), sel[:, 1, :], start=False, stop=True)
            pe.matmul(ps[:, 64:96], c("ones", 0, P), sel[:, 0, :], start=True, stop=False)
            pe.matmul(ps[:, 64:96], c("ones", 0, P), sel[:, 1, :], start=False, stop=True).then_inc(sig("small_full"), 1)
            embed(1)
            w = unit("pp")
            for i in range(4):
                half, j = divmod(i, 2)
                ps = small(f"pp {i}")
                for k in range(2):
                    mm = pe.matmul(ps[:, :], PTT[:, k, j * P:j * P + P], w[:, k, half * W:half * W + W], start=k == 0, stop=k == 1)
                mm.then_inc(sig("small_full"), 1)

            pe.wait_ge(sig("proj_out"), proj_no("G A 3") + 1)
            pe.wait_ge(sig("small_out"), small_no("pp 3") + 1)
            for j in range(TT):
                for half in range(2):
                    pe.matmul(acc_bank[2 * j + half][:, :], GTT[:, j * P:j * P + P], BD[:, half * W:half * W + W], start=True, stop=False, skip_group_check=True)

            def gather():
                for k in range(KD):
                    for j in range(TT):
                        mm = pe.matmul(x_bank[:, k * CAP:(k + 1) * CAP], x1[:, j, k * P:k * P + P], PICK[:, j, :], start=j == 0, stop=j == 1)
                mm.then_inc(sig("gathered"), 1)

            def scatter():
                for j in range(TT):
                    for half in range(2):
                        lo = CAP * half
                        mm = pe.matmul(acc_bank[2 * j + half][:, :], PTW[lo:lo + CAP, j * P:j * P + P], YSB[lo:lo + CAP, :],
                                       start=False, stop=False, skip_group_check=True)
                return mm

            pe.wait_ge(sig("pick_ready"), 1)
            gather()
            pe.nop().then_inc(sig("ptw_full"), 1)
            pe.wait_ge(sig("total_ready"), 1)
            n_steps = pe.value_load(total[0:1, 0:1], min_val=EXPERTS, max_val=EXPERTS * T // CAP)
            with pe.Fori(0, n_steps) as i:
                pe.wait_ge(sig("xg_ready"), i + 1)
                for k in range(KD):
                    if k % 2 == 0:
                        pe.wait_ge(sig(f"expert_in_{k // 2}"), 16 * i + 16)
                        w = expert_room(k // 2)
                    for n, bank in enumerate((gate_bank, up_bank)):
                        for half in range(2):
                            mm = pe.matmul(bank[CAP * half:CAP * half + CAP, :], XG[:, k, :], w[:, k % 2, n * D + half * W:n * D + half * W + W],
                                           start=k == 0, stop=False, skip_group_check=True)
                    if k % 2:
                        mm.then_inc(sig("gu_used"), 1)
                pe.wait_ge(sig("esel_ready"), i + 1)
                for n, bank in enumerate((gate_bank, up_bank)):
                    for half in range(2):
                        mm = pe.matmul(bank[CAP * half:CAP * half + CAP, :], ESEL, BGU[:, n * D + half * W:n * D + half * W + W],
                                       start=False, stop=True, skip_group_check=True)
                mm.then_inc(sig("gu_full"), 1)
                pe.wait_ge(sig("y_ready"), i + 1)
                pe.wait_ge(sig("ptw_ready"), i + 1)
                scatter()
                pe.wait_ge(sig("pickw_ready"), i + 1)
                for j in range(TT):
                    mm = pe.transpose(y_bank[:, j * P:j * P + P], PICKW[:, j, :], ident)
                mm.then_inc(sig("ptw_full"), 1)
                pe.wait_ge(sig("pick_ready"), i + 2)
                gather()
                pe.wait_ge(sig("h_ready"), i + 1)
                for m in range(4):
                    mm = pe.transpose(gate_bank[:, m * P:m * P + P], GH[:, m * P:m * P + P], ident)
                mm.then_inc(sig("ht_full"), 1)
                pe.wait_ge(sig("ptw_ready"), i + 2)
                pe.wait_ge(sig("hm_ready"), i + 1)
                for u in range(2):
                    pe.wait_ge(sig(f"expert_in_{4 + u}"), 16 * i + 16)
                    w = expert_room(4 + u)
                    for m in range(4):
                        for half in range(2):
                            mm = pe.matmul(y_bank[CAP * half:CAP * half + CAP, :], HM[:, m, u, :], w[:, m, half * W:half * W + W],
                                           start=u == 0 and m == 0, stop=u == 1 and m == 3, skip_group_check=True)
                    if u == 0:
                        mm.then_inc(sig("down_used"), 1)
                mm.then_inc(sig("y_full"), 1)
            pe.wait_ge(sig("last_y_ready"), 1)
            scatter().then_inc(sig("experts_done"), 1)

            def unit2(name):
                n = unit2_no(name)
                pe.wait_ge(sig(f"unit2_in_{n % 3}"), 16 * (n // 3 + 1))
                return weights2(name)

            def channels2(what, banks=(0, 1)):
                w = unit2(what)
                for b in banks:
                    name = f"{what} {b}" if what[:2] != "g2" else f"{what[:-1]}{int(what[-1]) * 2 + b}"
                    ps = proj(name)
                    for m in range(2):
                        for k in range(KD):
                            mm = pe.matmul(ps[:, m * T:m * T + T], w[:, k, (2 * b + m) * P:(2 * b + m + 1) * P], HT[:, k, :],
                                           start=k == 0, stop=k == KD - 1)
                    mm.then_inc(sig("proj_full"), 1)

            def tokens2(what, tiles_=(0, 1)):
                w = unit2(what)
                for j in tiles_:
                    ps = proj(f"{what} {j}")
                    for k in range(KD):
                        mm = pe.matmul(ps[:, :], HT[:, k, j * P:j * P + P], w[:, k, :], start=k == 0, stop=k == KD - 1)
                    mm.then_inc(sig("proj_full"), 1)

            def merge2(what, y):
                w = unit2(what)
                for i in range(4):
                    ps = small(f"{what} {i}")
                    for m in range(2):
                        for k in range(KW):
                            mm = pe.matmul(ps[:, m * T:m * T + T], w[:, k, (2 * i + m) * P:(2 * i + m + 1) * P], y[:, k, :],
                                           start=k == 0, stop=k == KW - 1)
                    mm.then_inc(sig("small_full"), 1)

            pe.wait_ge(sig("acc_read"), 1)
            for g in range(4):
                ps, j = small(f"h {g}"), g // 2
                pe.wait_ge(sig("x2n_done"), j + 1)
                for m in range(4):
                    k = 4 * (g % 2) + m
                    mm = pe.transpose(ps[:, m * P:m * P + P], base[:, j, k * P:k * P + P], ident)
                mm.then_inc(sig("small_full"), 1)
            pe.wait_ge(sig("small_out"), small_no("h 3") + 1)
            for n in QKV:
                (tokens2 if n[0] == "V" else channels2)(n)

            def scores(h):
                ho = 64 * (h % 2)
                for b, parts in enumerate((((0, 1, 0), (1, 1, 256)), ((2, 1, 0),), ((0, 0, 0), (1, 0, 128), (2, 0, 256)))):
                    ps = proj(f"L {h} {b}")
                    for g, j, at_ in parts:
                        n = T if j else P
                        mm = pe.matmul(ps[:, at_:at_ + n], qT[g][ho:ho + 64, h // 2, j * P:j * P + P], kT[g][ho:ho + 64, h // 2, 0:n],
                                       start=True, stop=True)
                    mm.then_inc(sig("proj_full"), 1)

            pe.wait_ge(sig("proj_out"), proj_no("V2 1") + 1)
            scores(0)
            for h in range(HEADS):
                if h < HEADS - 1:
                    scores(h + 1)
                pe.wait_ge(sig("exp_done"), 2 * (h + 1))
                for b in range(3):
                    ps = small(f"T {h} {b}")
                    for m in range(4 if b < 2 else 1):
                        mm = pe.transpose(ps[:, m * P:m * P + P], PB[h % 2][:, (4 * b + m) * P:(4 * b + m + 1) * P], ident)
                    mm.then_inc(sig("small_full"), 1)
                if h < 2:
                    tokens2("Z", (h,))
                else:
                    channels2(("U", "ZP", "g2a 0")[h // 2 - 1], (h % 2,))
                ps = small(f"O {h}")
                pe.wait_ge(sig("small_out"), small_no(f"T {h} 2") + 1)
                for n in range(6):
                    pe.matmul(ps[:, CH:2 * CH], PTr[:, n * P:n * P + P], vK[n // 2][:, n % 2, h * CH:h * CH + CH], start=n == 0, stop=n == 5)
                for n in range(3):
                    mm = pe.matmul(ps[:, 0:CH], PTr[:, (6 + n) * P:(7 + n) * P], vK[n][:, 0, h * CH:h * CH + CH], start=n == 0, stop=n == 2)
                mm.then_inc(sig("small_full"), 1)
            channels2("g2a 1")
            pe.wait_ge(sig("attn_done"), 1)
            for i in range(2):
                ps = small(f"aT {i}")
                for m in range(2):
                    for j in range(TT):
                        mm = pe.transpose(ps[:, m * T + j * P:m * T + j * P + P], attn[:, j, (2 * i + m) * P:(2 * i + m + 1) * P], ident)
                mm.then_inc(sig("small_full"), 1)
            pe.wait_ge(sig("poolw_loaded"), 16)
            pe.wait_ge(sig("pooled"), 1)
            for i in range(2):
                ps = small(f"pool {i}")
                for m in range(2):
                    mm = pe.matmul(ps[:, m * T:m * T + T], POOLW[:, 2 * i + m, :], pooled[:, 2 * i + m, :], start=True, stop=True)
                mm.then_inc(sig("small_full"), 1)
            pe.wait_ge(sig("small_out"), small_no("aT 1") + 1)
            merge2("Wb2a", attnT)
            channels2("g2p 0")
            channels2("g2p 1")
            pe.wait_ge(sig("pool_done"), 1)
            merge2("Wb2p", poolT)
            pe.wait_ge(sig("merged2"), 2)
            for half in range(2):
                w = unit2(f"out2 {half}")
                for j in range(TT):
                    ps = small(f"mix2 {2 * half + j}")
                    for k in range(KD):
                        mm = pe.matmul(ps[:, :], MERGED2[:, k, j * P:j * P + P], w[:, k, :], start=k == 0, stop=k == KD - 1)
                    mm.then_inc(sig("small_full"), 1)

        @block.scalar
        def _(act):
            count = {}

            def do(ins_, s="act_chain"):
                count[s] = count.get(s, 0) + 1
                ins_.then_inc(sig(s), 1)
                act.wait_ge(sig(s), count[s])

            def out(name, dst, func=ACT.Copy, src=None):
                n = proj_no(name)
                act.wait_ge(sig("proj_full"), n + 1)
                ps = proj_bank[n % 4]
                v = ps[:, :] if src is None else src(ps)
                if len(dst.shape) == 3 and src is None:
                    v = ps[:, :].rearrange("p (a b) -> p a b", b=dst.shape[2])
                act.activation(dst, v, func).then_inc(sig("proj_out"), 1)

            def channels(what, dst, func=ACT.Copy):
                for b in range(2):
                    out(f"{what} {b}", dst[:, 2 * b:2 * b + 2, :], func)

            def gates(b, before, banks=range(4)):
                if before:
                    act.wait_ge(sig("merged"), before)
                for i in banks:
                    out(f"G {b} {i}", SG[:, 2 * i:2 * i + 2, :], ACT.Sigmoid)

            act.dma_start(CO[:, 0:P], consts["consts"][:, 0:P]).then_inc(sig("ident_loaded"), 16)
            for name, (row, cnt) in VEC.items():
                act.dma_start(PROW[row:row + cnt, :], ins[name].flatten().rearrange("(a b) -> a b", b=P)).then_inc(sig("prow_loaded"), 16)
            act.wait_ge(sig("lam_abs"), 1)
            do(act.activation(lam[:, 1], lam[:, 0], ACT.Exp), "lam_exp")
            act.wait_ge(sig("lam_u"), 1)
            do(act.activation(lam[:, 3], lam[:, 2], ACT.Ln), "lam_ln")
            channels("D xr", xr[:, :, 3:])
            channels("D gate", lgate)
            channels("C q", cz[:, 0:4, 3:])
            act.wait_ge(sig("D_gates"), 1)
            do(act.activation(gx, gx, ACT.Sigmoid), "D_sig")
            do(act.activation(ga, ga, ACT.Sigmoid), "D_sig")
            act.wait_ge(sig("D_gelu"), 1)
            do(act.activation(lt1, lt1, ACT.Sigmoid, scale=2.0 * float(np.sqrt(2.0 / np.pi))), "D_gelu_sig")
            act.wait_ge(sig("D_loga"), 1)
            do(act.activation(lt2, ga, ACT.Tanh, scale=-1.0), "D_tanh")
            do(act.activation(ga, ga, ACT.Exp), "D_a")
            channels("C k", cz[:, 4:8, 3:])
            act.wait_ge(sig("D_m2"), 1)
            do(act.activation(lt2, lt2, ACT.Sqrt), "D_mult")
            out("C if", rows[0:4, 0:2, :], src=lambda ps: ps[0:4, :].rearrange("p (a b) -> p a b", b=T))
            for j in range(TT):
                out(f"C v {j}", vC[:, j, :])
            act.wait_ge(sig("C_absf"), 1)
            do(act.activation(e1C, e1C, ACT.Exp, scale=-1.0), "C_exp")
            act.wait_ge(sig("C_u1"), 1)
            do(act.activation(e2C, e2C, ACT.Ln), "C_ln")
            channels("C o", oC, ACT.Sigmoid)
            act.wait_ge(sig("C_conv"), 1)
            do(act.activation(cz[:, :, 0:T], qk, ACT.Sigmoid), "C_silu")
            act.wait_ge(sig("D_done"), 1)
            channels("B q", qB)
            act.wait_ge(sig("C_dist"), 1)
            do(act.activation(wC, wC, ACT.Exp, scale=-1.0), "C_w")
            do(act.activation(emC, colC[:, 1, :], ACT.Exp, scale=-1.0), "C_em")
            def rsqrt(v, wait, s, n=1):
                act.wait_ge(sig(wait), n)
                do(act.activation(v, v, ACT.Ln))
                do(act.activation(v, v, ACT.Exp, scale=-0.5), s)

            channels("B f", fB)
            for j in range(TT):
                out(f"B i {j}", vB[:, j, :])
            channels("B g", gB)
            act.wait_ge(sig("proj_out"), proj_no("B g 1") + 1)
            do(act.activation(tB, qB, ACT.Sigmoid))
            do(act.activation(kB, fB, ACT.Sigmoid, scale=-1.0))
            do(act.activation(eB, gB, ACT.Sigmoid), "B_sig")
            rsqrt(stC[:, 2, :], "C_var", "C_rstd")
            act.wait_ge(sig("B_absf"), 1)
            do(act.activation(cB, cB, ACT.Exp, scale=-1.0))
            do(act.activation(cB, cB, ACT.Ln, bias=1.0), "B_ln")
            gates("D", 0)
            PROJ_FILL = [f"A {x} {b}" for x in "rkv" for b in range(2)]
            fill = dict(enumerate(PROJ_FILL + ["A x"]))
            for l in range(9):
                if l < 8:
                    act.wait_ge(sig("B_diff"), l + 1)
                    act.activation(eBs[l % 2], eBs[l % 2], ACT.Exp).then_inc(sig("B_exp"), 1)
                if l == 1:
                    act.wait_ge(sig("C_done"), 1)
                if l > 0 and l - 1 in fill:
                    f = fill[l - 1]
                    if f[:3] == "A x":
                        out("A x", zA[:, 12:14, 1:])
                    else:
                        n = PROJ_FILL.index(f)
                        out(f, zA[:, 2 * n:2 * n + 2, 1:])
            act.wait_ge(sig("A_mixed"), 1)
            do(act.activation(zmix[0:64, 12, :], zmix[0:64, 12, :], ACT.Tanh))
            do(act.activation(zmix[:, 13, :], zmix[:, 13, :], ACT.Sigmoid), "A_tanh")
            rsqrt(stB[:, 1, :], "B_var", "B_rstd")
            gates("C", 1, (0, 1))
            act.wait_ge(sig("A_lowrank"), 1)
            do(act.activation(e2A, e2A, ACT.Sigmoid))
            do(act.activation(aA, aA, ACT.Sigmoid), "A_sig")
            act.wait_ge(sig("A_kksum"), 1)
            do(act.activation(e1A, e1A, ACT.Sqrt), "A_norm")
            act.wait_ge(sig("A_cum"), 1)
            do(act.activation(e1A, cumA, ACT.Exp, scale=-E_HALF))
            do(act.activation(e3A, e2A, ACT.Exp, scale=-E_HALF))
            do(act.activation(e2A, cumA, ACT.Exp, scale=E_HALF), "A_exps")
            gates("C", 1, (2, 3))
            gates("B", 2)
            gates("A", 3, (0, 1))
            rsqrt(stA[:, 1, :], "A_var", "A_rstd")
            gates("A", 3, (2, 3))
            for j in range(TT):
                rsqrt(rs1[:, j:j + 1], "ln1_var", "ln1_rstd", j + 1)
            act.wait_ge(sig("table_done"), 1)
            act.dma_start(scratch.rearrange("p h c -> h p c"), along(TAB, P)).then_inc(sig("table_stored"), 16)
            act.wait_ge(sig("logits_ready"), 1)
            do(act.activation(ex, ex, ACT.Exp), "router_exp")
            act.wait_ge(sig("ple_ready"), 1)
            do(act.activation(PG, PG, ACT.Sigmoid), "ple_sig")
            act.wait_ge(sig("gathered"), 1)
            act.activation(XG, x_bank[:, :].rearrange("p (a b) -> p a b", b=CAP), ACT.Copy).then_inc(sig("xg_ready"), 1)
            act.wait_ge(sig("total_ready"), 1)
            n_steps = act.value_load(total[0:1, 0:1], min_val=EXPERTS, max_val=EXPERTS * T // CAP)
            with act.Fori(0, n_steps) as i:
                act.wait_ge(sig("g_ready"), i + 1)
                act.activation(SGH, GH, ACT.Sigmoid, scale=1.702).then_inc(sig("sig_ready"), 1)
                act.wait_ge(sig("gathered"), i + 2)
                act.activation(XG, x_bank[:, :].rearrange("p (a b) -> p a b", b=CAP), ACT.Copy).then_inc(sig("xg_ready"), 1)
                act.wait_ge(sig("ht_full"), i + 1)
                act.activation(HM.rearrange("p m s c -> p (m s c)"), gate_bank[:, :], ACT.Copy).then_inc(sig("hm_ready"), 1)
                act.wait_ge(sig("y_full"), i + 1)
                act.activation(YSB, y_bank[:, :], ACT.Copy).then_inc(sig("y_ready"), 1)
            act.wait_ge(sig("y_ready"), n_steps + 1)
            act.nop().then_inc(sig("last_y_ready"), 1)
            for j in range(TT):
                rsqrt(rs2[:, j:j + 1], "ln2_var", "ln2_rstd", j + 1)
            for j in range(TT):
                act.wait_ge(sig("x2_done"), j + 1)
                do(act.activation(base[:, j, :], x2[:, j, :], ACT.Square, accum_out=ss2[:, j:j + 1]), "squares2")
            for j in range(TT):
                rsqrt(ss2[:, j:j + 1], "rms2_var", "rms2_rstd", j + 1)
            for g in range(GROUPS):
                for b in range(2):
                    out(f"Q{g} {b}", qT[g][:, 2 * b:2 * b + 2, :])
                for b in range(2):
                    out(f"K{g} {b}", kT[g][:, 2 * b:2 * b + 2, :])
                for j in range(TT):
                    out(f"V{g} {j}", vK[g][:, j, :])

            def exponentials(h):
                act.wait_ge(sig("max_ready"), h + 1)
                act.wait_ge(sig("proj_out"), proj_no(f"L {h} 0"))
                for b in range(3):
                    act.nop().then_inc(sig("proj_out"), 1)
                for j, (lo, n) in enumerate(((0, 768), (768, 384))):
                    v = PB[h % 2][:, lo:lo + n]
                    act.activation(v, v, ACT.Exp, scale=0.125, bias=nmax[:, h % 2, j:j + 1],
                                   accum_out=den[:, h % 2, j:j + 1]).then_inc(sig("exp_done"), 1)

            exponentials(0)
            for h in range(HEADS):
                if h < HEADS - 1:
                    if h >= 1:
                        act.wait_ge(sig("small_full"), small_no(f"T {h - 1} 2") + 1)
                        act.wait_ge(sig("small_out"), small_no(f"O {h - 1}") + 1)
                    exponentials(h + 1)
                b = h % 2
                if h < 2:
                    out(f"Z {b}", zat[:, b, :])
                elif h < 4:
                    out(f"U {b}", u0[:, 2 * b:2 * b + 2, 16:])
                elif h < 6:
                    out(f"ZP {b}", zp[:, 2 * b:2 * b + 2, :])
                else:
                    out(f"g2a {b}", SG[:, 2 * b:2 * b + 2, :], ACT.Sigmoid)
            act.wait_ge(sig("small_full"), small_no("T 7 2") + 1)
            act.wait_ge(sig("proj_out"), proj_no("ZP 1") + 1)
            do(act.activation(zsig, zat, ACT.Sigmoid), "zsig")
            do(act.activation(zpsig, zp, ACT.Sigmoid), "zpsig")
            for n, before in (("g2a", 0), ("g2p", 1)):
                if before:
                    act.wait_ge(sig("merged2"), before)
                for i in range(2 if n == "g2a" else 0, 4):
                    out(f"{n} {i}", SG[:, 2 * i:2 * i + 2, :], ACT.Sigmoid)
            for j in range(TT):
                act.wait_ge(sig("x3_ready"), j + 1)
                do(act.activation(squares[:, j, :], x3[:, j, :], ACT.Square, accum_out=ss3[:, j:j + 1]), "squares3")
            for j in range(TT):
                rsqrt(ss3[:, j:j + 1], "rms3_var", "rms3_rstd", j + 1)

        @block.vector
        def _(dve):
            count = {}

            def do(ins_, s="dve_chain"):
                count[s] = count.get(s, 0) + 1
                ins_.then_inc(sig(s), 1)
                dve.wait_ge(sig(s), count[s])

            def full(name):
                n = small_no(name)
                dve.wait_ge(sig("small_full"), n + 1)
                assert count.get("small_out", 0) == n, (name, n, count.get("small_out", 0))
                return small_bank[n % 4]

            def tiles(ps, n=T):
                return ps[:, :].rearrange("p (a b) -> p a b", b=n)

            TTn, TS, STT = dve.tensor_tensor, dve.tensor_scalar, dve.scalar_tensor_tensor

            def merge(b, first):
                for i in range(4):
                    ps = full(f"Wb {b} {i}")
                    g, m = SG[:, 2 * i:2 * i + 2, :], MERGED[:, 2 * i:2 * i + 2, :]
                    dve.wait_ge(sig("proj_out"), proj_no(f"G {b} {i}") + 1)
                    if first:
                        do(TTn(m, tiles(ps), g, ALU.mult), "small_out")
                    else:
                        do(TTn(g, tiles(ps), g, ALU.mult), "small_out")
                        do(TTn(m, m, g, ALU.add))
                dve.nop().then_inc(sig("merged"), 1)

            for g in range(4):
                do(dve.tensor_copy(XT[:, 2 * g:2 * g + 2, :], tiles(full(f"x {g}"))), "small_out")
            do(dve.tensor_copy(PV[:, 0:NVEC], full("vectors")[:, 0:NVEC]), "small_out")

            do(dve.memset(xr[:, :, 0:3], 0.0))
            do(dve.memset(cz[:, :, 0:3], 0.0))
            LAM = pv("lru_lambda")
            do(STT(lam[:, 0], LAM, -1.0, LAM, ALU.mult, ALU.min), "lam_abs")
            dve.wait_ge(sig("lam_exp"), 1)
            do(TS(lam[:, 2], lam[:, 1], 1.0, None, ALU.add), "lam_u")
            do(STT(lam[:, 4], lam[:, 2], -1.0, lam[:, 1], ALU.add, ALU.subtract))
            do(dve.reciprocal(lam[:, 0], lam[:, 2]))
            do(TTn(lam[:, 4], lam[:, 4], lam[:, 0], ALU.mult))
            dve.wait_ge(sig("lam_ln"), 1)
            do(TTn(lam[:, 4], lam[:, 3], lam[:, 4], ALU.subtract))
            do(STT(lam[:, 4], LAM, 0.0, lam[:, 4], ALU.min, ALU.subtract))
            do(TS(lam[:, 4], lam[:, 4], 8.0, None, ALU.mult))
            dve.wait_ge(sig("proj_out"), proj_no("D xr 1") + 1)

            def conv(dst, src, w, b, tiles_):
                for m in range(tiles_):
                    do(TS(dst[:, m, :], src[:, m, 0:T], w(0, m), b(m), ALU.mult, ALU.add))
                    for tap in range(1, 4):
                        do(STT(dst[:, m, :], src[:, m, tap:tap + T], w(tap, m), dst[:, m, :], ALU.mult, ALU.add))

            conv(xc, xr, lambda tap, m: pv("lru_conv_w", 4 * tap + m, 4 * tap + m + 1), lambda m: pv("lru_conv_b", m, m + 1), 4)
            dve.nop().then_inc(sig("D_conv"), 1)
            dve.wait_ge(sig("proj_out"), proj_no("D gate 1") + 1)
            do(TTn(lt1, lgate, lgate, ALU.mult))
            do(TS(lt1, lt1, 0.044715, 1.0, ALU.mult, ALU.add))
            do(TTn(lt1, lt1, lgate, ALU.mult), "D_gelu")
            for nm, dst in (("gx", gx), ("ga", ga)):
                bias = "lru_bx" if nm == "gx" else "lru_ba"
                for i in range(2):
                    do(TTn(dst[:, 2 * i:2 * i + 2, :], tiles(full(f"D {nm} {i}")), over(pv(bias, 2 * i, 2 * i + 2), T), ALU.add), "small_out")
            dve.nop().then_inc(sig("D_gates"), 1)
            dve.wait_ge(sig("D_sig"), 2)
            do(TTn(ga, ga, over(lam[:, 4], T), ALU.mult), "D_loga")
            do(TTn(gx, gx, xc, ALU.mult))
            dve.wait_ge(sig("D_gelu_sig"), 1)
            do(TTn(lgate, lgate, lt1, ALU.mult))
            dve.wait_ge(sig("D_a"), 1)
            do(TTn(lt1, ga, ga, ALU.mult))
            do(STT(lt2, lt1, 1.0, lt2, ALU.add, ALU.mult), "D_m2")
            dve.wait_ge(sig("D_mult"), 1)
            do(dve.memset(lt2[:, :, 0:1], 1.0))
            do(TTn(gx, gx, lt2, ALU.mult))
            for m in range(KW):
                do(dve.tensor_tensor_scan(lt1[:, m, :], ga[:, m, :], gx[:, m, :], 0.0, ALU.mult, ALU.add))
            do(TTn(YT["D"], lt1, lgate, ALU.mult), "D_done")

            def log_sigmoid(dst, f, e1, e2, absf, u1, ln, exp, tmp, tmp2, meanwhile):
                do(STT(e1, f, -1.0, f, ALU.mult, ALU.max), absf)
                meanwhile()
                dve.wait_ge(sig(exp), 1)
                do(TS(e2, e1, 1.0, None, ALU.add), u1)
                do(TS(tmp, e1, 1.0, None, ALU.add))
                do(STT(tmp2, tmp, -1.0, e1, ALU.add, ALU.subtract))
                do(dve.reciprocal(tmp, tmp))
                do(TTn(tmp, tmp, tmp2, ALU.mult))
                dve.wait_ge(sig(ln), 1)
                do(TTn(tmp, e2, tmp, ALU.subtract))
                do(STT(dst, f, 0.0, tmp, ALU.min, ALU.subtract))

            dve.wait_ge(sig("proj_out"), proj_no("C if") + 1)
            dve.wait_ge(sig("ifb_loaded"), 32)
            do(TS(iC, iC, ifb[0:4, 0:1], None, ALU.add))
            do(TS(fC, fC, ifb[0:4, 1:2], None, ALU.add))
            def conv_qk():
                conv(qk, cz, lambda tap, m: pv("mlstm_conv_w", 8 * tap + m, 8 * tap + m + 1), lambda m: pv("mlstm_conv_b", m, m + 1), 8)
                dve.nop().then_inc(sig("C_conv"), 1)

            log_sigmoid(fC, fC, e1C, e2C, "C_absf", "C_u1", "C_ln", "C_exp", uC, gC, conv_qk)
            dve.wait_ge(sig("const_loaded"), 16)
            on = c("ones")[0:4, :]
            do(dve.tensor_tensor_scan(mC, on, fC, 0.0, ALU.mult, ALU.add))
            do(TTn(uC, iC, mC, ALU.subtract))
            do(dve.tensor_tensor_scan(gC, on, uC, NEG, ALU.mult, ALU.max))
            do(TTn(mC, mC, gC, ALU.add), "C_rows")
            dve.wait_ge(sig("C_silu"), 1)
            do(TTn(qk[:, 0:4], qk[:, 0:4], cz[:, 0:4, 0:T], ALU.mult))
            do(STT(qk[:, 4:8], qk[:, 4:8], float(P) ** -0.5, cz[:, 4:8, 0:T], ALU.mult, ALU.mult), "C_qk")
            for i in range(2):
                n = small_no(f"C row {i}")
                dve.wait_ge(sig("small_full"), n + 1)
            dve.wait_ge(sig("small_full"), small_no("C col") + 1)
            cps = small_bank[small_no("C col") % 4]
            do(dve.tensor_copy(colC.rearrange("p a b -> p (a b)"), cps[:, 0:16]))
            for i in range(2):
                ps = full(f"C row {i}")
                for m in range(2):
                    h = 2 * i + m
                    do(TS(wC[:, h, 0:T], ps[:, m * T:m * T + T], colC[:, 0, h:h + 1], 0.0, ALU.subtract, ALU.max))
                    do(TS(wC[:, h, T:T + P], ps[:, m * T + P:m * T + T], colC[:, 0, 4 + h:5 + h], 0.0, ALU.subtract, ALU.max),
                       "small_out" if m == 1 else "dve_chain")
            full("C col")
            do(TS(emC, colC[:, 1, :], 0.0, None, ALU.add), "small_out")
            dve.nop().then_inc(sig("C_dist"), 1)
            dve.wait_ge(sig("C_w"), 1)
            do(TTn(wC[:, :, 0:P], wC[:, :, 0:P], along(c("upper"), 4), ALU.mult))
            do(TTn(wC[:, :, T:T + P], wC[:, :, T:T + P], along(c("upper"), 4), ALU.mult))
            for h in range(4):
                do(TTn(sC[:, h, :], full(f"C S {h}")[:, 0:384], wC[:, h, :], ALU.mult), "small_out")
            dve.nop().then_inc(sig("C_weights"), 1)
            for j in range(TT):
                do(dve.tensor_copy(hC[:, 4 * j:4 * j + 4, :], tiles(full(f"C num {j}"), P)), "small_out")
            do(dve.tensor_copy(denC, full("C den")[:, 0:8]), "small_out")
            dve.wait_ge(sig("C_em"), 1)
            do(STT(stC[:, 0, :], denC, -1.0, denC, ALU.mult, ALU.max))
            do(TTn(stC[:, 0, :], stC[:, 0, :], emC, ALU.max))
            do(dve.reciprocal(stC[:, 0, :], stC[:, 0, :]))
            do(TTn(hC, hC, over(stC[:, 0, :], P), ALU.mult))

            def centre(v, sq, mean, var, n, eps):
                do(dve.tensor_reduce(mean, v, AX.X, ALU.add))
                do(TS(mean, mean, 1.0 / n, None, ALU.mult))
                do(TTn(v, v, over(mean, n), ALU.subtract))
                do(TTn(sq, v, v, ALU.mult))
                do(dve.tensor_reduce(var, sq, AX.X, ALU.add))

            centre(hC, hC2, stC[:, 1, :], stC[:, 2, :], P, 1e-6)
            do(TS(stC[:, 2, :], stC[:, 2, :], 1.0 / P, 1e-6, ALU.mult, ALU.add), "C_var")
            dve.wait_ge(sig("C_rstd"), 1)
            do(TTn(hC, hC, over(stC[:, 2, :], P), ALU.mult), "C_normed")
            dve.wait_ge(sig("proj_out"), proj_no("B g 1") + 1)
            do(STT(cB, fB, -1.0, fB, ALU.mult, ALU.max), "B_absf")
            dve.wait_ge(sig("B_sig"), 1)
            do(TTn(qB, qB, tB, ALU.mult), "B_qk")
            do(TTn(gB, gB, eB, ALU.mult))
            for i in range(2):
                ps = full(f"C yT {i}")
                for m in range(2):
                    ct = 2 * i + m
                    do(STT(YT["C"][:, ct, :], ps[:, m * T:m * T + T], pv("mlstm_norm_w", ct, ct + 1), oC[:, ct, :], ALU.mult, ALU.mult),
                       "small_out" if m == 1 else "dve_chain")
            dve.nop().then_inc(sig("C_done"), 1)
            do(dve.memset(zA[:, :, 0:1], 0.0))
            dve.wait_ge(sig("B_ln"), 1)
            do(STT(fB, fB, 0.0, cB, ALU.min, ALU.subtract))
            for m in range(KW):
                do(dve.tensor_tensor_scan(cB[:, m, :], c("ones"), fB[:, m, :], 0.0, ALU.mult, ALU.add))
            def halves(v, l):
                v = v.rearrange("p a (n r i) -> p (a n) r i", r=2, i=1 << l)
                return v[:, :, 0, :], v[:, :, 1, :]

            def differences(l):
                left, right = halves(cB, l)
                e_left, e_right = halves(eBs[l % 2], l)
                ref = left[:, :, (1 << l) - 1:1 << l].to_broadcast([P, 4 * T // (2 << l), 1 << l])
                if l > 1:
                    dve.wait_ge(sig("small_full"), small_no(f"B level {l - 2} 1") + 1)
                do(TTn(e_right, right, ref, ALU.subtract))
                do(TTn(e_left, ref, left, ALU.subtract), "B_diff")

            differences(0)
            merge("D", True)

            def shifted(n):
                dve.wait_ge(sig("proj_out"), proj_no("A r 0") + n + 1)
                ms = slice(2 * n, 2 * n + 2)
                do(TTn(dA[:, ms], zA[:, ms, 0:T], zmix[:, ms], ALU.subtract))
                for m in (2 * n, 2 * n + 1):
                    do(STT(zmix[:, m, :], dA[:, m, :], pv("rwkv_mu", m, m + 1), zmix[:, m, :], ALU.mult, ALU.add))


            for j in range(TT):
                do(TTn(aB[:, 4 * j:4 * j + 4, :], tiles(full(f"B diag {j}"), P), along(ident, 4), ALU.mult), "small_out")
            def add_level(l):
                for j in range(TT):
                    t_ = tB.rearrange("p a b -> p (a b)")[:, 512 * j:512 * j + 512].rearrange("p (a b) -> p a b", b=P)
                    do(TTn(t_, tiles(full(f"B level {l} {j}"), P), along(c("level", l * P, l * P + P), 4), ALU.mult), "small_out")
                    do(TTn(aB[:, 4 * j:4 * j + 4, :], aB[:, 4 * j:4 * j + 4, :], t_, ALU.add))

            for l in range(8):
                if l < 7:
                    differences(l + 1)
                dve.wait_ge(sig("B_exp"), l + 1)
                for e, v in zip(halves(eBs[l % 2], l), (halves(kB, l)[0], halves(qB, l)[1])):
                    do(TTn(e, e, v, ALU.mult))
                dve.nop().then_inc(sig("B_level"), 1)
                if l > 0:
                    add_level(l - 1)
                if l > 1:
                    shifted(l - 2)
            do(dve.tensor_copy(aX, tiles(full("B cross"), P)), "small_out")
            shifted(6)
            dve.nop().then_inc(sig("A_mixed"), 1)
            o2 = tB2.rearrange("p a b -> p (a b)").rearrange("p (a b) -> p a b", b=P)
            sq = tB.rearrange("p a b -> p (a b)").rearrange("p (a b) -> p a b", b=P)
            for j in range(TT):
                do(dve.tensor_copy(o2[:, 4 * j:4 * j + 4, :], tiles(full(f"B o {j}"), P)), "small_out")
            do(TTn(sq, o2, o2, ALU.mult))
            do(dve.tensor_reduce(stB[:, 1, :], sq, AX.X, ALU.add))
            do(TS(stB[:, 1, :], stB[:, 1, :], 1.0 / P, 1e-6, ALU.mult, ALU.add), "B_var")
            def ada_rows(i):
                do(dve.tensor_copy(ADAROW[i][:, i % 2, :], full(f"ada rows {i}")[:, :]), "small_out")

            def ada(i):
                do(TTn(MODT[:, 4 * i:4 * i + 4], full(f"ada {i}")[:, 0:4], PV2[:, 16 + 4 * i:20 + 4 * i], ALU.add), "small_out")

            do(dve.tensor_copy(PV2, full("vectors2")[:, 0:40]), "small_out")
            do(dve.tensor_copy(CB, over(PV2[:, 0:8], 32)))
            do(dve.tensor_reduce(SEL, ident.rearrange("p (a b) -> p a b", b=32)[:, :, 0], AX.X, ALU.add), "cond_ready")
            for nm, dst in (("w", e2A), ("a", aA), ("g", gA)):
                for i in range(2):
                    d = dst[:, 2 * i:2 * i + 2, :]
                    ps = tiles(full(f"A {nm} {i}"))
                    if nm == "g":
                        do(dve.tensor_copy(d, ps), "small_out")
                    else:
                        do(TTn(d, ps, over(pv("rwkv_w0" if nm == "w" else "rwkv_a0", 2 * i, 2 * i + 2), T), ALU.add), "small_out")
                if nm == "a":
                    dve.nop().then_inc(sig("A_lowrank"), 1)
            do(TTn(kkA, kA, over(pv("rwkv_k_k"), T), ALU.mult))
            do(TTn(bA, kkA, kkA, ALU.mult), "A_kksq")
            dve.wait_ge(sig("B_rstd"), 1)
            do(TTn(o2, o2, over(stB[:, 1, :], P), ALU.mult), "B_normed")
            for i in range(2):
                do(dve.tensor_copy(e1A[:, 2 * i:2 * i + 2, :], tiles(full(f"A kk {i}"))), "small_out")
            dve.nop().then_inc(sig("A_kksum"), 1)
            dve.wait_ge(sig("A_sig"), 1)
            do(STT(bonusA, aA, -1.0, over(pv("rwkv_k_a"), T), ALU.add, ALU.mult))
            do(STT(kA, bonusA, 1.0, kA, ALU.add, ALU.mult))
            do(TTn(bonusA, rA, kA, ALU.mult))
            do(TTn(bonusA, bonusA, over(pv("rwkv_r_k"), T), ALU.mult), "A_rk")
            for i in range(2):
                ps = full(f"B yT {i}")
                for m in range(2):
                    ct = 2 * i + m
                    do(STT(YT["B"][:, ct, :], ps[:, m * T:m * T + T], pv("hgrn_norm_w", ct, ct + 1), gB[:, ct, :], ALU.mult, ALU.mult),
                       "small_out" if m == 1 else "dve_chain")
            dve.nop().then_inc(sig("B_done"), 1)
            for i in range(2):
                do(dve.tensor_copy(Vt[:, i, :], full(f"A V {i}")[:, :]), "small_out")
            dve.wait_ge(sig("A_norm"), 1)
            do(TS(e1A, e1A, 1e-12, None, ALU.max))
            do(dve.reciprocal(e1A, e1A))
            do(TTn(kkA, kkA, e1A, ALU.mult))
            do(TTn(bA, kkA, aA, ALU.mult))
            for m in range(KW):
                do(dve.tensor_tensor_scan(cumA[:, m, :], c("reset64"), e2A[:, m, :], 0.0, ALU.mult, ALU.add))
            do(TTn(e2A, cumA, e2A, ALU.subtract), "A_cum")
            ada_rows(0)
            for i in range(2):
                do(TTn(bonusA[:, 2 * i:2 * i + 2, :], tiles(full(f"A bonus {i}")), vA[:, 2 * i:2 * i + 2, :], ALU.mult), "small_out")
            dve.wait_ge(sig("A_exps"), 1)
            do(STT(kkA, kkA, -1.0, e3A, ALU.mult, ALU.mult), "A_tilde")
            do(TTn(bA, bA, e2A, ALU.mult), "A_tilde")
            do(TTn(kA, kA, e2A, ALU.mult), "A_tilde")
            do(TTn(rA, rA, e1A, ALU.mult), "A_tilde")
            ada(0)
            ada_rows(1)
            for nm, dst in (("At", At), ("Bt", Bt), ("Kt", Kt)):
                for i in range(2):
                    do(dve.tensor_copy(dst[:, i, :], full(f"A {nm} {i}")[:, :]), "small_out")
            ada(1)
            ada_rows(2)

            def masked(name, dst, mask):
                for i in range(4):
                    do(TTn(dst[:, 4 * i:4 * i + 4, :], tiles(full(f"A {name} {i}"), P), along(c(mask), 4), ALU.mult), "small_out")

            masked("NT", NT, "strict64")
            ada(2)
            ada_rows(3)
            dve.wait_ge(sig("NTm_ready"), 1)
            do(TTn(DTa, NTm, along(ident, 16), ALU.add))
            for i in range(4):
                do(TTn(Da[:, 4 * i:4 * i + 4, :], tiles(full(f"A X0 {i}"), P), along(ident, 4), ALU.add), "small_out")
            ada(3)
            merge("C", False)
            for l in range(1, 6):
                for i in range(4):
                    do(dve.tensor_copy(X[:, 4 * i:4 * i + 4, :], tiles(full(f"A X{l} {i}"), P)), "small_out")
                for nm, m in (("D", Da), ("DT", DTa)):
                    if (nm, l) == ("D", 5):
                        continue
                    for i in range(4):
                        do(TTn(m[:, 4 * i:4 * i + 4, :], tiles(full(f"A {nm}{l} {i}"), P), m[:, 4 * i:4 * i + 4, :], ALU.add), "small_out")
            merge("B", False)
            masked("AkT", AkT, "strict64")
            for j in range(TT):
                do(dve.tensor_copy(GT[:, :, j * P:j * P + P], tiles(full(f"A GT {j}"), P)), "small_out")
            for j in range(TT):
                do(dve.tensor_copy(WU[:, j, :], full(f"A W {j}")[:, :]), "small_out")
            for j in range(TT):
                do(dve.tensor_copy(Ut[:, j, :], full(f"A U0 {j}")[:, :]), "small_out")
            dve.nop().then_inc(sig("A_u"), 1)
            for ch in range(4):
                j, po = ch // 2, 64 * (ch % 2)
                if ch > 0:
                    for odd in range(2):
                        u = Ut[po:po + 64, j, :].rearrange("p (a r v) -> p a r v", r=2, v=CH)[:, :, odd, :]
                        ps = full(f"A U {ch} {odd}")[po:po + 64, 0:256].rearrange("p (a v) -> p a v", v=CH)
                        do(TTn(u, ps, u, ALU.add), "small_out")
                    dve.nop().then_inc(sig("A_u"), 1)
                if ch < 3:
                    s = S_all[:, ch + 1, :].rearrange("p (a b) -> p a b", b=CH)
                    decay = over(e1A[:, :, ch * CH + CH - 1], CH)
                    ps = full(f"A S {ch}")[:, 0:256].rearrange("p (a b) -> p a b", b=CH)
                    if ch == 0:
                        do(TTn(s, ps, decay, ALU.mult), "small_out")
                    else:
                        do(TTn(s, ps, S_all[:, ch, :].rearrange("p (a b) -> p a b", b=CH), ALU.add), "small_out")
                        do(TTn(s, s, decay, ALU.mult))
                    dve.nop().then_inc(sig("A_state"), 1)
            dve.nop().then_inc(sig("A_states_done"), 1)
            masked("RbT", RbT, "upper64")
            masked("RkT", RkT, "upper64")
            for i in range(4):
                j, odd = divmod(i, 2)
                ps = full(f"A Y {i}")[:, 0:256].rearrange("p (a v) -> p a v", v=CH)
                do(dve.tensor_copy(Ysum[:, 8 * j + odd:8 * j + 8:2, :], ps), "small_out")
            centre(Ysum, Ysq, stA[:, 0, :], stA[:, 1, :], CH, 64e-5)
            do(TS(stA[:, 1, :], stA[:, 1, :], 1.0 / CH, 64e-5, ALU.mult, ALU.add), "A_var")
            dve.wait_ge(sig("A_rstd"), 1)
            do(TTn(Ysum, Ysum, over(stA[:, 1, :], CH), ALU.mult), "A_normed")
            for i in range(2):
                ps = full(f"A yT {i}")
                for m in range(2):
                    ct = 2 * i + m
                    do(TS(YT["A"][:, ct, :], ps[:, m * T:m * T + T], pv("rwkv_lnx_g", ct, ct + 1), pv("rwkv_lnx_b", ct, ct + 1), ALU.mult, ALU.add),
                       "small_out" if m == 1 else "dve_chain")
            do(TTn(YT["A"], YT["A"], bonusA, ALU.add))
            do(TTn(YT["A"], YT["A"], gA, ALU.mult), "A_done")
            merge("A", False)

            def half_stats(v, st, j, half_):
                do(dve.bn_stats(st[:, j, 6 * half_:6 * half_ + 6], v[:, j, half_ * W:half_ * W + W]))

            def centred(v, st, mv, rs, g, j, var):
                do(dve.bn_aggr(mv[:, j, :], st[:, j, :]))
                do(TS(rs[:, j:j + 1], mv[:, j, 1:2], 1e-5, None, ALU.add), var)
                do(STT(v[:, j, :], v[:, j, :], mv[:, j, 0:1], g, ALU.subtract, ALU.mult))

            def normed(dst, v, rs, b, j, rstd, done):
                dve.wait_ge(sig(rstd), j + 1)
                do(STT(dst[:, j, :], v[:, j, :], rs[:, j:j + 1], b, ALU.mult, ALU.add), done)

            dve.wait_ge(sig("ln1_loaded"), 32)
            for half_ in range(2):
                for j in range(TT):
                    cols = slice(half_ * W, half_ * W + W)
                    do(STT(mixv[:, j, cols], XTOK[:, j, cols], ALPHA, full(f"mix {2 * half_ + j}")[:, :], ALU.mult, ALU.add), "small_out")
                    half_stats(mixv, st1, j, half_)
                    if half_:
                        centred(mixv, st1, mv1, rs1, bcg, j, "ln1_var")
                        normed(x1, mixv, rs1, bcb, j, "ln1_rstd", "x1_done")
            dve.wait_ge(sig("table_loaded"), 48)
            do(TTn(TAB, full("bias")[0:24, 0:BKT], BM, ALU.add), "small_out")
            dve.nop().then_inc(sig("table_done"), 1)
            ada_rows(4)
            ada_rows(5)
            ada(4)
            ada(5)
            do(dve.tensor_copy(G8, full("gate8")[0:8, 0:P]), "small_out")

            for g in range(4):
                do(dve.tensor_copy(XT[:, 2 * g:2 * g + 2, :], tiles(full(f"x1 {g}"))), "small_out")
            for i in range(2):
                do(dve.tensor_copy(gateB[:, i * W:i * W + W], full(f"gateB {i}")[:, :]), "small_out")
            do(STT(mod_a, MODT[:, 8:16], 1.0, PV2[:, 8:16], ALU.add, ALU.mult))
            dve.wait_ge(sig("router_loaded"), 80)
            do(TTn(lg, full("logits")[:, 0:64].rearrange("p (a b) -> p a b", b=EXPERTS), along(RB, TT), ALU.add), "small_out")
            for j in range(TT):
                do(dve.max(mx8[:, j, :], lg[:, j, :]))
                do(TS(ex[:, j, :], lg[:, j, :], mx8[:, j, 0:1], None, ALU.subtract), "logits_ready" if j == 1 else "dve_chain")
                do(TS(above[:, j, :], lg[:, j, :], mx8[:, j, 3:4], None, ALU.is_gt))
                do(TS(tie[:, j, :], lg[:, j, :], mx8[:, j, 3:4], None, ALU.is_equal))
                do(dve.tensor_tensor_scan(cum[:, j, :], c("ones", 0, EXPERTS), tie[:, j, :], 0.0, ALU.mult, ALU.add))
            do(dve.tensor_reduce(n_above, above, AX.X, ALU.add))
            do(TS(n_ties, n_above, -1.0, 4.0, ALU.mult, ALU.add))
            do(TTn(cum, cum, over(n_ties, EXPERTS), ALU.is_le))
            do(TTn(cum, cum, tie, ALU.mult))
            do(TTn(sel, above, cum, ALU.add))
            dve.wait_ge(sig("router_exp"), 1)
            do(TTn(gates_, ex, sel, ALU.mult))
            do(dve.tensor_reduce(gate_sum, gates_, AX.X, ALU.add))
            do(dve.reciprocal(gate_scale, gate_sum))
            do(TTn(gates_, gates_, over(gate_scale, EXPERTS), ALU.mult), "gates_ready")
            do(dve.tensor_copy(PTT, tiles(full("pT"))), "small_out")

            def embed(half_):
                for j in range(TT):
                    do(dve.tensor_copy(PG[:, j, half_ * W:half_ * W + W], full(f"ple {2 * half_ + j}")[:, :]), "small_out")

            embed(0)
            do(dve.tensor_copy(GTT, full("gateT")[0:EXPERTS, 0:T]), "small_out")
            ps = full("rank")
            do(dve.tensor_reduce(top[:, 0:1], ps[:, 64:96], AX.X, ALU.max))
            do(STT(rank, ps[:, 0:64].rearrange("p (a b) -> p a b", b=EXPERTS), 4096.0, sel, ALU.add, ALU.mult), "small_out")
            do(TS(rank, rank, -4096.0, None, ALU.add))
            do(TS(top[:, 1:2], top[:, 0:1], float(CAP), 1.0, ALU.is_gt, ALU.add))
            for n in (2, 3):
                do(STT(top[:, 1:2], top[:, 0:1], float(n * CAP), top[:, 1:2], ALU.is_gt, ALU.add))
            do(TS(total, top[:, 1:2], float(EXPERTS), None, ALU.mult), "total_ready")
            embed(1)
            dve.nop().then_inc(sig("ple_ready"), 1)
            dve.wait_ge(sig("ple_sig"), 1)
            for i in range(4):
                half_, j = divmod(i, 2)
                do(TTn(base[:, j, half_ * W:half_ * W + W], full(f"pp {i}")[:, :], PG[:, j, half_ * W:half_ * W + W], ALU.mult), "small_out")
            do(STT(base, x1, ALPHA, base, ALU.mult, ALU.add), "base_done")

            def pick(dst, e, ready, weight):
                for j in range(TT):
                    if weight:
                        op = TS(dst[:, j, :].rearrange("p (s c) -> p s c", s=2), along(c("slot"), 2), rank[:, j, bass.ds(e, 1)], gates_[:, j, bass.ds(e, 1)], ALU.is_equal, ALU.mult)
                    else:
                        op = TS(dst[:, j, :], c("slot"), rank[:, j, bass.ds(e, 1)], None, ALU.is_equal)
                op.then_inc(sig(ready), 1)

            do(dve.memset(YSB, 0.0), "y_ready")
            do(dve.memset(PTW, 0.0), "ptw_ready")
            do(dve.tensor_copy(ESEL, c("ident", 0, 1).to_broadcast([P, CAP])), "esel_ready")
            pick(PICK, 0, "pick_ready", False)
            n_steps = dve.value_load(total[0:1, 0:1], min_val=EXPERTS, max_val=EXPERTS * T // CAP)
            LINKS = 3
            with dve.Fori(0, n_steps) as i:
                link = [0]

                def then(ins_):
                    link[0] += 1
                    ins_.then_inc(sig("expert_chain"), 1)
                    dve.wait_ge(sig("expert_chain"), LINKS * i + link[0])

                e, nxt = i % EXPERTS, (i + 1) % EXPERTS
                dve.wait_ge(sig("ptw_full"), i + 1)
                pick(PICKW, e, "pickw_ready", True)
                dve.wait_ge(sig("pickw_ready"), i + 1)
                then(TS(rank[:, :, bass.ds(e, 1)], rank[:, :, bass.ds(e, 1)], -float(CAP), None, ALU.add))
                dve.wait_ge(sig("gathered"), i + 1)
                pick(PICK, nxt, "pick_ready", False)
                dve.wait_ge(sig("gu_full"), i + 1)
                TS(GH, gate_bank[:, :], 7.0, None, ALU.min).then_inc(sig("g_ready"), 1)
                then(TS(UH, up_bank[:, :], 7.0, -7.0, ALU.min, ALU.max))
                dve.tensor_copy(ESEL, c("ident", 0, EXPERTS)[:, bass.ds(nxt, 1)].to_broadcast([P, CAP])).then_inc(sig("esel_ready"), 1)
                dve.wait_ge(sig("sig_ready"), i + 1)
                then(TTn(GH, GH, SGH, ALU.mult))
                STT(GH, UH, 1.0, GH, ALU.add, ALU.mult).then_inc(sig("h_ready"), 1)
                dve.wait_ge(sig("ptw_full"), i + 2)
                dve.tensor_copy(PTW, y_bank[:, 0:T]).then_inc(sig("ptw_ready"), 1)
                assert link[0] == LINKS
            dve.wait_ge(sig("experts_done"), 1)
            dve.wait_ge(sig("ln2_loaded"), 32)
            for j in range(TT):
                for half_ in range(2):
                    v = base[:, j, half_ * W:half_ * W + W]
                    do(TTn(v, acc_bank[2 * j + half_][:, :], v, ALU.add))
                    half_stats(base, st2, j, half_)
                if j == 1:
                    dve.nop().then_inc(sig("acc_read"), 1)
                centred(base, st2, mv2, rs2, ln2g, j, "ln2_var")
            for j in range(TT):
                normed(x2, base, rs2, ln2b, j, "ln2_rstd", "x2_done")

            for j in range(TT):
                dve.wait_ge(sig("squares2"), j + 1)
                do(TS(ss2[:, j:j + 1], ss2[:, j:j + 1], 1.0 / D, 1e-6, ALU.mult, ALU.add), "rms2_var")
            for j in range(TT):
                dve.wait_ge(sig("rms2_rstd"), j + 1)
                do(TS(base[:, j, :], x2[:, j, :], ss2[:, j:j + 1], None, ALU.mult), "x2n_done")
            for g in range(4):
                ps, j = full(f"h {g}"), g // 2
                for m in range(4):
                    k = 4 * (g % 2) + m
                    do(TS(HT[:, k, j * P:j * P + P], ps[:, m * P:m * P + P], mod_a[:, k:k + 1], MODT[:, k:k + 1], ALU.mult, ALU.add),
                       "small_out" if m == 3 else "dve_chain")
            do(dve.memset(u0[:, :, 0:16], 0.0))

            def maxima(h):
                for b, (gs, lo, n) in enumerate(((slice(0, 2), 0, T), (slice(2, 3), 2 * T, T), (slice(0, 3), 3 * T, P))):
                    k = proj_no(f"L {h} {b}")
                    dve.wait_ge(sig("proj_full"), k + 1)
                    bias = HK.rearrange("p (g h) c -> p g h c", g=GROUPS)[:, gs, h, T - n:T]
                    w_ = bias.shape[1] * n
                    do(TTn(PB[h % 2][:, lo:lo + w_].rearrange("p (g c) -> p g c", c=n),
                           proj_bank[k % 4][:, 0:w_].rearrange("p (g c) -> p g c", c=n), bias, ALU.add))
                for j, (lo, n) in enumerate(((0, 768), (768, 384))):
                    do(dve.tensor_reduce(nmax[:, h % 2, j:j + 1], PB[h % 2][:, lo:lo + n], AX.X, ALU.max))
                do(TS(nmax[:, h % 2, 0:2], nmax[:, h % 2, 0:2], -0.125, None, ALU.mult), "max_ready")

            dve.wait_ge(sig("hankel_loaded"), 16)
            maxima(0)
            for h in range(HEADS):
                if h < HEADS - 1:
                    maxima(h + 1)
                for b in range(3):
                    n = 512 if b < 2 else P
                    do(dve.tensor_copy(PTr[:, 512 * b:512 * b + n], full(f"T {h} {b}")[:, 0:n]), "small_out")
                d = den[:, h % 2, :]
                do(dve.reciprocal(d[:, 0:2], d[:, 0:2]))
                ps = full(f"O {h}")
                do(TS(attn[:, 1, h * CH:h * CH + CH], ps[:, CH:2 * CH], d[:, 0:1], None, ALU.mult))
                do(TS(attn[:, 0, h * CH:h * CH + CH], ps[:, 0:CH], d[:, 1:2], None, ALU.mult), "small_out")
            dve.wait_ge(sig("zsig"), 1)
            do(TTn(attn, attn, zat, ALU.mult))
            do(TTn(attn, attn, zsig, ALU.mult), "attn_done")
            src = u0
            for n in range(4):
                w_, dst = 1 << n, (uA, uB)[n % 2]
                do(TTn(dst[:, n:, w_:], src[:, n:, w_:], src[:, n:, 0:T + 16 - w_], ALU.add))
                if n < 3:
                    do(dve.tensor_copy(dst[:, n:, 0:w_], src[:, n:, 0:w_]))
                do(TTn(pooled[:, n, :], dst[:, n, 16:], c("poolcnt", n * T, n * T + T), ALU.mult))
                do(TTn(pooled[:, n, :], pooled[:, n, :], u0[:, n, 16:], ALU.subtract))
                src = dst
            dve.nop().then_inc(sig("pooled"), 1)
            for i in range(2):
                do(dve.tensor_copy(attnT[:, 2 * i:2 * i + 2, :], tiles(full(f"aT {i}"))), "small_out")
            dve.wait_ge(sig("zpsig"), 1)
            do(TTn(zp, zp, zpsig, ALU.mult))
            for i in range(2):
                ps = full(f"pool {i}")
                for m in range(2):
                    ct = 2 * i + m
                    do(STT(poolT[:, ct, :], ps[:, m * T:m * T + T], pv("pool_scale_2", ct, ct + 1), zp[:, ct, :], ALU.mult, ALU.mult),
                       "small_out" if m else "dve_chain")
            dve.nop().then_inc(sig("pool_done"), 1)
            for n, name in enumerate(("a", "p")):
                for i in range(4):
                    ps = full(f"Wb2{name} {i}")
                    g, m = SG[:, 2 * i:2 * i + 2, :], MERGED2[:, 2 * i:2 * i + 2, :]
                    dve.wait_ge(sig("proj_out"), proj_no(f"g2{name} {i}") + 1)
                    do(TTn(g if n else m, tiles(ps), g, ALU.mult), "small_out")
                    if n:
                        do(TTn(m, m, g, ALU.add))
                dve.nop().then_inc(sig("merged2"), 1)
            for i in range(4):
                half_, j = divmod(i, 2)
                cols = slice(half_ * W, half_ * W + W)
                do(TTn(x3[:, j, cols], full(f"mix2 {i}")[:, :], gateB[:, cols], ALU.mult), "small_out")
                do(TTn(x3[:, j, cols], x3[:, j, cols], x2[:, j, cols], ALU.add), "x3_ready" if half_ else "dve_chain")
            for j in range(TT):
                dve.wait_ge(sig("squares3"), j + 1)
                do(TS(ss3[:, j:j + 1], ss3[:, j:j + 1], 1.0 / D, 1e-6, ALU.mult, ALU.add), "rms3_var")
            dve.wait_ge(sig("fing_loaded"), 16)
            for j in range(TT):
                dve.wait_ge(sig("rms3_rstd"), j + 1)
                do(STT(x3[:, j, :], x3[:, j, :], ss3[:, j:j + 1], fing, ALU.mult, ALU.mult), "final")


def kernel(**inputs):
    import numpy as _np
    import concourse.bacc as _bacc
    from concourse import mybir as _mybir
    from concourse.bass_utils import run_bass_kernel_spmd as _run

    nc = _bacc.Bacc("TRN2", target_bir_lowering=False, num_devices=1)
    arrays, ins, consts = {}, {}, {}
    for name, a in inputs.items():
        a = _np.ascontiguousarray(a)
        if not a.size or name in UNUSED:
            continue
        arrays[f"in_{name}"] = a
        ins[name] = nc.dram_tensor(f"in_{name}", a.shape, _mybir.dt.from_np(a.dtype), kind="ExternalInput").ap()
    hot, mask = bias_tables()
    for name, a in (("consts", constants()), ("hot", hot), ("mask", mask)):
        arrays[f"shape_{name}"] = a
        consts[name] = nc.dram_tensor(f"shape_{name}", a.shape, F32, kind="ExternalInput").ap()
    out = nc.dram_tensor("out", (1, T, D), F32, kind="ExternalOutput").ap()
    build(nc, ins, consts, [out])
    r = _run(nc, [arrays], core_ids=[0])
    return r.results[0]["out"]
```
